# Optimizing a Trainium2 kernel written in Bass

```python
import jax
import jax.numpy as jnp
from jax import lax
import numpy as np

D_MODEL = 1024
BATCH = 1
SEQ = 256
DEPTH = 1

ML_HEADS = 4
ML_DQK = 128
ML_DV = 128
ML_W = ML_HEADS * ML_DQK
ML_CHUNK = 64
ML_CONV = 4
NSA_QH = 8
NSA_KVH = 2
NSA_DH = 64
NSA_GROUP = NSA_QH // NSA_KVH
NSA_W = NSA_QH * NSA_DH
NSA_KV_W = NSA_KVH * NSA_DH
CMP_BLOCK = 32
CMP_STRIDE = 16
CMP_HIDDEN = 256
SEL_BLOCK = 64
SEL_TOPN = 8
SEL_FORCE_BONUS = 1e4
WINDOW = 512
Q_BLOCK = 128
MEM_LEN = 256
MEM_HEADS = 4
MEM_DH = 128
MEM_W = MEM_HEADS * MEM_DH
N_EXPERTS = 32
TOP_K = 4
D_FF = D_MODEL
SWIGLU_ALPHA = 1.702
SWIGLU_LIMIT = 7.0
MOE_BLOCK = 256
N_BRANCH = 3
ROPE_THETA = 10000.0
EPS = 1e-6
NEG = -1e30

IN_SPLITS = (ML_W, ML_W, ML_HEADS * ML_DV, ML_HEADS * ML_DV, ML_HEADS, ML_HEADS,
             NSA_W, NSA_KV_W, NSA_KV_W, NSA_KV_W, NSA_KV_W, NSA_KV_W, NSA_KV_W, NSA_QH * 3,
             MEM_W, N_BRANCH * D_MODEL)
D_IN = sum(IN_SPLITS)

kernel_name = "hybrid_mlstm_nsa_memxattn_moe_block"

def _rmsnorm(t, g):
    t32 = t.astype(jnp.float32)
    y = t32 * lax.rsqrt(jnp.mean(t32 * t32, axis=-1, keepdims=True) + EPS)
    return (y * g.astype(jnp.float32)).astype(t.dtype)

def _rope(t, pos):
    half = t.shape[-1] // 2
    inv_freq = jnp.power(ROPE_THETA, -jnp.arange(half, dtype=jnp.float32) / half)
    ang = pos.astype(jnp.float32)[:, None] * inv_freq[None, :]
    cos = jnp.cos(ang)[:, None, :]
    sin = jnp.sin(ang)[:, None, :]
    t32 = t.astype(jnp.float32)
    t1, t2 = t32[..., :half], t32[..., half:]
    return jnp.concatenate([t1 * cos - t2 * sin, t2 * cos + t1 * sin], axis=-1).astype(t.dtype)

def _masked_softmax(s, mask):
    s = jnp.where(mask, s.astype(jnp.float32), NEG)
    e = jnp.exp(s - jnp.max(s, axis=-1, keepdims=True)) * mask
    return e / jnp.maximum(jnp.sum(e, axis=-1, keepdims=True), 1e-30)

def _split_cols(t, sizes):
    out, off = [], 0
    for s in sizes:
        out.append(t[..., off:off + s])
        off += s
    return out

def _causal_conv(t, w, b):
    c = t.shape[-1]
    y = lax.conv_general_dilated(t, w.astype(t.dtype)[:, None, :], window_strides=(1,),
                                 padding=[(ML_CONV - 1, 0)],
                                 dimension_numbers=("NWC", "WIO", "NWC"),
                                 feature_group_count=c)
    return y + b.astype(t.dtype)

def _mlstm(q, k, v, i_pre, f_pre):
    bsz, seq, nh, _ = q.shape
    nc = seq // ML_CHUNK
    f32 = jnp.float32

    def chunks(t):
        return t.astype(f32).reshape(bsz, nc, ML_CHUNK, nh, -1).transpose(0, 3, 1, 2, 4)

    def gchunks(t):
        return t.astype(f32).reshape(bsz, nc, ML_CHUNK, nh).transpose(0, 3, 1, 2)

    q = chunks(q) * (ML_DQK ** -0.5)
    k = chunks(k)
    v = chunks(v)
    ig = gchunks(i_pre)
    b = jnp.cumsum(jax.nn.log_sigmoid(gchunks(f_pre)), axis=-1)
    b_last = b[..., -1]

    g = b_last[..., None] - b + ig
    m_c = jnp.max(g, axis=-1)
    w = jnp.exp(g - m_c[..., None])
    kv_c = jnp.einsum("bhclk,bhclv->bhckv", k * w[..., None], v)
    n_c = jnp.einsum("bhcl,bhclk->bhck", w, k)

    def step(carry, xs):
        c_st, n_st, m_st = carry
        kv, nn, mc, bl = xs
        m_new = jnp.maximum(bl + m_st, mc)
        a_old = jnp.exp(bl + m_st - m_new)
        a_new = jnp.exp(mc - m_new)
        c_next = a_old[..., None, None] * c_st + a_new[..., None, None] * kv
        n_next = a_old[..., None] * n_st + a_new[..., None] * nn
        return (c_next, n_next, m_new), (c_st, n_st, m_st)

    init = (jnp.zeros((bsz, nh, ML_DQK, ML_DV), f32), jnp.zeros((bsz, nh, ML_DQK), f32),
            jnp.zeros((bsz, nh), f32))
    xs = (jnp.moveaxis(kv_c, 2, 0), jnp.moveaxis(n_c, 2, 0), jnp.moveaxis(m_c, 2, 0),
          jnp.moveaxis(b_last, 2, 0))
    _, (c_prev, n_prev, m_prev) = lax.scan(step, init, xs)
    c_prev = jnp.moveaxis(c_prev, 0, 2)
    n_prev = jnp.moveaxis(n_prev, 0, 2)
    m_prev = jnp.moveaxis(m_prev, 0, 2)

    tri = jnp.tril(jnp.ones((ML_CHUNK, ML_CHUNK), bool))
    d_log = jnp.where(tri, b[..., :, None] - b[..., None, :] + ig[..., None, :], NEG)
    a_log = b + m_prev[..., None]
    m_t = jnp.maximum(a_log, jnp.max(d_log, axis=-1))
    wd = jnp.exp(d_log - m_t[..., None]) * jnp.einsum("bhctd,bhcsd->bhcts", q, k)
    inter = jnp.exp(a_log - m_t)
    num = inter[..., None] * jnp.einsum("bhctk,bhckv->bhctv", q, c_prev) + \
        jnp.einsum("bhcts,bhcsv->bhctv", wd, v)
    den = inter * jnp.einsum("bhctk,bhck->bhct", q, n_prev) + jnp.sum(wd, axis=-1)
    h = num / jnp.maximum(jnp.abs(den), jnp.exp(-m_t))[..., None]
    return h.transpose(0, 2, 3, 1, 4).reshape(bsz, seq, nh, ML_DV)

def _nsa(q, k_cmp, v_cmp, k_sel, v_sel, k_win, v_win, gate, g_q, g_k,
         pos_k, w1_k, b1_k, w2_k, pos_v, w1_v, b1_v, w2_v):
    bsz, seq = q.shape[:2]
    pos = jnp.arange(seq)

    def heads(t, h):
        return t.reshape(bsz, seq, h, NSA_DH)

    q = _rope(_rmsnorm(heads(q, NSA_QH), g_q), pos) * (NSA_DH ** -0.5)
    qg = q.reshape(bsz, seq, NSA_KVH, NSA_GROUP, NSA_DH)

    n_cmp = (seq - CMP_BLOCK) // CMP_STRIDE + 1
    cmp_start = jnp.arange(n_cmp) * CMP_STRIDE
    cmp_end = cmp_start + CMP_BLOCK - 1
    win_idx = cmp_start[:, None] + jnp.arange(CMP_BLOCK)[None, :]

    def compress(t, pe, w1, b1, w2):
        blocks = heads(t, NSA_KVH)[:, win_idx] + pe[None, None, :, None, :]
        hid = jax.nn.silu(jnp.einsum("bnlhd,ldf->bnhf", blocks, w1) + b1)
        return hid @ w2

    kc = _rope(_rmsnorm(compress(k_cmp, pos_k, w1_k, b1_k, w2_k), g_k[0]), cmp_end)
    vc = compress(v_cmp, pos_v, w1_v, b1_v, w2_v)
    s_cmp = jnp.einsum("bshgd,bnhd->bshgn", qg, kc)
    mask_cmp = (cmp_end[None, :] <= pos[:, None])[None, :, None, None, :]
    p_cmp = _masked_softmax(s_cmp, mask_cmp)
    o_cmp = jnp.einsum("bshgn,bnhd->bshgd", p_cmp.astype(vc.dtype), vc)

    n_sel = seq // SEL_BLOCK
    sel_start = jnp.arange(n_sel) * SEL_BLOCK
    cmp_to_sel = ((cmp_start[:, None] < sel_start[None, :] + SEL_BLOCK) &
                  (cmp_start[:, None] + CMP_BLOCK > sel_start[None, :])).astype(jnp.float32)
    importance = jnp.einsum("bshn,nj->bshj", jnp.sum(p_cmp, axis=3), cmp_to_sel)
    blk = jnp.arange(n_sel)[None, :]
    cur = (pos // SEL_BLOCK)[:, None]
    forced = (blk == 0) | (blk == cur) | (blk == cur - 1)
    score = jnp.where((blk > cur)[None, :, None, :], NEG,
                      importance + SEL_FORCE_BONUS * forced[None, :, None, :])
    _, sel_idx = lax.top_k(score, min(SEL_TOPN, n_sel))
    n_top = sel_idx.shape[-1]

    ks = _rope(_rmsnorm(heads(k_sel, NSA_KVH), g_k[1]), pos)
    ks_blk = ks.reshape(bsz, n_sel, SEL_BLOCK, NSA_KVH, NSA_DH).transpose(0, 3, 1, 2, 4)
    vs_blk = heads(v_sel, NSA_KVH).reshape(bsz, n_sel, SEL_BLOCK, NSA_KVH, NSA_DH).transpose(0, 3, 1, 2, 4)
    kw = _rope(_rmsnorm(heads(k_win, NSA_KVH), g_k[2]), pos)
    pad = ((0, 0), (WINDOW, 0), (0, 0), (0, 0))
    kw_pad = jnp.pad(kw, pad)
    vw_pad = jnp.pad(heads(v_win, NSA_KVH), pad)
    b_ix = jnp.arange(bsz)[:, None, None, None]
    h_ix = jnp.arange(NSA_KVH)[None, None, :, None]

    def query_block(args):
        qb_i, q_blk, idx_blk = args
        start = qb_i * Q_BLOCK
        tq = start + jnp.arange(Q_BLOCK)
        kg = ks_blk[b_ix, h_ix, idx_blk]
        vg = vs_blk[b_ix, h_ix, idx_blk]
        s_sel = jnp.einsum("bqhgd,bqhnld->bqhgnl", q_blk, kg)
        kpos = idx_blk[..., None] * SEL_BLOCK + jnp.arange(SEL_BLOCK)
        m_sel = (kpos <= tq[None, :, None, None, None]).reshape(bsz, Q_BLOCK, NSA_KVH, 1, n_top * SEL_BLOCK)
        p_sel = _masked_softmax(s_sel.reshape(bsz, Q_BLOCK, NSA_KVH, NSA_GROUP, -1), m_sel)
        o_sel = jnp.einsum("bqhgk,bqhkd->bqhgd", p_sel.astype(vg.dtype),
                           vg.reshape(bsz, Q_BLOCK, NSA_KVH, n_top * SEL_BLOCK, NSA_DH))
        kwb = lax.dynamic_slice_in_dim(kw_pad, start, Q_BLOCK + WINDOW, axis=1)
        vwb = lax.dynamic_slice_in_dim(vw_pad, start, Q_BLOCK + WINDOW, axis=1)
        kpos_w = start - WINDOW + jnp.arange(Q_BLOCK + WINDOW)
        diff = tq[:, None] - kpos_w[None, :]
        m_win = (diff >= 0) & (diff < WINDOW) & (kpos_w[None, :] >= 0)
        s_win = jnp.einsum("bqhgd,bkhd->bqhgk", q_blk, kwb)
        p_win = _masked_softmax(s_win, m_win[None, :, None, None, :])
        o_win = jnp.einsum("bqhgk,bkhd->bqhgd", p_win.astype(vwb.dtype), vwb)
        return o_sel, o_win

    n_qb = seq // Q_BLOCK
    q_blocks = qg.reshape(bsz, n_qb, Q_BLOCK, NSA_KVH, NSA_GROUP, NSA_DH).swapaxes(0, 1)
    idx_blocks = sel_idx.reshape(bsz, n_qb, Q_BLOCK, NSA_KVH, n_top).swapaxes(0, 1)
    o_sel, o_win = lax.map(query_block, (jnp.arange(n_qb), q_blocks, idx_blocks))
    o_sel = o_sel.swapaxes(0, 1).reshape(bsz, seq, NSA_KVH, NSA_GROUP, NSA_DH)
    o_win = o_win.swapaxes(0, 1).reshape(bsz, seq, NSA_KVH, NSA_GROUP, NSA_DH)

    g = jax.nn.sigmoid(gate.reshape(bsz, seq, NSA_KVH, NSA_GROUP, 3))
    o = g[..., 0:1] * o_cmp + g[..., 1:2] * o_sel + g[..., 2:3] * o_win
    return o.reshape(bsz, seq, NSA_W)

def _mem_attn(q, mem, g_mem, w_mem_kv, g_q, g_k):
    bsz, seq = q.shape[:2]
    m_len = mem.shape[1]
    kv = _rmsnorm(mem, g_mem) @ w_mem_kv
    k = _rmsnorm(kv[..., :MEM_W].reshape(bsz, m_len, MEM_HEADS, MEM_DH), g_k)
    v = kv[..., MEM_W:].reshape(bsz, m_len, MEM_HEADS, MEM_DH)
    q = _rmsnorm(q.reshape(bsz, seq, MEM_HEADS, MEM_DH), g_q) * (MEM_DH ** -0.5)
    p = jax.nn.softmax(jnp.einsum("bshd,bmhd->bhsm", q, k).astype(jnp.float32), axis=-1)
    return jnp.einsum("bhsm,bmhd->bshd", p.astype(v.dtype), v).reshape(bsz, seq, MEM_W)

def _moe(t, w_router, b_router, w_gu, b_gu, w_down, b_down):
    bsz, seq, d = t.shape
    tok = t.reshape(-1, d)
    n_tok = tok.shape[0]
    n_rows = n_tok * TOP_K
    logits = (tok @ w_router + b_router).astype(jnp.float32)
    top_val, top_idx = lax.top_k(logits, TOP_K)
    top_w = jax.nn.softmax(top_val, axis=-1)
    flat_e = top_idx.reshape(-1)
    flat_w = top_w.reshape(-1)
    order = jnp.argsort(flat_e)
    sorted_e = flat_e[order]
    counts = jnp.bincount(flat_e, length=N_EXPERTS)
    padded = (counts + MOE_BLOCK - 1) // MOE_BLOCK * MOE_BLOCK
    start = jnp.cumsum(counts) - counts
    pad_end = jnp.cumsum(padded)
    pad_start = pad_end - padded
    dest = pad_start[sorted_e] + jnp.arange(n_rows) - start[sorted_e]
    n_blocks = -(-(n_rows + N_EXPERTS * (MOE_BLOCK - 1)) // MOE_BLOCK)
    cap = n_blocks * MOE_BLOCK
    row_tok = jnp.zeros((cap,), jnp.int32).at[dest].set((order // TOP_K).astype(jnp.int32))
    row_w = jnp.zeros((cap,), jnp.float32).at[dest].set(flat_w[order])
    blk_e = jnp.minimum(jnp.searchsorted(pad_end, jnp.arange(n_blocks) * MOE_BLOCK, side="right"),
                        N_EXPERTS - 1)

    def expert_block(args):
        rows, wts, e = args
        hgu = tok[rows] @ w_gu[e] + b_gu[e]
        gate = jnp.minimum(hgu[:, 0::2], SWIGLU_LIMIT)
        up = jnp.clip(hgu[:, 1::2], -SWIGLU_LIMIT, SWIGLU_LIMIT)
        act = (up + 1.0) * (gate * jax.nn.sigmoid(SWIGLU_ALPHA * gate))
        y = act @ w_down[e] + b_down[e]
        return y.astype(jnp.float32) * wts[:, None]

    ys = lax.map(expert_block, (row_tok.reshape(n_blocks, MOE_BLOCK),
                                row_w.reshape(n_blocks, MOE_BLOCK), blk_e))
    out = jnp.zeros((n_tok, d), jnp.float32).at[row_tok].add(ys.reshape(cap, d))
    return out.astype(t.dtype).reshape(bsz, seq, d)

def _hybrid_layer(x, mem, g_mix, w_in, ml_conv_w, ml_conv_b, ml_b_i, ml_b_f, ml_g_out,
                  nsa_g_q, nsa_g_k, cmp_pos_k, cmp_w1_k, cmp_b1_k, cmp_w2_k,
                  cmp_pos_v, cmp_w1_v, cmp_b1_v, cmp_w2_v, g_mem, w_mem_kv, mem_g_q, mem_g_k,
                  w_br_ml, w_br_nsa, w_br_mem, w_out, g_ffn, w_router, b_router,
                  w_gu, b_gu, w_down, b_down):
    bsz, seq, d = x.shape
    u = _rmsnorm(x, g_mix)
    (ml_q, ml_k, ml_v, ml_o, ml_i, ml_f, n_q, n_kc, n_vc, n_ks, n_vs, n_kw, n_vw, n_gate,
     m_q, br_gate) = _split_cols(u @ w_in, IN_SPLITS)

    qk = jax.nn.silu(_causal_conv(jnp.concatenate([ml_q, ml_k], axis=-1), ml_conv_w, ml_conv_b))

    def mh(t):
        return t.reshape(bsz, seq, ML_HEADS, -1)

    h_ml = _mlstm(mh(qk[..., :ML_W]), mh(qk[..., ML_W:]), mh(ml_v), ml_i + ml_b_i, ml_f + ml_b_f)
    h_ml = (_rmsnorm(h_ml, ml_g_out).astype(x.dtype) * jax.nn.sigmoid(mh(ml_o))).reshape(bsz, seq, -1)

    h_nsa = _nsa(n_q, n_kc, n_vc, n_ks, n_vs, n_kw, n_vw, n_gate, nsa_g_q, nsa_g_k,
                 cmp_pos_k, cmp_w1_k, cmp_b1_k, cmp_w2_k, cmp_pos_v, cmp_w1_v, cmp_b1_v, cmp_w2_v)

    h_mem = _mem_attn(m_q, mem, g_mem, w_mem_kv, mem_g_q, mem_g_k)

    gates = jax.nn.sigmoid(br_gate.reshape(bsz, seq, N_BRANCH, d))
    merged = (gates[:, :, 0] * (h_ml @ w_br_ml) + gates[:, :, 1] * (h_nsa @ w_br_nsa)
              + gates[:, :, 2] * (h_mem @ w_br_mem))
    x = x + merged @ w_out
    return x + _moe(_rmsnorm(x, g_ffn), w_router, b_router, w_gu, b_gu, w_down, b_down)

def setup_inputs(seed: int = 0) -> dict:
    key = jax.random.key(seed)
    keys = iter(jax.random.split(key, 40))
    L, D = DEPTH, D_MODEL

    def normal(shape, scale):
        return jax.random.normal(next(keys), shape, jnp.float32) * scale

    def gain(shape):
        return 1.0 + normal(shape, 0.02)

    return {
        "x": normal((BATCH, SEQ, D), 1.0),
        "mem": normal((BATCH, MEM_LEN, D), 1.0),
        "g_mix": gain((L, D)),
        "w_in": normal((L, D, D_IN), D ** -0.5),
        "ml_conv_w": normal((L, ML_CONV, 2 * ML_W), ML_CONV ** -0.5),
        "ml_conv_b": normal((L, 2 * ML_W), 0.02),
        "ml_b_i": normal((L, ML_HEADS), 0.1),
        "ml_b_f": jnp.linspace(3.0, 6.0, ML_HEADS, dtype=jnp.float32)[None, :] + normal((L, ML_HEADS), 0.1),
        "ml_g_out": gain((L, ML_HEADS, ML_DV)),
        "nsa_g_q": gain((L, NSA_DH)),
        "nsa_g_k": gain((L, 3, NSA_DH)),
        "cmp_pos_k": normal((L, CMP_BLOCK, NSA_DH), 0.1),
        "cmp_w1_k": normal((L, CMP_BLOCK, NSA_DH, CMP_HIDDEN), (CMP_BLOCK * NSA_DH) ** -0.5),
        "cmp_b1_k": normal((L, CMP_HIDDEN), 0.02),
        "cmp_w2_k": normal((L, CMP_HIDDEN, NSA_DH), CMP_HIDDEN ** -0.5),
        "cmp_pos_v": normal((L, CMP_BLOCK, NSA_DH), 0.1),
        "cmp_w1_v": normal((L, CMP_BLOCK, NSA_DH, CMP_HIDDEN), (CMP_BLOCK * NSA_DH) ** -0.5),
        "cmp_b1_v": normal((L, CMP_HIDDEN), 0.02),
        "cmp_w2_v": normal((L, CMP_HIDDEN, NSA_DH), CMP_HIDDEN ** -0.5),
        "g_mem": gain((L, D)),
        "w_mem_kv": normal((L, D, 2 * MEM_W), D ** -0.5),
        "mem_g_q": gain((L, MEM_DH)),
        "mem_g_k": gain((L, MEM_DH)),
        "w_br_ml": normal((L, ML_HEADS * ML_DV, D), (ML_HEADS * ML_DV) ** -0.5),
        "w_br_nsa": normal((L, NSA_W, D), NSA_W ** -0.5),
        "w_br_mem": normal((L, MEM_W, D), MEM_W ** -0.5),
        "w_out": normal((L, D, D), D ** -0.5),
        "g_ffn": gain((L, D)),
        "w_router": normal((L, D, N_EXPERTS), D ** -0.5),
        "b_router": normal((L, N_EXPERTS), 0.01),
        "w_gu": normal((L, N_EXPERTS, D, 2 * D_FF), D ** -0.5),
        "b_gu": normal((L, N_EXPERTS, 2 * D_FF), 0.01),
        "w_down": normal((L, N_EXPERTS, D_FF, D), D_FF ** -0.5),
        "b_down": normal((L, N_EXPERTS, D), 0.01),
    }

def reference(x, mem, g_mix, w_in, ml_conv_w, ml_conv_b, ml_b_i, ml_b_f, ml_g_out,
              nsa_g_q, nsa_g_k, cmp_pos_k, cmp_w1_k, cmp_b1_k, cmp_w2_k,
              cmp_pos_v, cmp_w1_v, cmp_b1_v, cmp_w2_v, g_mem, w_mem_kv, mem_g_q, mem_g_k,
              w_br_ml, w_br_nsa, w_br_mem, w_out, g_ffn, w_router, b_router,
              w_gu, b_gu, w_down, b_down):
    h = x
    for l in range(DEPTH):
        h = _hybrid_layer(h, mem, g_mix[l], w_in[l], ml_conv_w[l], ml_conv_b[l], ml_b_i[l], ml_b_f[l],
                          ml_g_out[l], nsa_g_q[l], nsa_g_k[l], cmp_pos_k[l], cmp_w1_k[l], cmp_b1_k[l],
                          cmp_w2_k[l], cmp_pos_v[l], cmp_w1_v[l], cmp_b1_v[l], cmp_w2_v[l], g_mem[l],
                          w_mem_kv[l], mem_g_q[l], mem_g_k[l], w_br_ml[l], w_br_nsa[l], w_br_mem[l],
                          w_out[l], g_ffn[l], w_router[l], b_router[l], w_gu[l], b_gu[l], w_down[l],
                          b_down[l])
    return h


_drawn_inputs = setup_inputs


def setup_inputs(seed=0):
    import zlib

    import numpy as np

    out = dict(_drawn_inputs(seed))
    spreads = {}
    factors = {'ml_b_i': 64.0,
     'ml_g_out': 25.112,
     'nsa_g_q': 65.21,
     'nsa_g_k': 83.194,
     'cmp_pos_k': 8.807,
     'cmp_b1_k': 34.684,
     'cmp_b1_v': 37.448,
     'g_mem': 8.0,
     'mem_g_q': 8.0,
     'mem_g_k': 6.09,
     'b_gu': 40.224,
     'b_down': 46.036,
     'ml_conv_b': 8.0,
     'cmp_pos_v': 8.0,
     'g_ffn': 4.628,
     'b_router': 6.153}
    for name, (base, spread) in spreads.items():
        noise = np.random.default_rng([zlib.crc32(name.encode()), seed]).standard_normal(out[name].shape)
        drawn = base * np.exp(spread * noise) if base else spread * noise
        out[name] = jnp.asarray(drawn.astype(out[name].dtype))
    for name, factor in factors.items():
        out[name] = (out[name] * factor).astype(out[name].dtype)
    return out
```

```python
from contextlib import ExitStack

import numpy as np

import concourse.bass as bass
from concourse import mybir

F32 = mybir.dt.float32
I32 = mybir.dt.int32
ALU = mybir.AluOpType
ACT = mybir.ActivationFunctionType
AX = mybir.AxisListType

P = 128
D = 1024
SEQ = 256
NT = SEQ // P
KT = D // P
NH_ML, DH_ML = 4, 128
QH, KVH, DH = 8, 2, 64
GROUP = QH // KVH
NH_MEM, DH_MEM = 4, 128
CMP_BLOCK, CMP_STRIDE, CMP_HID = 32, 16, 256
NCMP = (SEQ - CMP_BLOCK) // CMP_STRIDE + 1
CONV = 4
NE, TOPK = 32, 4
SLOT_TOK = 64
MAX_OVER = SEQ * TOPK // SLOT_TOK
ITEMS = NE + MAX_OVER
EPS = 1e-6
NEG = -1e30
LIMIT, ALPHA = 7.0, 1.702
UNSEL = -4096.0

C_MLQ, C_V, C_O, C_IF = 0, 1024, 1536, 2048
C_NQ, C_KCVC, C_NKV, C_NG, C_MQ, C_BR = 2056, 2568, 2824, 3336, 3360, 3872

NSLOT = 6
SLOT = 4096


CHUNKS = [("mk", "mk1"), ("mv", "mv1"), ("mq", "mq1"), ("qk0", "qk1"), ("qk1", "qk3"), ("v", "v1"),
          ("o", "o1"), ("nq", "nq1"), ("bgm0", "bgm01"), ("bgm1", "bgm11"), ("nkv", "nkv1"),
          ("kcvc", "kcvc"), ("w1k", "hk"), ("w1v", "hv"), ("bgl0", "bgl01"), ("bgl1", "bgl11"),
          ("wbm", "pm11"), ("wbl", "pl11"), ("bgn0", "bgn01"), ("bgn1", "bgn11"), ("wbn", "pn11"),
          ("wo0", "wo01"), ("wo1", "wo11"), ("wr", "rt")]
SLOT_OF = {name: n % NSLOT for n, (name, _) in enumerate(CHUNKS)}
CHUNK_NO = {name: n for n, (name, _) in enumerate(CHUNKS)}
TRUNK_TURNS = len(CHUNKS) // NSLOT
assert TRUNK_TURNS * NSLOT == len(CHUNKS)


def job_order():
    four = [f"{a}{b}" for a in range(2) for b in range(2)]
    jobs = ["vecT"] + [f"memT{x}" for x in four] + [f"uT{x}" for x in four]
    jobs += ["mk0", "mk1", "mv0", "mv1", "mq0", "mq1", "qk0", "qk1", "qk2", "qk3"]
    jobs += ["mkT0", "mkT1", "v0", "v1", "mqT0", "mqT1", "gif", "ms0", "ms1", "o0", "o1", "gT"]
    jobs += ["mP0", "ms2", "mP1", "ms3", "mo0", "nq0", "nq1", "ngate", "mP2", "mP3", "mo1"]
    jobs += ["ST0", "MB0", "bgm00", "ST1", "MB1", "num0", "bgm01", "ST2", "MB2", "num1",
             "bgm10", "ST3", "MB3", "num2", "bgm11", "num3"]
    jobs += ["nkv0", "nkv1", "kcvc", "nqT0", "nqT1", "hmlT0", "hmlT1", "hk", "hv", "nkT0", "nkT1"]
    jobs += ["bgl00", "bgl01", "kc", "vc", "bgl10", "bgl11", "kcT"]
    jobs += ["sA0", "sB0", "sA1", "sB1"]
    jobs += [f"pm{x}" for x in four]
    filler = {0: [f"pl{x}" for x in four], 1: ["bgn00"], 2: ["bgn01"], 4: ["bgn10"], 5: ["bgn11"]}
    for h in range(QH):
        jobs += [f"tA{h}", f"tB{h}"]
        if h + 2 < QH:
            jobs += [f"sA{h + 2}", f"sB{h + 2}"]
        jobs += filler.get(h, [])
        if h % 2 == 1:
            jobs += [f"nv{h // 2}"]
    jobs += [f"pn{x}" for x in four]
    jobs += [f"mgT{x}" for x in four] + [f"wo{x}" for x in four]
    jobs += [f"xT{x}" for x in four] + ["rt", "rank", "rT", "ov", "it"]
    return jobs


JOBS = job_order()
NB = 8
BANK = {name: n % NB for n, name in enumerate(JOBS)}
TURN = {name: n // NB for n, name in enumerate(JOBS)}
assert len(BANK) == len(JOBS)


def const_table():
    parts, at = {}, 0
    cols = []

    def add(name, a):
        nonlocal at
        full = np.zeros((P, a.shape[1]), np.float32)
        full[:a.shape[0]] = a
        parts[name] = (at, a.shape[1])
        at += a.shape[1]
        cols.append(full)

    p = np.arange(P)
    add("ident", np.eye(P, dtype=np.float32))
    causal = np.where(p[None, :] > p[:, None], np.float32(NEG), np.float32(0)).astype(np.float32)
    add("mask256", np.concatenate([np.zeros((P, P), np.float32), causal], 1))
    add("upper", (p[:, None] <= p[None, :]).astype(np.float32))
    add("strict", (p[:, None] < p[None, :]).astype(np.float32))
    add("ones", np.ones((P, P), np.float32))
    ends = np.arange(NCMP) * CMP_STRIDE + CMP_BLOCK - 1
    ok = np.stack([ends[None, :] <= (p + P * i)[:, None] for i in range(NT)], 1)
    add("cmp01", ok.astype(np.float32).reshape(P, -1))
    add("cmpadd", np.where(ok, np.float32(0), np.float32(NEG)).astype(np.float32).reshape(P, -1))
    half = DH // 2
    inv = np.power(10000.0, (-np.arange(half, dtype=np.float32) / np.float32(half)).astype(np.float64))
    inv = inv.astype(np.float32)

    def rope(pos):
        ang = (pos.astype(np.float32)[:, None] * inv[None, :]).astype(np.float64)
        return np.cos(ang).astype(np.float32), np.sin(ang).astype(np.float32)

    for i in range(NT):
        c, s = rope(p + P * i)
        add(f"cos{i}", c)
        add(f"sin{i}", s)
    c, s = rope(np.tile(ends, KVH))
    add("cosc", c)
    add("sinc", s)
    add("iota", np.tile(np.arange(SLOT_TOK, dtype=np.float32), (P, 2)))
    add("over", np.tile(np.arange(MAX_OVER, dtype=np.float32), (P, 1)))
    add("mhalf", np.full((P, 8), -0.5, np.float32))
    add("pcol", p[:, None].astype(np.float32))
    return np.concatenate(cols, 1), parts


CONST, CPART = const_table()
VROWS = 92


def hybrid_layer(nc, A, const, out):
    with ExitStack() as ctx:
        def sb(name, *shape, dt=F32):
            return ctx.enter_context(nc.sbuf_tensor(name, list(shape), dt))

        sems = {}

        def S(name):
            if name not in sems:
                sems[name] = ctx.enter_context(nc.semaphore(name))
            return sems[name]

        ring = sb("ring", P, NSLOT, SLOT)
        cst = sb("cst", P, CONST.shape[1])
        x_sb = sb("x_sb", P, NT, D)
        uT = sb("uT", P, KT, SEQ)
        mT = sb("mT", P, 2048)
        sc = sb("sc", P, 2048)
        cp = sb("cp", P, 8 * (SEQ + 3))
        qk = sb("qk", P, 8, SEQ)
        vo = sb("vo", P, 2056)
        nkv = sb("nkv", P, NT, 512)
        nqr = sb("nqr", P, 1024)
        mq = sb("mq", P, 2048)
        bg0 = sb("bg0", P, 2048)
        bg1 = sb("bg1", P, 2048)
        sp_ = sb("sp_", P, 3712)
        kcv = sb("kcv", P, 158)
        vcol = sb("vcol", P, VROWS)
        bcg = sb("bcg", P, 288)
        st = sb("st", P, 256)
        bif = sb("bif", 4, 2)
        gsb = sb("gsb", P, NT, 24)
        rank_it = sb("rank_it", P, NT, ITEMS + 1)
        w_it = sb("w_it", P, NT, ITEMS)
        idx = sb("idx", 1, 32, dt=I32)

        banks = [ctx.enter_context(nc.psum_tensor(f"bank{i}", [P, 512], F32)) for i in range(NB)]
        bank_full = [S(f"bank_full{i}") for i in range(NB)]
        bank_free = [S(f"bank_free{i}") for i in range(NB)]
        w_full = [S(f"w_full{i}") for i in range(NSLOT)]

        def C(name):
            a, n = CPART[name]
            return cst[:, a:a + n]

        def bank(job):
            return banks[BANK[job]]

        def arrived(eng, job):
            eng.wait_ge(bank_full[BANK[job]], TURN[job] + 1)

        def read(ins, job):
            return ins.then_inc(bank_free[BANK[job]], 1)

        def was_read(eng, job):
            eng.wait_ge(bank_free[BANK[job]], TURN[job] + 1)

        def mid(ap, n):
            return ap.unsqueeze(1).to_broadcast([ap.shape[0], n, ap.shape[1]])

        def last(ap, n):
            return ap.unsqueeze(2).to_broadcast([ap.shape[0], ap.shape[1], n])

        ident = C("ident")
        ones = C("ones")
        memn = sc[:, :].rearrange("p (i d) -> p i d", i=NT)
        un = cp[:, 0:2048].rearrange("p (i d) -> p i d", i=NT)
        memT = mT[:, :].rearrange("p (k t) -> p k t", k=KT)
        merged = mT[:, :].rearrange("p (i d) -> p i d", i=NT)
        mkv = sc[:, :].rearrange("p (i d) -> p i d", i=NT)
        pre = cp[:, :].rearrange("p (j t) -> p j t", j=8)
        x2 = sc[:, :].rearrange("p (i d) -> p i d", i=NT)
        vaug = vo[:, 0:NT * 4 * 129].rearrange("p (i h e) -> p i h e", i=NT, h=4)
        osig = vo[:, 1032:2056].rearrange("p (i n) -> p i n", i=NT)
        k2 = vo[:, 0:1024].rearrange("p (b h t) -> p b h t", b=2, h=2)
        blk = vo[:, 1024:1984].rearrange("p (b m h n) -> p b m h n", b=2, m=16, h=2)
        vec = bg0[0:VROWS, 0:P]
        wif = bg0[:, 128:192].rearrange("p (k n) -> p k n", k=KT)
        wng = bg0[:, 192:384].rearrange("p (k n) -> p k n", k=KT)
        rows = bg1[0:4, 0:1280]
        nq_sb = nqr[:, :].rearrange("p (i n) -> p i n", i=NT)
        heads = sc[:, :].rearrange("p (i k t) -> p i k t", i=2, k=4)
        hT_mem = [heads[:, k // 2, k % 2, :] for k in range(4)]
        hT_nsa = [heads[:, k // 2, 2 + k % 2, :] for k in range(4)]
        hT_ml = [nqr[:, 256 * k:256 * k + 256] for k in range(4)]
        mqn = nq_sb
        mqT = mq[:, 0:1024].rearrange("p (h t) -> p h t", h=4)
        mkT = mq[:, 1024:2048].rearrange("p (h t) -> p h t", h=4)
        qT = mq[:, 0:1024].rearrange("p (h t) -> p h t", h=4)
        kT = mq[:, 1024:2048].rearrange("p (b t) -> p b t", b=4)
        kcT, vc = kcv[:, 0:30], kcv[:, 30:158]
        tmp = mT[:, 0:512]
        w2 = mT[:, 512:768].rearrange("p (b f d) -> p b f d", b=2, f=2)
        kcn = mT[:, 768:896]
        hid = mT[:, 896:1016].rearrange("p (b f n) -> p b f n", b=2, f=2)
        hsg = mT[:, 1016:1136].rearrange("p (b f n) -> p b f n", b=2, f=2)
        ksq = mT[:, 1136:1536]
        qr = cp[:, 0:1024].rearrange("p (i n) -> p i n", i=NT)
        kr = cp[:, 1024:2048].rearrange("p (i b g u d) -> p i b g u d", i=NT, b=2, g=2, u=2)
        Pm = [sp_[:, 800 * b:800 * b + 512].rearrange("p (i m) -> p i m", i=NT) for b in range(2)]
        PTm = [sp_[:, 1600 + 1024 * b:1600 + 1024 * b + 512].rearrange("p (m t) -> p m t", m=2) for b in range(2)]
        sqA = sp_[:, 1600:2624].rearrange("p (i n) -> p i n", i=NT)
        sqB = sp_[:, 2624:3648].rearrange("p (i n) -> p i n", i=NT)
        Dt = sp_[:, 0:384]
        wd = [sp_[:, 384:768], sp_[:, 768:1152]]
        num = sp_[:, 1152:2184].rearrange("p (h i e) -> p h i e", h=4, i=NT)
        hml = sp_[:, 2184:3208].rearrange("p (i h e) -> p i h e", i=NT, h=4)
        Sn = [sp_[:, 800 * b:800 * b + 798] for b in range(2)]
        PTn = [sp_[:, 1600 + 1024 * b:2624 + 1024 * b] for b in range(2)]

        g_q, g_k = bcg[:, 0:64], bcg[:, 64:256]
        g_ml, g_mq, g_mk = bg1[:, 1280:1792], bg1[:, 1792:1920], bg1[:, 1920:2048]
        b_r = bcg[:, 256:288]
        g_ffn = bg1[:, 0:1024]
        b_dn = nqr[0:32, :]

        r_f, r_B, r_g, r_M, r_nm = (rows[:, 256 * n:256 * n + 256] for n in range(5))

        Gm = sp_[:, 0:128].rearrange("p (i n) -> p i n", i=NT)
        Gw = sp_[:, 128:384].rearrange("p (i n) -> p i n", i=NT)
        STs = sp_[:, 384:640]
        xgT = sp_[:, 640:1152].rearrange("p (c n) -> p c n", c=KT)
        gt = [sp_[:, 1152 + 256 * b:1408 + 256 * b] for b in range(2)]
        ut = [sp_[:, 1664 + 256 * b:1920 + 256 * b] for b in range(2)]
        sg = [sp_[:, 2176 + 256 * b:2432 + 256 * b] for b in range(2)]
        act_sb = sp_[:, 2688:3200]
        actT = sp_[:, 3200:3712]
        y_sb = mq[:, 0:512]
        brow = bg0[0:1, :]
        lg = bg1[:, 1024:1088].rearrange("p (i e) -> p i e", i=NT)
        top = bg1[:, 1088:1104].rearrange("p (i e) -> p i e", i=NT)
        sel = bg1[:, 1104:1168].rearrange("p (i e) -> p i e", i=NT)
        eqv = bg1[:, 1168:1232].rearrange("p (i e) -> p i e", i=NT)
        cum = bg1[:, 1232:1296].rearrange("p (i e) -> p i e", i=NT)
        ngt = bg1[:, 1296:1298]
        rTs = mq[0:32, 512:1024]
        nov = bg1[0:32, 1300:1301]
        ost = bg1[0:32, 1302:1303]
        oen = bg1[0:32, 1304:1305]
        ovs = bg1[0:32, 1306:1307]
        Eov = bg1[0:32, 1312:1312 + MAX_OVER]
        Aov = bg1[0:32, 1328:1328 + MAX_OVER]
        cntc = bg1[0:32, 1344:1347]

        ACC = [[banks[2 * i + h] for h in range(2)] for i in range(NT)]
        BG, BX, BH = banks[4], banks[5], [banks[6], banks[7]]

        w_in = A["w_in"][0]
        w_mkv = A["w_mem_kv"][0]
        w_gu, b_gu, w_dn = A["w_gu"][0], A["b_gu"][0], A["w_down"][0]

        block = ctx.enter_context(nc.Block())

        def item_chunks(eng, e):
            for q in range(4):
                yield (ring[:, q, :].rearrange("p (c n) -> p c n", c=2),
                       w_gu[e].rearrange("(c p) n -> p c n", p=P)[:, 2 * q:2 * q + 2, :])
            for d in range(2):
                yield (ring[:, 4 + d, :].rearrange("p (c n) -> p c n", c=4),
                       w_dn[e].rearrange("(c p) n -> p c n", p=P)[:, 4 * d:4 * d + 4, :])

        @block.sync
        def _(sp):
            sp.dma_start(memn, A["mem"][0].rearrange("(i p) d -> p i d", p=P)).then_inc(S("mem_in"), 16)
            sp.dma_start(x_sb[:, :, :], A["x"][0].rearrange("(i p) d -> p i d", p=P)).then_inc(S("x_in"), 16)

            def cols(a, c0, n=512):
                return a[:, c0:c0 + n].rearrange("(c p) n -> p c n", p=P)

            src = {
                "mk": cols(w_mkv, 0), "mv": cols(w_mkv, 512), "mq": cols(w_in, C_MQ),
                "qk0": cols(w_in, 0), "qk1": cols(w_in, 512), "v": cols(w_in, C_V), "o": cols(w_in, C_O),
                "nq": cols(w_in, C_NQ), "nkv": cols(w_in, C_NKV), "kcvc": cols(w_in, C_KCVC, 256),
                "w1k": A["cmp_w1_k"][0].rearrange("(m l) d f -> (l d) m f", l=2),
                "w1v": A["cmp_w1_v"][0].rearrange("(m l) d f -> (l d) m f", l=2),
                "wbm": cols(A["w_br_mem"][0], 0, D), "wbl": cols(A["w_br_ml"][0], 0, D),
                "wbn": cols(A["w_br_nsa"][0], 0, D),
                "wo0": cols(A["w_out"][0], 0), "wo1": cols(A["w_out"][0], 512),
                "wr": A["w_router"][0].rearrange("(c p) n -> p c n", p=P),
            }
            for b, name in enumerate(("bgl", "bgn", "bgm")):
                for h in range(2):
                    src[f"{name}{h}"] = cols(w_in, C_BR + D * b + 512 * h)
            for n, (name, _) in enumerate(CHUNKS):
                s = src[name]
                if n >= NSLOT:
                    arrived(sp, CHUNKS[n - NSLOT][1])
                dst = ring[:, n % NSLOT, 0:s.shape[1] * s.shape[2]].rearrange("p (c n) -> p c n", c=s.shape[1])
                sp.dma_start(dst, s).then_inc(w_full[n % NSLOT], 16)
            for q, (dst, s) in enumerate(item_chunks(sp, 0)):
                arrived(sp, CHUNKS[len(CHUNKS) - NSLOT + q][1])
                sp.dma_start(dst, s).then_inc(w_full[q], 16)

            arrived(sp, "pn11")
            sp.wait_ge(S("merged"), 8)
            sp.dma_start(brow, b_gu[0:1, :]).then_inc(S("brow_in"), 16)

            def load_item(i, e):
                sp.wait_ge(S("brow_used"), i)
                sp.dma_start(brow, b_gu[bass.ds(e, 1), :]).then_inc(S("brow_in"), 16)
                for q, (dst, s) in enumerate(item_chunks(sp, e)):
                    if q < 4:
                        sp.wait_ge(S("gu_done"), i * 4 + (q - 3))
                    else:
                        sp.wait_ge(S("down_done"), i * 2 + (q - 5))
                    sp.dma_start(dst, s).then_inc(w_full[q], 16)

            with sp.Fori(1, NE) as e:
                load_item(e, e)
            sp.wait_ge(S("idx_ready"), 1)
            n_over = sp.value_load(idx[0:1, 16:17], min_val=0, max_val=MAX_OVER)
            with sp.If(n_over > 0):
                with sp.Fori(0, n_over) as k:
                    e = sp.value_load(idx[0:1, bass.ds(k, 1)], min_val=0, max_val=NE - 1)
                    load_item(k + NE, e)
            for i in range(NT):
                sp.wait_ge(S("out_ready"), i + 1)
                sp.dma_start(out[0].rearrange("(i p) d -> p i d", p=P)[:, i, :], x_sb[:, i, :]).then_inc(S("out_done"), 16)
            sp.wait_ge(S("out_done"), 16 * NT)

        @block.gpsimd
        def _(pool):
            pool.dma_start(cst[:, :], const).then_inc(S("cst_in"), 16)

            def row(a, r, n):
                pool.dma_start(vec[r:r + n, :], a).then_inc(S("vec_in"), 16)

            row(A["g_mix"].rearrange("a (n p) -> (a n) p", p=P), 0, 8)
            row(A["g_mem"].rearrange("a (n p) -> (a n) p", p=P), 8, 8)
            row(A["ml_conv_w"][0].rearrange("j (n p) -> (j n) p", p=P), 16, 32)
            row(A["ml_conv_b"].rearrange("a (n p) -> (a n) p", p=P), 48, 8)
            row(A["cmp_b1_k"].rearrange("a (n p) -> (a n) p", p=P), 56, 2)
            row(A["cmp_b1_v"].rearrange("a (n p) -> (a n) p", p=P), 58, 2)
            row(A["cmp_pos_k"][0].rearrange("(m l) d -> m (l d)", l=2), 60, 16)
            row(A["cmp_pos_v"][0].rearrange("(m l) d -> m (l d)", l=2), 76, 16)
            pool.dma_start(wif, w_in[:, C_IF:C_IF + 8].rearrange("(c p) n -> p c n", p=P)).then_inc(S("small_in"), 16)
            pool.dma_start(wng, w_in[:, C_NG:C_NG + 24].rearrange("(c p) n -> p c n", p=P)).then_inc(S("small_in"), 16)
            pool.dma_start(bif[:, 0:1], A["ml_b_i"].rearrange("a h -> h a")).then_inc(S("small_in"), 16)
            pool.dma_start(bif[:, 1:2], A["ml_b_f"].rearrange("a h -> h a")).then_inc(S("small_in"), 16)

            def everywhere(dst, a):
                pool.dma_start(dst, a.partition_broadcast(P)).then_inc(S("bc_in"), 16)

            everywhere(g_q, A["nsa_g_q"][0])
            everywhere(g_k, A["nsa_g_k"][0].rearrange("b d -> (b d)"))
            everywhere(g_ml, A["ml_g_out"][0].rearrange("b d -> (b d)"))
            everywhere(g_mq, A["mem_g_q"][0])
            everywhere(g_mk, A["mem_g_k"][0])
            everywhere(b_r, A["b_router"][0])
            powers = [0]

            def power(ap):
                powers[0] += 1
                pool.wait_ge(S("mean_ready"), powers[0])
                nc.gpsimd.tensor_tensor(ap, ap, C("mhalf")[0:ap.shape[0], 0:ap.shape[1]], ALU.pow).then_inc(S("rstd_done"), 1)

            pool.wait_ge(S("cst_in"), 16)
            for c in range(8, 12):
                power(st[:, c:c + 1])
            for c in range(16, 32, 4):
                power(st[:, c:c + 4])
            arrived(pool, "mv1")
            pool.dma_start(w2[:, 0], A["cmp_w2_k"][0].rearrange("(f p) d -> p f d", p=P)).then_inc(S("w2_in"), 16)
            pool.dma_start(w2[:, 1], A["cmp_w2_v"][0].rearrange("(f p) d -> p f d", p=P)).then_inc(S("w2_in"), 16)
            for c in (128, 136):
                power(st[:, c:c + 8])
            power(st[:, 168:176])
            for c in range(144, 152, 2):
                power(st[:, c:c + 2])
            power(st[0:30, 152:153])
            pool.wait_ge(S("merged"), 4)
            pool.dma_start(b_dn, A["b_down"][0]).then_inc(S("bdn_in"), 16)
            pool.dma_start(g_ffn, A["g_ffn"][0].partition_broadcast(P)).then_inc(S("gffn_in"), 16)
            for c in (12, 13):
                power(st[:, c:c + 1])

        @block.tensor
        def _(pe):
            at = [0]

            def begin(job):
                assert JOBS[at[0]] == job, (job, JOBS[at[0]])
                at[0] += 1
                if TURN[job] >= 1:
                    pe.wait_ge(bank_free[BANK[job]], TURN[job])
                return banks[BANK[job]]

            def done(mm, job):
                mm.then_inc(bank_full[BANK[job]], 1)

            def chunk(name):
                n = CHUNK_NO[name]
                pe.wait_ge(w_full[n % NSLOT], 16 * (n // NSLOT + 1))
                return ring[:, n % NSLOT, :]

            def transposes(job, parts):
                b = begin(job)
                for o, a in parts:
                    mm = nc.tensor.transpose(b[0:a.shape[1], o:o + a.shape[0]], a, ident[0:a.shape[0], 0:a.shape[0]])
                done(mm, job)

            def tiles(a):
                return [a[:, k, :] for k in range(KT)]

            def natural(jobs, w, n, src=tiles(uT), kt=KT, c0=0):
                for i, job in jobs:
                    b = begin(job)
                    for k in range(kt):
                        mm = nc.tensor.matmul(b[:, 0:n], src[k][:, P * i:P * i + P], w[:, k, c0:c0 + n],
                                              start=k == 0, stop=k == kt - 1)
                    done(mm, job)

            def slot3(name, kt, n):
                return chunk(name)[:, 0:kt * n].rearrange("p (k n) -> p k n", k=kt)

            pe.wait_ge(S("cst_in"), 16)
            pe.wait_ge(S("vec_in"), 16 * 8)
            transposes("vecT", [(0, vec)])
            for i in range(NT):
                pe.wait_ge(S("mem_norm"), i + 1)
                for h in range(2):
                    transposes(f"memT{i}{h}", [(P * k, memn[:, i, P * (4 * h + k):P * (4 * h + k) + P]) for k in range(4)])
            for i in range(NT):
                pe.wait_ge(S("x_norm"), i + 1)
                for h in range(2):
                    transposes(f"uT{i}{h}", [(P * k, un[:, i, P * (4 * h + k):P * (4 * h + k) + P]) for k in range(4)])
            for x in ("00", "01", "10", "11"):
                was_read(pe, f"memT{x}")
            for part in ("mk", "mv"):
                natural([(i, f"{part}{i}") for i in range(NT)], slot3(part, KT, 512), 512, src=tiles(memT))
            for x in ("00", "01", "10", "11"):
                was_read(pe, f"uT{x}")
            natural([(i, f"mq{i}") for i in range(NT)], slot3("mq", KT, 512), 512)
            for n in range(4):
                w = slot3(f"qk{n // 2}", KT, 512)
                b = begin(f"qk{n}")
                for j in range(2):
                    c0 = 256 * (n % 2) + P * j
                    for k in range(KT):
                        mm = nc.tensor.matmul(b[:, 256 * j:256 * j + 256], w[:, k, c0:c0 + P], uT[:, k, :],
                                              start=k == 0, stop=k == KT - 1)
                done(mm, f"qk{n}")
            pe.wait_ge(S("mk_norm"), 1)
            for i in range(NT):
                transposes(f"mkT{i}", [(P * h, mkv[:, i, P * h:P * h + P]) for h in range(4)])
            natural([(i, f"v{i}") for i in range(NT)], slot3("v", KT, 512), 512)
            pe.wait_ge(S("mq_norm"), 1)
            for i in range(NT):
                transposes(f"mqT{i}", [(P * h, mqn[:, i, P * h:P * h + P]) for h in range(4)])
            pe.wait_ge(S("small_in"), 16 * 4)
            b = begin("gif")
            for j in range(2):
                for k in range(KT):
                    mm = nc.tensor.matmul(b[0:4, 256 * j:256 * j + 256], wif[:, k, 4 * j:4 * j + 4], uT[:, k, :],
                                          start=k == 0, stop=k == KT - 1)
            done(mm, "gif")
            for i in range(NT):
                was_read(pe, f"mkT{i}")
                was_read(pe, f"mqT{i}")

            def mem_scores(h):
                b = begin(f"ms{h}")
                for i in range(NT):
                    mm = nc.tensor.matmul(b[:, 256 * i:256 * i + 256], mqT[:, h, P * i:P * i + P], mkT[:, h, :],
                                          start=True, stop=True)
                done(mm, f"ms{h}")

            def mem_turn(h):
                pe.wait_ge(S("memP"), h + 1)
                transposes(f"mP{h}", [(256 * m + P * i, Pm[h % 2][:, i, P * m:P * m + P]) for m in range(2) for i in range(NT)])

            def mem_out(pair):
                b = begin(f"mo{pair}")
                for j in range(2):
                    h = 2 * pair + j
                    was_read(pe, f"mP{h}")
                    for m in range(2):
                        mm = nc.tensor.matmul(b[:, 256 * j:256 * j + 256], mkv[:, m, 512 + P * h:512 + P * h + P],
                                              PTm[h % 2][:, m, :], start=m == 0, stop=m == 1)
                done(mm, f"mo{pair}")

            mem_scores(0)
            mem_scores(1)
            natural([(i, f"o{i}") for i in range(NT)], slot3("o", KT, 512), 512)
            pe.wait_ge(S("rows_ready"), 1)
            transposes("gT", [(4 * i, r_g[:, P * i:P * i + P]) for i in range(NT)]
                       + [(8 + 4 * i, r_nm[:, P * i:P * i + P]) for i in range(NT)])
            mem_turn(0)
            mem_scores(2)
            mem_turn(1)
            mem_scores(3)
            mem_out(0)
            natural([(i, f"nq{i}") for i in range(NT)], slot3("nq", KT, 512), 512)
            b = begin("ngate")
            for i in range(NT):
                for k in range(KT):
                    mm = nc.tensor.matmul(b[:, 24 * i:24 * i + 24], uT[:, k, P * i:P * i + P], wng[:, k, :],
                                          start=k == 0, stop=k == KT - 1)
            done(mm, "ngate")
            mem_turn(2)
            mem_turn(3)
            mem_out(1)

            def ml_scores(h):
                b = begin(f"ST{h}")
                nc.tensor.matmul(b[:, 0:256], qk[:, 4 + h, 0:P], qk[:, h, :], start=True, stop=True)
                mm = nc.tensor.matmul(b[:, 256:384], qk[:, 4 + h, P:SEQ], qk[:, h, P:SEQ], start=True, stop=True)
                done(mm, f"ST{h}")
                b = begin(f"MB{h}")
                mm = nc.tensor.matmul(b[:, 0:256], ident[0:4, h:h + 1].to_broadcast([4, P]), r_M, start=True, stop=True)
                done(mm, f"MB{h}")

            def ml_out(h):
                pe.wait_ge(S("wd_ready"), h + 1)
                b = begin(f"num{h}")
                w = wd[h % 2]
                nc.tensor.matmul(b[:, 0:129], w[:, 0:P], vaug[:, 0, h, :], start=True, stop=True)
                nc.tensor.matmul(b[:, 256:385], w[:, P:256], vaug[:, 0, h, :], start=True, stop=False)
                mm = nc.tensor.matmul(b[:, 256:385], w[:, 256:384], vaug[:, 1, h, :], start=False, stop=True)
                done(mm, f"num{h}")

            def bgate(name, hh, i):
                w = slot3(f"{name}{hh}", KT, 512)
                natural([(i, f"{name}{hh}{i}")], w, 512)

            pe.wait_ge(S("qk_ready"), 2)
            pe.wait_ge(S("ones_col"), 1)
            was_read(pe, "v0")
            was_read(pe, "v1")
            ml_scores(0)
            bgate("bgm", 0, 0)
            ml_scores(1)
            ml_out(0)
            bgate("bgm", 0, 1)
            ml_scores(2)
            ml_out(1)
            bgate("bgm", 1, 0)
            ml_scores(3)
            ml_out(2)
            bgate("bgm", 1, 1)
            ml_out(3)

            natural([(i, f"nkv{i}") for i in range(NT)], slot3("nkv", KT, 512), 512)
            w = slot3("kcvc", KT, 256)
            b = begin("kcvc")
            for j in range(2):
                for k in range(KT):
                    mm = nc.tensor.matmul(b[:, 256 * j:256 * j + 256], w[:, k, P * j:P * j + P], uT[:, k, :],
                                          start=k == 0, stop=k == KT - 1)
            done(mm, "kcvc")
            pe.wait_ge(S("q_roped"), 1)
            for i in range(NT):
                transposes(f"nqT{i}", [(P * j, qr[:, i, P * j:P * j + P]) for j in range(4)])
            pe.wait_ge(S("hml_ready"), 1)
            for i in range(NT):
                transposes(f"hmlT{i}", [(P * h, hml[:, i, h, :]) for h in range(4)])
            for n, (name, job) in enumerate((("w1k", "hk"), ("w1v", "hv"))):
                w = slot3(name, 16, CMP_HID)
                pe.wait_ge(S("blk_ready"), 2 * n + 2)
                b = begin(job)
                for f in range(2):
                    for m in range(16):
                        mm = nc.tensor.matmul(b[:, 30 * f:30 * f + 30], w[:, m, P * f:P * f + P],
                                              blk[:, n, m].rearrange("p h n -> p (h n)"), start=m == 0, stop=m == 15)
                done(mm, job)
            pe.wait_ge(S("k_roped"), 1)
            for i in range(NT):
                transposes(f"nkT{i}", [(P * (2 * br + g), kr[:, i, br, g].rearrange("p u d -> p (u d)"))
                                       for br in range(2) for g in range(2)])
            bgate("bgl", 0, 0)
            bgate("bgl", 0, 1)
            pe.wait_ge(S("hid_ready"), 1)
            pe.wait_ge(S("w2_in"), 32)
            b = begin("kc")
            for f in range(2):
                mm = nc.tensor.matmul(b[0:30, 0:DH], hid[:, 0, f, :], w2[:, 0, f, :], start=f == 0, stop=f == 1)
            done(mm, "kc")
            pe.wait_ge(S("hid_ready"), 2)
            b = begin("vc")
            for g in range(2):
                for f in range(2):
                    mm = nc.tensor.matmul(b[0:NCMP, DH * g:DH * g + DH], hid[:, 1, f, NCMP * g:NCMP * g + NCMP],
                                          w2[:, 1, f, :], start=f == 0, stop=f == 1)
            done(mm, "vc")
            bgate("bgl", 1, 0)
            bgate("bgl", 1, 1)
            pe.wait_ge(S("kc_roped"), 1)
            transposes("kcT", [(0, kcn[0:30, :])])
            for x in ("nqT0", "nqT1", "nkT0", "nkT1", "vc", "kcT"):
                was_read(pe, x)

            def nsa_scores(h):
                r, j, g = DH * (h % 2), h // 2, h // GROUP
                q = [qT[r:r + DH, j, P * i:P * i + P] for i in range(NT)]
                b = begin(f"sA{h}")
                for br in range(2):
                    mm = nc.tensor.matmul(b[:, 256 * br:256 * br + 256], q[1], kT[r:r + DH, 2 * br + g, :], start=True, stop=True)
                done(mm, f"sA{h}")
                b = begin(f"sB{h}")
                for br in range(2):
                    nc.tensor.matmul(b[:, P * br:P * br + P], q[0], kT[r:r + DH, 2 * br + g, 0:P], start=True, stop=True)
                for i in range(NT):
                    o = 256 + NCMP * i
                    mm = nc.tensor.matmul(b[:, o:o + NCMP], q[i], kcT[r:r + DH, NCMP * g:NCMP * g + NCMP], start=True, stop=True)
                done(mm, f"sB{h}")

            def nsa_turn(h):
                pe.wait_ge(S("nsaP"), h + 1)
                s = Sn[h % 2]
                for br, job in enumerate((f"tA{h}", f"tB{h}")):
                    transposes(job, [(0, s[:, 512 + P * br:512 + P * br + P]),
                                     (P, s[:, 256 * br:256 * br + P]),
                                     (256, s[:, 256 * br + P:256 * br + 256]),
                                     (384, s[:, 768 + NCMP * br:768 + NCMP * br + NCMP])])

            def nsa_out(h):
                r, g = DH * (h % 2), h // GROUP
                was_read(pe, f"tA{h}")
                was_read(pe, f"tB{h}")
                if h % 2 == 0:
                    return
                b = begin(f"nv{h // 2}")
                for hh in (h - 1, h):
                    r, t = DH * (hh % 2), PTn[hh % 2]
                    o = b[r:r + DH, :]
                    for br in range(2):
                        v = nkv[:, :, 256 * br + P + DH * g:256 * br + P + DH * g + DH]
                        nc.tensor.matmul(o[:, 0:256], v[:, 0, :], t[:, 384 * br:384 * br + 256], start=br == 0, stop=False)
                        nc.tensor.matmul(o[:, P:256], v[:, 1, :], t[:, 384 * br + 256:384 * br + 384], start=False, stop=False)
                    mm = nc.tensor.matmul(o[:, 0:256], vc[0:NCMP, DH * g:DH * g + DH], t[0:NCMP, 768:1024], start=False, stop=True)
                done(mm, f"nv{h // 2}")

            def project(name, wname, hT):
                w = slot3(wname, 4, D)
                for i in range(NT):
                    for hh in range(2):
                        natural([(i, f"{name}{i}{hh}")], w, 512, src=hT, kt=4, c0=512 * hh)

            nsa_scores(0)
            nsa_scores(1)
            was_read(pe, "mo0")
            was_read(pe, "mo1")
            project("pm", "wbm", hT_mem)
            for h in range(QH):
                nsa_turn(h)
                if h + 2 < QH:
                    nsa_scores(h + 2)
                if h == 0:
                    was_read(pe, "hmlT0")
                    was_read(pe, "hmlT1")
                    project("pl", "wbl", hT_ml)
                if h in (1, 2):
                    bgate("bgn", 0, h - 1)
                if h in (4, 5):
                    bgate("bgn", 1, h - 4)
                nsa_out(h)
            for j in range(4):
                was_read(pe, f"nv{j}")
            project("pn", "wbn", hT_nsa)

            for i in range(NT):
                pe.wait_ge(S("merged"), 4 + 2 * i + 2)
                for h in range(2):
                    transposes(f"mgT{i}{h}", [(P * k, merged[:, i, P * (4 * h + k):P * (4 * h + k) + P]) for k in range(4)])
            for x in ("00", "01", "10", "11"):
                was_read(pe, f"mgT{x}")
            for hh in range(2):
                natural([(i, f"wo{hh}{i}") for i in range(NT)], slot3(f"wo{hh}", KT, 512), 512, src=tiles(qk))
            for i in range(NT):
                pe.wait_ge(S("x2_ready"), i + 1)
                for h in range(2):
                    transposes(f"xT{i}{h}", [(P * k, x2[:, i, P * (4 * h + k):P * (4 * h + k) + P]) for k in range(4)])
            for x in ("00", "01", "10", "11"):
                was_read(pe, f"xT{x}")
            w = slot3("wr", KT, NE)
            b = begin("rt")
            for i in range(NT):
                for k in range(KT):
                    mm = nc.tensor.matmul(b[:, NE * i:NE * i + NE], uT[:, k, P * i:P * i + P], w[:, k, :],
                                          start=k == 0, stop=k == KT - 1)
            done(mm, "rt")
            pe.wait_ge(S("sel_ready"), 1)
            b = begin("rank")
            nc.tensor.matmul(b[:, 0:NE], C("strict"), sel[:, 0, :], start=True, stop=True)
            nc.tensor.matmul(b[:, NE:2 * NE], ones, sel[:, 0, :], start=True, stop=False)
            nc.tensor.matmul(b[:, NE:2 * NE], C("strict"), sel[:, 1, :], start=False, stop=True)
            for i in range(NT):
                mm = nc.tensor.matmul(b[0:NE, 64:65], sel[:, i, :], ones[:, 0:1], start=i == 0, stop=i == NT - 1)
            done(mm, "rank")
            pe.wait_ge(S("rank_ready"), 1)
            transposes("rT", [(P * i, rank_it[:, i, 0:NE]) for i in range(NT)]
                       + [(256 + P * i, w_it[:, i, 0:NE]) for i in range(NT)])
            b = begin("ov")
            nc.tensor.matmul(b[0:NE, 0:1], C("strict")[0:NE, 0:NE], nov, start=True, stop=True)
            mm = nc.tensor.matmul(b[0:1, 1:2], nov, ones[0:NE, 0:1], start=True, stop=True)
            done(mm, "ov")
            pe.wait_ge(S("over_ready"), 1)
            b = begin("it")
            for i in range(NT):
                o = MAX_OVER * i
                nc.tensor.matmul(b[:, o:o + MAX_OVER], rTs[:, P * i:P * i + P], Eov, start=True, stop=False)
                nc.tensor.matmul(b[:, o:o + MAX_OVER], ones[0:NE, :], Aov, start=False, stop=True)
            for i in range(NT):
                o = MAX_OVER * (2 + i)
                nc.tensor.matmul(b[:, o:o + MAX_OVER], rTs[:, 256 + P * i:256 + P * i + P], Eov, start=True, stop=True)
            mm = nc.tensor.matmul(b[0:1, 64:64 + MAX_OVER], C("pcol")[0:NE, :], Eov, start=True, stop=True)
            done(mm, "it")
            assert at[0] == len(JOBS)
            for name in JOBS[-NB:]:
                was_read(pe, name)

            pe.wait_ge(S("bdn_in"), 16)
            for i in range(NT):
                for hh in range(2):
                    nc.tensor.matmul(ACC[i][hh][:, :], rTs[:, 256 + P * i:256 + P * i + P],
                                     b_dn[:, 512 * hh:512 * hh + 512], start=True, stop=False, skip_group_check=True)

            def gather():
                for c in range(KT):
                    for i in range(NT):
                        mm = nc.tensor.matmul(BG[:, 64 * c:64 * c + 64], x2[:, i, P * c:P * c + P], Gm[:, i, :],
                                              start=i == 0, stop=i == NT - 1)
                mm.then_inc(S("g_full"), 1)

            pe.wait_ge(S("G_ready"), 1)
            gather()

            def item(i):
                pe.wait_ge(S("g_evac"), i * 2 + 1)
                pe.wait_ge(S("brow_in"), i * 16 + 16)
                for b in range(2):
                    for hh in range(2):
                        o = 1024 * b + 512 * hh
                        mm = nc.tensor.matmul(BH[b][64 * hh:64 * hh + 64, :], ones[0:1, 0:64], brow[:, o:o + 512],
                                              start=True, stop=False, skip_group_check=True)
                mm.then_inc(S("brow_used"), 1)
                for q in range(4):
                    pe.wait_ge(w_full[q], i * 16 + 16 * (TRUNK_TURNS + 1))
                    w = ring[:, q, :].rearrange("p (c n) -> p c n", c=2)
                    for c in range(2):
                        k = 2 * q + c
                        for b in range(2):
                            for hh in range(2):
                                o = 1024 * b + 512 * hh
                                mm = nc.tensor.matmul(BH[b][64 * hh:64 * hh + 64, :], xgT[:, k, :], w[:, c, o:o + 512],
                                                      start=False, stop=k == KT - 1, skip_group_check=True)
                    mm.then_inc(S("gu_done"), 1)
                pe.wait_ge(S("Gw_ready"), i + 1)
                for t in range(NT):
                    mm = nc.tensor.transpose(BX[:, P * t:P * t + P], Gw[:, t, :], ident)
                mm.then_inc(S("x_full"), 1)
                pe.wait_ge(S("G_ready"), i + 2)
                gather()
                pe.wait_ge(S("act_ready"), i * 2 + 2)
                pe.wait_ge(S("x_evac"), i * 2 + 1)
                for q in range(4):
                    mm = nc.tensor.transpose(BX[:, P * q:P * q + P], act_sb[:, P * q:P * q + P], ident)
                mm.then_inc(S("x_full"), 1)
                pe.wait_ge(S("x_evac"), i * 2 + 2)
                pe.wait_ge(S("g_evac"), i * 2 + 2)
                for d in range(2):
                    pe.wait_ge(w_full[4 + d], i * 16 + 16 * (TRUNK_TURNS + 1))
                    w = ring[:, 4 + d, :].rearrange("p (c n) -> p c n", c=4)
                    for c in range(4):
                        k = 4 * d + c
                        o = P * (2 * (k // 4) + k % 2) + 64 * ((k // 2) % 2)
                        for hh in range(2):
                            mm = nc.tensor.matmul(BG[64 * hh:64 * hh + 64, :], actT[:, o:o + 64],
                                                  w[:, c, 512 * hh:512 * hh + 512],
                                                  start=k == 0, stop=k == KT - 1, skip_group_check=True)
                    mm.then_inc(S("down_done"), 1)
                pe.wait_ge(S("g_evac"), i * 2 + 3)
                for t in range(NT):
                    for hh in range(2):
                        mm = nc.tensor.matmul(ACC[t][hh][:, :], STs[64 * hh:64 * hh + 64, P * t:P * t + P],
                                              y_sb[64 * hh:64 * hh + 64, :], start=False, stop=False, skip_group_check=True)
                mm.then_inc(S("scattered"), 1)

            with pe.Fori(0, NE) as i:
                item(i)
            pe.wait_ge(S("idx_ready"), 1)
            n_over = pe.value_load(idx[0:1, 16:17], min_val=0, max_val=MAX_OVER)
            with pe.If(n_over > 0):
                with pe.Fori(0, n_over) as k:
                    item(k + NE)
            for t in range(NT):
                for hh in range(2):
                    mm = nc.tensor.matmul(ACC[t][hh][:, :], ident, x_sb[:, t, 512 * hh:512 * hh + 512],
                                          start=False, stop=True, skip_group_check=True)
                mm.then_inc(S("sum_ready"), 1)

        @block.scalar
        def _(act):
            def copy(job, dst, src):
                arrived(act, job)
                read(nc.scalar.activation(dst, src, ACT.Copy), job)

            act.wait_ge(S("mem_in"), 16)
            for i in range(NT):
                nc.scalar.activation(uT[:, 0:4, :].rearrange("p k t -> p (k t)"), memn[:, i, :], ACT.Square,
                                     accum_out=st[:, i:i + 1]).then_inc(S("sumsq"), 1)
                act.wait_ge(S("sumsq"), i + 1)
            act.wait_ge(S("x_in"), 16)
            for i in range(NT):
                nc.scalar.activation(uT[:, 4:8, :].rearrange("p k t -> p (k t)"), x_sb[:, i, :], ACT.Square,
                                     accum_out=st[:, 2 + i:3 + i]).then_inc(S("sumsq"), 1)
                act.wait_ge(S("sumsq"), 3 + i)

            def copy_and_square(job, dst, sq):
                arrived(act, job)
                nc.scalar.activation(dst, bank(job)[:, :], ACT.Copy)
                read(nc.scalar.activation(sq, bank(job)[:, :], ACT.Square), job)

            for x in ("10", "11"):
                arrived(act, f"memT{x}")
            for i in range(NT):
                copy_and_square(f"mk{i}", mkv[:, i, 0:512], sqA[:, i, :])
            for i in range(NT):
                copy(f"mv{i}", mkv[:, i, 512:1024], bank(f"mv{i}")[:, :])
            for i in range(NT):
                copy_and_square(f"mq{i}", mqn[:, i, :], sqB[:, i, :])
            arrived(act, "uT11")
            act.wait_ge(S("pad_zero"), 1)
            for n in range(4):
                copy(f"qk{n}", pre[:, 2 * n:2 * n + 2, 3:3 + SEQ],
                     bank(f"qk{n}")[:, :].rearrange("p (j t) -> p j t", j=2))
            for i in range(NT):
                copy(f"mkT{i}", mkT[:, :, P * i:P * i + P], bank(f"mkT{i}")[:, :].rearrange("p (h t) -> p h t", h=4))
            for i in range(NT):
                copy(f"v{i}", vaug[:, i, :, 0:P], bank(f"v{i}")[:, :].rearrange("p (h t) -> p h t", h=4))
            for i in range(NT):
                copy(f"mqT{i}", mqT[:, :, P * i:P * i + P], bank(f"mqT{i}")[:, :].rearrange("p (h t) -> p h t", h=4))
            for n in range(2):
                act.wait_ge(S("conv_done"), 1)
                nc.scalar.activation(cp[:, 1024 * n:1024 * n + 1024], qk[:, 4 * n:4 * n + 4, :].rearrange("p j t -> p (j t)"),
                                     ACT.Sigmoid).then_inc(S("conv_sig"), 1)
            act.wait_ge(S("absf"), 1)
            nc.scalar.activation(r_B, r_B, ACT.Exp, scale=-1.0).then_inc(S("act_rows"), 1)
            act.wait_ge(S("act_rows"), 1)
            nc.scalar.activation(r_B, r_B, ACT.Ln, bias=1.0).then_inc(S("act_rows"), 1)

            def mem_exp(h):
                act.wait_ge(S("mem_nmax"), h + 1)
                if h >= 2:
                    arrived(act, f"mP{h - 2}")
                for i in range(NT):
                    ins = nc.scalar.activation(Pm[h % 2][:, i, :], bank(f"ms{h}")[:, 256 * i:256 * i + 256], ACT.Exp,
                                               bias=st[:, 32 + 2 * h + i:33 + 2 * h + i],
                                               accum_out=st[:, 40 + 2 * h + i:41 + 2 * h + i])
                read(ins, f"ms{h}")

            def mem_turned(h):
                copy(f"mP{h}", PTm[h % 2], bank(f"mP{h}")[:, :].rearrange("p (m t) -> p m t", m=2))

            act.wait_ge(S("mk_norm"), 1)
            act.wait_ge(S("mq_norm"), 1)
            mem_exp(0)
            mem_exp(1)
            for i in range(NT):
                arrived(act, f"o{i}")
                read(nc.scalar.activation(osig[:, i, :], bank(f"o{i}")[:, :], ACT.Sigmoid), f"o{i}")
            mem_turned(0)
            mem_exp(2)
            mem_turned(1)
            mem_exp(3)
            arrived(act, "mkT1")
            copy("mo0", heads[:, 0, 0:2, :], bank("mo0")[:, :].rearrange("p (h t) -> p h t", h=2))
            for i in range(NT):
                copy(f"nq{i}", nq_sb[:, i, :], bank(f"nq{i}")[:, :])
            arrived(act, "ngate")
            read(nc.scalar.activation(gsb[:, :, :].rearrange("p i n -> p (i n)"), bank("ngate")[:, 0:48], ACT.Sigmoid), "ngate")
            mem_turned(2)
            mem_turned(3)
            copy("mo1", heads[:, 1, 0:2, :], bank("mo1")[:, :].rearrange("p (h t) -> p h t", h=2))

            def gate(name, dst, hh, i):
                job = f"{name}{hh}{i}"
                arrived(act, job)
                read(nc.scalar.activation(dst[:, D * i + 512 * hh:D * i + 512 * hh + 512], bank(job)[:, :], ACT.Sigmoid), job)

            def ml_exp(h):
                was_read(act, f"MB{h}")
                nc.scalar.activation(Dt, Dt, ACT.Exp, scale=-1.0).then_inc(S("ml_exp"), 1)

            def ml_num(h):
                copy(f"num{h}", num[:, h], bank(f"num{h}")[:, :].rearrange("p (i e) -> p i e", i=2)[:, :, 0:129])

            was_read(act, "gT")
            nc.scalar.activation(st[:, 64:72], st[:, 56:64], ACT.Exp).then_inc(S("expm"), 1)
            ml_exp(0)
            gate("bgm", bg0, 0, 0)
            ml_exp(1)
            ml_num(0)
            gate("bgm", bg0, 0, 1)
            ml_exp(2)
            ml_num(1)
            gate("bgm", bg0, 1, 0)
            ml_exp(3)
            ml_num(2)
            gate("bgm", bg0, 1, 1)
            ml_num(3)
            act.wait_ge(S("h_div"), 1)
            nc.scalar.activation(sp_[:, 0:1024], hml.rearrange("p i h e -> p (i h e)"), ACT.Square).then_inc(S("h_sq"), 1)
            for i in range(NT):
                copy(f"nkv{i}", nkv[:, i, :], bank(f"nkv{i}")[:, :])
            act.wait_ge(S("hml_ready"), 1)
            arrived(act, "kcvc")
            for n in range(2):
                for g in range(2):
                    s = bank("kcvc")[DH * g:DH * g + DH, 256 * n:256 * n + 256]
                    nc.scalar.activation(k2[0:DH, n, g, :], s, ACT.Copy)
                    ins = nc.scalar.activation(k2[DH:P, n, g, 0:255], s[:, 1:256], ACT.Copy)
            read(ins, "kcvc")
            arrived(act, "mo1")
            for i in range(NT):
                copy(f"nqT{i}", qT[:, :, P * i:P * i + P], bank(f"nqT{i}")[:, :].rearrange("p (h t) -> p h t", h=4))
            for i in range(NT):
                copy(f"hmlT{i}", nqr[:, :].rearrange("p (h t) -> p h t", h=4)[:, :, P * i:P * i + P], bank(f"hmlT{i}")[:, :].rearrange("p (h t) -> p h t", h=4))
            for n, job in enumerate(("hk", "hv")):
                arrived(act, job)
                for f in range(2):
                    s = bank(job)[:, 30 * f:30 * f + 30]
                    col = vcol[:, 56 + 2 * n + f:57 + 2 * n + f]
                    nc.scalar.activation(hid[:, n, f, :], s, ACT.Identity, bias=col)
                    ins = nc.scalar.activation(hsg[:, n, f, :], s, ACT.Sigmoid, bias=col)
                read(ins, job)
            for i in range(NT):
                copy(f"nkT{i}", kT[:, :, P * i:P * i + P], bank(f"nkT{i}")[:, :].rearrange("p (h t) -> p h t", h=4))
            gate("bgl", bg1, 0, 0)
            gate("bgl", bg1, 0, 1)
            copy("vc", vc[0:NCMP, :], bank("vc")[0:NCMP, 0:128])
            gate("bgl", bg1, 1, 0)
            gate("bgl", bg1, 1, 1)
            copy("kcT", kcT, bank("kcT")[:, 0:30])

            def nsa_exp(h):
                act.wait_ge(S("nsa_nmax"), h + 1)
                s, o = Sn[h % 2], 80 + 16 * (h % 2)
                segs = [(768 + NCMP * i, NCMP, 3 * i) for i in range(2)]
                segs += [(512 + P * br, P, 1 + br) for br in range(2)] + [(256 * br, 256, 4 + br) for br in range(2)]
                for a, n, c in segs:
                    ins = nc.scalar.activation(s[:, a:a + n], s[:, a:a + n], ACT.Exp, bias=st[:, o + c:o + c + 1],
                                               accum_out=st[:, o + 8 + c:o + 9 + c])
                ins.then_inc(S("nsa_exp"), 1)

            def nsa_turned(h):
                if h >= 2:
                    arrived(act, f"nv{h // 2 - 1}")
                for br, job in enumerate((f"tA{h}", f"tB{h}")):
                    arrived(act, job)
                    nc.scalar.activation(PTn[h % 2][:, 384 * br:384 * br + 384], bank(job)[:, 0:384], ACT.Copy)
                    read(nc.scalar.activation(PTn[h % 2][0:NCMP, 768 + P * br:768 + P * br + P],
                                              bank(job)[0:NCMP, 384:512], ACT.Copy), job)

            nsa_exp(0)
            nsa_exp(1)
            for h in range(QH):
                nsa_turned(h)
                if h + 2 < QH:
                    nsa_exp(h + 2)
                if h in (1, 2):
                    was_read(act, "pm11")
                    gate("bgn", bg0, 0, h - 1)
                if h in (4, 5):
                    gate("bgn", bg0, 1, h - 4)
                if h % 2 == 1:
                    copy(f"nv{h // 2}", hT_nsa[h // 2], bank(f"nv{h // 2}")[:, 0:256])
            for i in range(NT):
                for h in range(2):
                    copy(f"mgT{i}{h}", qk[:, 4 * h:4 * h + 4, P * i:P * i + P],
                         bank(f"mgT{i}{h}")[:, :].rearrange("p (k t) -> p k t", k=4))
            for i in range(NT):
                was_read(act, f"wo1{i}")
                nc.scalar.activation(cp[:, 0:1024], x_sb[:, i, :], ACT.Square,
                                     accum_out=st[:, 4 + i:5 + i]).then_inc(S("sumsq"), 1)
                act.wait_ge(S("sumsq"), 5 + i)
            for i in range(NT):
                for h in range(2):
                    copy(f"xT{i}{h}", uT[:, 4 * h:4 * h + 4, P * i:P * i + P],
                         bank(f"xT{i}{h}")[:, :].rearrange("p (k t) -> p k t", k=4))
            act.wait_ge(S("lg_ready"), 1)
            for i in range(NT):
                ins = nc.scalar.activation(lg[:, i, :], lg[:, i, :], ACT.Exp, bias=st[:, 120 + i:121 + i])
            ins.then_inc(S("lg_exp"), 1)

            act.wait_ge(S("g_full"), 1)
            nc.scalar.activation(xgT.rearrange("p c n -> p (c n)"), BG[:, :], ACT.Copy).then_inc(S("g_evac"), 1)

            def item(i):
                for b in range(2):
                    act.wait_ge(S("g_clip"), i * 2 + (b + 1))
                    nc.scalar.activation(sg[b], gt[b], ACT.Sigmoid, scale=ALPHA).then_inc(S("g_sig"), 1)
                act.wait_ge(S("x_full"), i * 2 + 1)
                nc.scalar.activation(STs, BX[:, 0:256], ACT.Copy).then_inc(S("x_evac"), 1)
                act.wait_ge(S("g_full"), i + 2)
                nc.scalar.activation(xgT.rearrange("p c n -> p (c n)"), BG[:, :], ACT.Copy).then_inc(S("g_evac"), 1)
                act.wait_ge(S("x_full"), i * 2 + 2)
                nc.scalar.activation(actT, BX[:, :], ACT.Copy).then_inc(S("x_evac"), 1)
                act.wait_ge(S("down_done"), i * 2 + 2)
                nc.scalar.activation(y_sb, BG[:, :], ACT.Copy).then_inc(S("g_evac"), 1)

            with act.Fori(0, NE) as i:
                item(i)
            act.wait_ge(S("idx_ready"), 1)
            n_over = act.value_load(idx[0:1, 16:17], min_val=0, max_val=MAX_OVER)
            with act.If(n_over > 0):
                with act.Fori(0, n_over) as k:
                    item(k + NE)

        @block.vector
        def _(dve):
            V = nc.vector
            counts = {}

            def step(ins, name="dve"):
                counts[name] = counts.get(name, 0) + 1
                ins.then_inc(S(name), 1)
                dve.wait_ge(S(name), counts[name])

            def step_read(ins, job):
                read(ins, job)
                was_read(dve, job)

            def rstd(dst, src, n):
                step(V.tensor_scalar(dst, src, 1.0 / n, EPS, ALU.mult, ALU.add), "mean_ready")
                dve.wait_ge(S("rstd_done"), counts["mean_ready"])

            step(V.memset(rank_it[:, :, ITEMS:], UNSEL))
            step(V.memset(vaug[:, :, :, P:P + 1], 1.0), "ones_col")
            for i in range(NT):
                dve.wait_ge(S("sumsq"), i + 1)
                rstd(st[:, 8 + i:9 + i], st[:, i:i + 1], D)
                step(V.tensor_scalar(memn[:, i, :], memn[:, i, :], st[:, 8 + i:9 + i], None, ALU.mult), "mem_norm")
            for i in range(NT):
                dve.wait_ge(S("sumsq"), 3 + i)
                rstd(st[:, 10 + i:11 + i], st[:, 2 + i:3 + i], D)
                step(V.tensor_scalar(un[:, i, :], x_sb[:, i, :], st[:, 10 + i:11 + i], None, ALU.mult), "x_norm")
            arrived(dve, "vecT")
            step_read(V.tensor_copy(vcol[:, :], bank("vecT")[:, 0:VROWS]), "vecT")
            for name, dst, g0 in (("memT", memT, 8), ("uT", uT, 0)):
                for i in range(NT):
                    for h in range(2):
                        job = f"{name}{i}{h}"
                        arrived(dve, job)
                        read(V.tensor_tensor(dst[:, 4 * h:4 * h + 4, P * i:P * i + P],
                                             bank(job)[:, :].rearrange("p (k t) -> p k t", k=4),
                                             last(vcol[:, g0 + 4 * h:g0 + 4 * h + 4], P), ALU.mult), job)
            dve.wait_ge(S("cst_in"), 16)
            dve.wait_ge(S("bc_in"), 16 * 6)
            step(V.tensor_scalar(g_q, g_q, DH ** -0.5, None, ALU.mult))
            step(V.tensor_scalar(g_mq, g_mq, DH_MEM ** -0.5, None, ALU.mult))
            arrived(dve, "uT11")
            step(V.memset(pre[:, :, 0:3], 0.0), "pad_zero")

            def head_norm(x, ss, g, hd, sq, nh):
                step(V.tensor_reduce(ss, sq, AX.X, ALU.add))
                rstd(ss, ss, hd)
                step(V.tensor_tensor(x, x, last(ss, hd), ALU.mult))
                return V.tensor_tensor(x, x, mid(g, nh), ALU.mult)

            for name, x, sq, g, o in (("mk", mkv[:, :, 0:512], sqA, g_mk, 16), ("mq", mqn, sqB, g_mq, 24)):
                for i in range(NT):
                    was_read(dve, f"{name}{i}")
                for i in range(NT):
                    ins = head_norm(x[:, i, :].rearrange("p (h e) -> p h e", h=4), st[:, o + 4 * i:o + 4 * i + 4], g, DH_MEM,
                                    sq[:, i, :].rearrange("p (h e) -> p h e", h=4), 4)
                    step(ins, f"{name}_norm" if i == NT - 1 else "dve")
            for n in range(2):
                for j in range(4 * n, 4 * n + 4):
                    was_read(dve, f"qk{j // 2}")
                    step(V.tensor_scalar(qk[:, j, :], pre[:, j, 0:SEQ], vcol[:, 16 + j:17 + j], vcol[:, 48 + j:49 + j],
                                         ALU.mult, ALU.add))
                    for a in range(1, CONV):
                        col = vcol[:, 16 + 8 * a + j:17 + 8 * a + j]
                        ins = V.scalar_tensor_tensor(out=qk[:, j, :], in0=pre[:, j, a:a + SEQ], scalar=col, in1=qk[:, j, :],
                                                     op0=ALU.mult, op1=ALU.add)
                        step(ins, "conv_done" if (j, a) == (7, CONV - 1) else "dve")
            arrived(dve, "gif")
            step(V.tensor_scalar(r_f, bank("gif")[0:4, 256:512], bif[:, 1:2], None, ALU.add))
            step(V.scalar_tensor_tensor(out=r_B, in0=r_f, scalar=-1.0, in1=r_f, op0=ALU.mult, op1=ALU.max), "absf")
            for n in range(2):
                dve.wait_ge(S("conv_sig"), n + 1)
                q = qk[:, 4 * n:4 * n + 4, :].rearrange("p j t -> p (j t)")
                step(V.tensor_tensor(q, q, cp[:, 1024 * n:1024 * n + 1024], ALU.mult), "qk_ready")
            dve.wait_ge(S("act_rows"), 2)
            step(V.scalar_tensor_tensor(out=r_f, in0=r_f, scalar=0.0, in1=r_B, op0=ALU.min, op1=ALU.subtract))
            step(V.memset(r_M, 1.0))
            step(V.tensor_tensor_scan(r_B, r_M, r_f, 0.0, ALU.mult, ALU.add))
            step_read(V.scalar_tensor_tensor(out=r_g, in0=bank("gif")[0:4, 0:256], scalar=bif[:, 0:1], in1=r_B,
                                             op0=ALU.add, op1=ALU.subtract), "gif")
            step(V.memset(r_f, 0.0))
            step(V.tensor_tensor_scan(r_M, r_f, r_g, 0.0, ALU.add, ALU.max))
            step(V.scalar_tensor_tensor(out=r_nm, in0=r_B, scalar=-1.0, in1=r_M, op0=ALU.mult, op1=ALU.subtract), "rows_ready")

            def mem_max(h):
                arrived(dve, f"ms{h}")
                c = st[:, 32 + 2 * h:34 + 2 * h]
                step(V.tensor_reduce(c, bank(f"ms{h}")[:, :].rearrange("p (i m) -> p i m", i=2), AX.X, ALU.max))
                step(V.tensor_scalar(c, c, -1.0, None, ALU.mult), "mem_nmax")

            def mem_norm(h):
                was_read(dve, f"ms{h}")
                c = st[:, 40 + 2 * h:42 + 2 * h]
                step(V.reciprocal(c, c))
                step(V.tensor_tensor(Pm[h % 2], Pm[h % 2], last(c, 256), ALU.mult), "memP")

            mem_max(0)
            mem_max(1)
            mem_norm(0)
            arrived(dve, "gT")
            step(V.tensor_copy(st[:, 48:64], bank("gT")[:, 0:16]))
            step_read(V.tensor_copy(st[:, 72:80], bank("gT")[:, 0:8]), "gT")
            mem_max(2)
            mem_norm(1)
            mem_max(3)
            mem_norm(2)
            mem_norm(3)

            def rope(dst, src, cos, sin, nh):
                pr = src.shape[0]
                c, s = mid(cos[0:pr], nh), mid(sin[0:pr], nh)
                a = tmp[0:pr, 0:32 * nh].rearrange("p (h d) -> p h d", h=nh)
                b = tmp[0:pr, 256:256 + 32 * nh].rearrange("p (h d) -> p h d", h=nh)
                lo, hi = src[:, :, 0:32], src[:, :, 32:64]
                V.tensor_tensor(a, lo, c, ALU.mult)
                step(V.tensor_tensor(b, hi, s, ALU.mult))
                for d in dst:
                    ins = V.tensor_tensor(d[:, :, 0:32], a, b, ALU.subtract)
                step(ins)
                V.tensor_tensor(a, hi, c, ALU.mult)
                step(V.tensor_tensor(b, lo, s, ALU.mult))
                for d in dst:
                    ins = V.tensor_tensor(d[:, :, 32:64], a, b, ALU.add)
                return ins

            for i in range(NT):
                was_read(dve, f"nq{i}")
                q = nq_sb[:, i, :].rearrange("p (h e) -> p h e", h=QH)
                sq = qr[:, i, :].rearrange("p (h e) -> p h e", h=QH)
                step(V.tensor_tensor(sq, q, q, ALU.mult))
                step(head_norm(q, st[:, 128 + 8 * i:136 + 8 * i], g_q, DH, sq, QH))
                step(rope([sq], q, C(f"cos{i}"), C(f"sin{i}"), QH), "q_roped" if i == NT - 1 else "dve")

            arrived(dve, "mo1")
            was_read(dve, "mP3")
            for h in range(NH_ML):
                arrived(dve, f"MB{h}")
                V.tensor_scalar(Dt[:, 0:256], bank(f"MB{h}")[:, 0:256], st[:, 72 + h:73 + h], 0.0, ALU.subtract, ALU.max)
                step_read(V.tensor_scalar(Dt[:, 256:384], bank(f"MB{h}")[:, P:256], st[:, 76 + h:77 + h], 0.0,
                                          ALU.subtract, ALU.max), f"MB{h}")
                arrived(dve, f"ST{h}")
                dve.wait_ge(S("ml_exp"), h + 1)
                if h >= 2:
                    arrived(dve, f"num{h - 2}")
                w = wd[h % 2]
                step_read(V.scalar_tensor_tensor(out=w, in0=bank(f"ST{h}")[:, 0:384], scalar=DH_ML ** -0.5, in1=Dt,
                                                 op0=ALU.mult, op1=ALU.mult), f"ST{h}")
                V.tensor_tensor(w[:, 0:P], w[:, 0:P], C("upper"), ALU.mult)
                step(V.tensor_tensor(w[:, 256:384], w[:, 256:384], C("upper"), ALU.mult), "wd_ready")
            for h in range(NH_ML):
                was_read(dve, f"num{h}")
            dve.wait_ge(S("expm"), 1)
            den = st[:, 160:168].rearrange("p (i h) -> p i h", i=NT)
            nd = num[:, :, :, P].rearrange("p h i -> p i h")
            step(V.scalar_tensor_tensor(out=den, in0=nd, scalar=-1.0, in1=nd, op0=ALU.mult, op1=ALU.max))
            step(V.tensor_tensor(st[:, 160:168], st[:, 160:168], st[:, 64:72], ALU.max))
            step(V.reciprocal(st[:, 160:168], st[:, 160:168]))
            for i in range(NT):
                ins = V.tensor_tensor(hml[:, i], num[:, :, i, 0:P], last(st[:, 160 + 4 * i:164 + 4 * i], P), ALU.mult)
            step(ins, "h_div")
            dve.wait_ge(S("h_sq"), 1)
            hv = hml.rearrange("p i h e -> p (i h) e")
            step(V.tensor_reduce(st[:, 168:176], sp_[:, 0:1024].rearrange("p (a e) -> p a e", e=P), AX.X, ALU.add))
            rstd(st[:, 168:176], st[:, 168:176], DH_ML)
            step(V.tensor_tensor(hv, hv, last(st[:, 168:176], P), ALU.mult))
            h2 = hml.rearrange("p i h e -> p i (h e)")
            step(V.tensor_tensor(h2, h2, mid(g_ml, NT), ALU.mult))
            was_read(dve, "o1")
            step(V.tensor_tensor(h2, h2, osig, ALU.mult), "hml_ready")

            was_read(dve, "kcvc")
            for n in range(2):
                for g in range(2):
                    src = k2[:, n, g, :]
                    src = bass.AP(src.tensor, src.offset, [list(src.ap[0]), [2, 16], [16, NCMP]])
                    pos = last(vcol[:, 60 + 16 * n:76 + 16 * n], NCMP)
                    step(V.tensor_tensor(blk[:, n, :, g, :], src, pos, ALU.add), "blk_ready")

            for i in range(NT):
                was_read(dve, f"nkv{i}")
                for br in range(2):
                    k = nkv[:, i, 256 * br:256 * br + P].rearrange("p (g e) -> p g e", g=KVH)
                    sq = ksq[:, 0:P].rearrange("p (g e) -> p g e", g=KVH)
                    step(V.tensor_tensor(sq, k, k, ALU.mult))
                    o = 144 + 2 * (2 * i + br)
                    step(head_norm(k, st[:, o:o + 2], g_k[:, DH * (1 + br):DH * (2 + br)], DH, sq, KVH))
                    ins = rope([kr[:, i, br, :, u, :] for u in range(2)], k, C(f"cos{i}"), C(f"sin{i}"), KVH)
                    step(ins, "k_roped" if (i, br) == (1, 1) else "dve")
            for n, job in enumerate(("hk", "hv")):
                was_read(dve, job)
                step(V.tensor_tensor(hid[:, n], hid[:, n], hsg[:, n], ALU.mult), "hid_ready")
            arrived(dve, "kc")
            kn = ksq[0:30, 128:192].unsqueeze(1)
            step_read(V.tensor_copy(ksq[0:30, 128:192], bank("kc")[0:30, 0:DH]), "kc")
            ksq1 = ksq[0:30, 192:256].unsqueeze(1)
            step(V.tensor_tensor(ksq1, kn, kn, ALU.mult))
            step(head_norm(kn, st[0:30, 152:153], g_k[0:30, 0:DH], DH, ksq1, 1))
            step(rope([kcn[0:30, DH * u:DH * u + DH].unsqueeze(1) for u in range(2)], kn, C("cosc"), C("sinc"), 1), "kc_roped")

            def merge(name, gates, i, hh, first):
                job = f"{name}{i}{hh}"
                arrived(dve, job)
                m = merged[:, i, 512 * hh:512 * hh + 512]
                g = gates[:, D * i + 512 * hh:D * i + 512 * hh + 512]
                if first:
                    step_read(V.tensor_tensor(m, bank(job)[:, :], g, ALU.mult), job)
                else:
                    step_read(V.tensor_tensor(g, bank(job)[:, :], g, ALU.mult), job)
                    step(V.tensor_tensor(m, m, g, ALU.add), "merged")

            def nsa_mask(h):
                s, o = Sn[h % 2], 80 + 16 * (h % 2)
                if h >= 2:
                    arrived(dve, f"tB{h - 2}")
                arrived(dve, f"sA{h}")
                s1 = s[:, 0:512].rearrange("p (b m) -> p b m", b=2)
                s0 = s[:, 512:768].rearrange("p (b m) -> p b m", b=2)
                sc_ = s[:, 768:798]
                step_read(V.tensor_tensor(s1, bank(f"sA{h}")[:, :].rearrange("p (b m) -> p b m", b=2),
                                          mid(C("mask256"), 2), ALU.add), f"sA{h}")
                arrived(dve, f"sB{h}")
                V.tensor_tensor(s0, bank(f"sB{h}")[:, 0:256].rearrange("p (b m) -> p b m", b=2),
                                mid(C("mask256")[:, P:256], 2), ALU.add)
                step_read(V.tensor_tensor(sc_, bank(f"sB{h}")[:, 256:286], C("cmpadd"), ALU.add), f"sB{h}")
                V.tensor_reduce(st[:, o + 4:o + 6], s1, AX.X, ALU.max)
                V.tensor_reduce(st[:, o + 1:o + 3], s0, AX.X, ALU.max)
                step(V.tensor_reduce(st[:, o:o + 6].rearrange("p (i b) -> p i b", i=2)[:, :, 0],
                                     sc_.rearrange("p (i n) -> p i n", i=2), AX.X, ALU.max))
                step(V.tensor_scalar(st[:, o:o + 6], st[:, o:o + 6], -1.0, None, ALU.mult), "nsa_nmax")

            def nsa_weights(h):
                s, o = Sn[h % 2], 88 + 16 * (h % 2)
                dve.wait_ge(S("nsa_exp"), h + 1)
                sc_ = s[:, 768:798]
                step(V.tensor_tensor(sc_, sc_, C("cmp01"), ALU.mult))
                c3 = st[:, o:o + 6].rearrange("p (i b) -> p i b", i=2)
                step(V.tensor_reduce(c3[:, :, 0], sc_.rearrange("p (i n) -> p i n", i=2), AX.X, ALU.add))
                step(V.tensor_scalar(st[:, o:o + 6], st[:, o:o + 6], 1e-30, None, ALU.max))
                step(V.reciprocal(st[:, o:o + 6], st[:, o:o + 6]))
                step(V.tensor_tensor(c3, c3, gsb[:, :, 3 * h:3 * h + 3], ALU.mult))
                s1 = s[:, 0:512].rearrange("p (b m) -> p b m", b=2)
                s0 = s[:, 512:768].rearrange("p (b m) -> p b m", b=2)
                sc2 = sc_.rearrange("p (i n) -> p i n", i=2)
                V.tensor_tensor(s1, s1, last(st[:, o + 4:o + 6], 256), ALU.mult)
                V.tensor_tensor(s0, s0, last(st[:, o + 1:o + 3], P), ALU.mult)
                step(V.tensor_tensor(sc2, sc2, c3[:, :, 0].unsqueeze(2).to_broadcast([P, 2, NCMP]), ALU.mult), "nsaP")

            arrived(dve, "hmlT1")
            was_read(dve, "ngate")
            nsa_mask(0)
            nsa_mask(1)
            nsa_weights(0)
            was_read(dve, "bgm11")
            for i in range(NT):
                for hh in range(2):
                    merge("pm", bg0, i, hh, True)
            for h in range(QH):
                if h + 2 < QH:
                    nsa_mask(h + 2)
                if h == 0:
                    was_read(dve, "bgl11")
                    nsa_weights(1)
                    for i in range(NT):
                        for hh in range(2):
                            merge("pl", bg1, i, hh, False)
                elif h + 1 < QH:
                    nsa_weights(h + 1)
            was_read(dve, "bgn11")
            for i in range(NT):
                for hh in range(2):
                    merge("pn", bg0, i, hh, False)
            for hh in range(2):
                for i in range(NT):
                    job = f"wo{hh}{i}"
                    arrived(dve, job)
                    xs = x_sb[:, i, 512 * hh:512 * hh + 512]
                    step_read(V.tensor_tensor(xs, xs, bank(job)[:, :], ALU.add), job)
            dve.wait_ge(S("gffn_in"), 16)
            for i in range(NT):
                dve.wait_ge(S("sumsq"), 5 + i)
                rstd(st[:, 12 + i:13 + i], st[:, 4 + i:5 + i], D)
                step(V.scalar_tensor_tensor(out=x2[:, i, :], in0=x_sb[:, i, :], scalar=st[:, 12 + i:13 + i], in1=g_ffn,
                                            op0=ALU.mult, op1=ALU.mult), "x2_ready")

            arrived(dve, "rt")
            step_read(V.tensor_tensor(lg, bank("rt")[:, 0:64].rearrange("p (i e) -> p i e", i=2), mid(b_r, 2), ALU.add), "rt")
            for i in range(NT):
                ins = V.max(top[:, i, :], lg[:, i, :])
            step(ins)
            for i in range(NT):
                V.tensor_scalar(sel[:, i, :], lg[:, i, :], top[:, i, TOPK - 1:TOPK], None, ALU.is_gt)
                ins = V.tensor_scalar(eqv[:, i, :], lg[:, i, :], top[:, i, TOPK - 1:TOPK], None, ALU.is_equal)
            step(ins)
            step(V.tensor_scalar(st[:, 120:122], top[:, :, 0], -1.0, None, ALU.mult), "lg_ready")
            step(V.tensor_reduce(ngt, sel, AX.X, ALU.add))
            step(V.tensor_scalar(ngt, ngt, -1.0, float(TOPK), ALU.mult, ALU.add))
            for i in range(NT):
                ins = V.tensor_tensor_scan(cum[:, i, :], ones[:, 0:NE], eqv[:, i, :], 0.0, ALU.mult, ALU.add)
            step(ins)
            for i in range(NT):
                ins = V.scalar_tensor_tensor(out=cum[:, i, :], in0=cum[:, i, :], scalar=ngt[:, i:i + 1], in1=eqv[:, i, :],
                                             op0=ALU.is_le, op1=ALU.mult)
            step(ins)
            step(V.tensor_tensor(sel, sel, cum, ALU.add), "sel_ready")
            dve.wait_ge(S("lg_exp"), 1)
            wts = w_it[:, :, 0:NE]
            step(V.tensor_tensor(wts, lg, sel, ALU.mult))
            step(V.tensor_reduce(st[:, 122:124], wts, AX.X, ALU.add))
            step(V.reciprocal(st[:, 122:124], st[:, 122:124]))
            step(V.tensor_tensor(wts, wts, last(st[:, 122:124], NE), ALU.mult))
            arrived(dve, "rank")
            rk = rank_it[:, :, 0:NE]
            step(V.scalar_tensor_tensor(out=rk, in0=bank("rank")[:, 0:64].rearrange("p (i e) -> p i e", i=2), scalar=-UNSEL,
                                        in1=sel, op0=ALU.add, op1=ALU.mult))
            step(V.tensor_scalar(rk, rk, UNSEL, None, ALU.add))
            for n in range(3):
                ins = V.tensor_scalar(cntc[:, n:n + 1], bank("rank")[0:NE, 64:65], float(SLOT_TOK * (n + 1)), None, ALU.is_gt)
            step_read(ins, "rank")
            step(V.tensor_reduce(nov, cntc, AX.X, ALU.add), "rank_ready")
            arrived(dve, "rT")
            step_read(V.tensor_copy(rTs, bank("rT")[0:NE, :]), "rT")
            arrived(dve, "ov")
            step(V.tensor_copy(ost, bank("ov")[0:NE, 0:1]))
            step_read(V.tensor_copy(idx[0:1, 16:17], bank("ov")[0:1, 1:2]), "ov")
            step(V.tensor_tensor(oen, ost, nov, ALU.add))
            ov = C("over")[0:NE, :]
            step(V.tensor_scalar(Eov, ov, ost, None, ALU.is_ge))
            step(V.scalar_tensor_tensor(out=Eov, in0=ov, scalar=oen, in1=Eov, op0=ALU.is_lt, op1=ALU.mult))
            step(V.tensor_scalar(Aov, ov, ost, 1.0, ALU.subtract, ALU.add))
            step(V.scalar_tensor_tensor(out=Aov, in0=Aov, scalar=-float(SLOT_TOK), in1=Eov, op0=ALU.mult, op1=ALU.mult), "over_ready")
            arrived(dve, "it")
            step(V.tensor_copy(idx[0:1, 0:MAX_OVER], bank("it")[0:1, 64:64 + MAX_OVER]), "idx_ready")
            V.tensor_copy(w_it[:, :, NE:ITEMS], bank("it")[:, 2 * MAX_OVER:4 * MAX_OVER].rearrange("p (i k) -> p i k", i=2))
            step_read(V.tensor_copy(rank_it[:, :, NE:ITEMS], bank("it")[:, 0:2 * MAX_OVER].rearrange("p (i k) -> p i k", i=2)), "it")

            def onehot(i):
                for t in range(NT):
                    ins = V.tensor_scalar(Gm[:, t, :], C("iota")[:, 0:64], rank_it[:, t, bass.ds(i, 1)], None, ALU.is_equal)
                ins.then_inc(S("G_ready"), 1)

            onehot(0)

            def item(i):
                dve.wait_ge(S("gu_done"), i * 4 + 1)
                for t in range(NT):
                    ins = V.tensor_scalar(Gw[:, t, :], C("iota"), rank_it[:, t, bass.ds(i, 1)], w_it[:, t, bass.ds(i, 1)],
                                          ALU.is_equal, ALU.mult)
                ins.then_inc(S("Gw_ready"), 1)
                onehot(i + 1)
                dve.wait_ge(S("gu_done"), i * 4 + 4)
                for b in range(2):
                    h = BH[b][:, :].rearrange("p (f two) -> p f two", two=2)
                    V.tensor_scalar(gt[b], h[:, :, 0], LIMIT, None, ALU.min).then_inc(S("g_clip"), 1)
                    V.tensor_scalar(ut[b], h[:, :, 1], -LIMIT, LIMIT, ALU.max, ALU.min).then_inc(S("h_free"), 1)
                for b in range(2):
                    dve.wait_ge(S("g_sig"), i * 2 + (b + 1))
                    V.tensor_tensor(gt[b], gt[b], sg[b], ALU.mult).then_inc(S("gs_done"), 1)
                dve.wait_ge(S("h_free"), i * 2 + 2)
                dve.wait_ge(S("gs_done"), i * 2 + 2)
                for b in range(2):
                    V.scalar_tensor_tensor(out=act_sb[:, 256 * b:256 * b + 256], in0=ut[b], scalar=1.0, in1=gt[b],
                                           op0=ALU.add, op1=ALU.mult).then_inc(S("act_ready"), 1)

            with dve.Fori(0, NE) as i:
                item(i)
            dve.wait_ge(S("idx_ready"), 1)
            n_over = dve.value_load(idx[0:1, 16:17], min_val=0, max_val=MAX_OVER)
            with dve.If(n_over > 0):
                with dve.Fori(0, n_over) as k:
                    item(k + NE)
            for t in range(NT):
                dve.wait_ge(S("sum_ready"), t + 1)
                for hh in range(2):
                    ins = V.tensor_copy(x_sb[:, t, 512 * hh:512 * hh + 512], ACC[t][hh][:, :])
                ins.then_inc(S("out_ready"), 1)


_INS = ["x", "mem", "g_mix", "w_in", "ml_conv_w", "ml_conv_b", "ml_b_i", "ml_b_f", "ml_g_out", "nsa_g_q", "nsa_g_k",
        "cmp_pos_k", "cmp_w1_k", "cmp_b1_k", "cmp_w2_k", "cmp_pos_v", "cmp_w1_v", "cmp_b1_v", "cmp_w2_v", "g_mem",
        "w_mem_kv", "mem_g_q", "mem_g_k", "w_br_ml", "w_br_nsa", "w_br_mem", "w_out", "g_ffn", "w_router", "b_router",
        "w_gu", "b_gu", "w_down", "b_down"]


def kernel(**inputs):
    import concourse.bacc as bacc
    from concourse.bass_utils import run_bass_kernel_spmd as run

    nc = bacc.Bacc("TRN2", target_bir_lowering=False, num_devices=1)
    arrays, A = {}, {}
    for name in _INS:
        a = np.ascontiguousarray(inputs[name])
        arrays[f"in_{name}"] = a
        A[name] = nc.dram_tensor(f"in_{name}", a.shape, mybir.dt.from_np(a.dtype), kind="ExternalInput").ap()
    arrays["shape_consts"] = CONST
    const = nc.dram_tensor("shape_consts", CONST.shape, F32, kind="ExternalInput").ap()
    out = nc.dram_tensor("out", (1, SEQ, D), F32, kind="ExternalOutput").ap()
    hybrid_layer(nc, A, const, out)
    r = run(nc, [arrays], core_ids=[0])
    return r.results[0]["out"]
```

```python
from contextlib import ExitStack

import numpy as np

import concourse.bass as bass
from concourse import mybir

F32 = mybir.dt.float32
I32 = mybir.dt.int32
ALU = mybir.AluOpType
ACT = mybir.ActivationFunctionType
AX = mybir.AxisListType

P = 128
D = 1024
SEQ = 256
NT = SEQ // P
KT = D // P
NH_ML, DH_ML = 4, 128
QH, KVH, DH = 8, 2, 64
GROUP = QH // KVH
NH_MEM, DH_MEM = 4, 128
CMP_BLOCK, CMP_STRIDE, CMP_HID = 32, 16, 256
NCMP = (SEQ - CMP_BLOCK) // CMP_STRIDE + 1
CONV = 4
NE, TOPK = 32, 4
SLOT_TOK = 64
MAX_OVER = SEQ * TOPK // SLOT_TOK
ITEMS = NE + MAX_OVER
EPS = 1e-6
NEG = -1e30
LIMIT, ALPHA = 7.0, 1.702
UNSEL = -4096.0

C_MLQ, C_V, C_O, C_IF = 0, 1024, 1536, 2048
C_NQ, C_KCVC, C_NKV, C_NG, C_MQ, C_BR = 2056, 2568, 2824, 3336, 3360, 3872

NSLOT = 6
SLOT = 4096


CHUNKS = [("mk", "mk1"), ("mv", "mv1"), ("mq", "mq1"), ("qk0", "qk1"), ("qk1", "qk3"), ("v", "v1"),
          ("o", "o1"), ("nq", "nq1"), ("bgm0", "bgm01"), ("bgm1", "bgm11"), ("nkv", "nkv1"),
          ("kcvc", "kcvc"), ("w1k", "hk"), ("w1v", "hv"), ("bgl0", "bgl01"), ("bgl1", "bgl11"),
          ("wbm", "pm11"), ("wbl", "pl11"), ("bgn0", "bgn01"), ("bgn1", "bgn11"), ("wbn", "pn11"),
          ("wo0", "wo01"), ("wo1", "wo11"), ("wr", "lT")]
SLOT_OF = {name: n % NSLOT for n, (name, _) in enumerate(CHUNKS)}
CHUNK_NO = {name: n for n, (name, _) in enumerate(CHUNKS)}
TRUNK_TURNS = len(CHUNKS) // NSLOT
assert TRUNK_TURNS * NSLOT == len(CHUNKS)


def job_order():
    four = [f"{a}{b}" for a in range(2) for b in range(2)]
    jobs = ["vecT"] + [f"memT{x}" for x in four] + [f"uT{x}" for x in four]
    jobs += ["mk0", "mk1", "mv0", "mv1", "mq0", "mq1", "qk0", "qk1", "qk2", "qk3"]
    jobs += ["mkT0", "mkT1", "v0", "v1", "mqT0", "mqT1", "gif", "ms0", "ms1", "o0", "o1", "gT"]
    jobs += ["mP0", "ms2", "mP1", "ms3", "mo0", "nq0", "nq1", "ngate", "mP2", "mP3", "mo1"]
    jobs += ["ST0", "MB0", "bgm00", "ST1", "MB1", "num0", "bgm01", "ST2", "MB2", "num1",
             "bgm10", "ST3", "MB3", "num2", "bgm11", "num3"]
    jobs += ["nkv0", "nkv1", "kcvc", "nqT0", "nqT1", "hmlT0", "hmlT1", "hk", "hv", "nkT0", "nkT1", "hkT", "hvT"]
    jobs += ["bgl00", "bgl01", "kc", "vc", "bgl10", "bgl11", "kcT"]
    jobs += ["sA0", "sB0", "sA1", "sB1"]
    jobs += [f"pm{x}" for x in four]
    filler = {0: [f"pl{x}" for x in four], 1: ["bgn00"], 2: ["bgn01"], 4: ["bgn10"], 5: ["bgn11"]}
    for h in range(QH):
        jobs += [f"tA{h}", f"tB{h}"]
        if h + 2 < QH:
            jobs += [f"sA{h + 2}", f"sB{h + 2}"]
        jobs += filler.get(h, [])
        if h % 2 == 1:
            jobs += [f"nv{h // 2}"]
    jobs += [f"pn{x}" for x in four]
    jobs += ["wo00", "wo01", "wo10", "wo11"]
    return jobs


JOBS = job_order()
NB = 8
TAIL = ["xT00", "xT10", "xT01", "xT11", "lT", "lg", "rank", "rT", "ov", "it"]
BANK, TURN = {}, {}
for n, name in enumerate(JOBS + TAIL):
    BANK[name] = n % NB if n < len(JOBS) else 4 + (n - len(JOBS)) % 4
    TURN[name] = sum(BANK[other] == BANK[name] for other in list(BANK)[:-1])
JOBS += TAIL
assert len(BANK) == len(JOBS)


def const_table():
    parts, at = {}, 0
    cols = []

    def add(name, a):
        nonlocal at
        full = np.zeros((P, a.shape[1]), np.float32)
        full[:a.shape[0]] = a
        parts[name] = (at, a.shape[1])
        at += a.shape[1]
        cols.append(full)

    p = np.arange(P)
    add("ident", np.eye(P, dtype=np.float32))
    causal = np.where(p[None, :] > p[:, None], np.float32(NEG), np.float32(0)).astype(np.float32)
    add("mask256", np.concatenate([np.zeros((P, P), np.float32), causal], 1))
    add("upper", (p[:, None] <= p[None, :]).astype(np.float32))
    add("strict", (p[:, None] < p[None, :]).astype(np.float32))
    add("ones", np.ones((P, P), np.float32))
    ends = np.arange(NCMP) * CMP_STRIDE + CMP_BLOCK - 1
    ok = np.stack([ends[None, :] <= (p + P * i)[:, None] for i in range(NT)], 1)
    add("cmp01", ok.astype(np.float32).reshape(P, -1))
    add("cmpadd", np.where(ok, np.float32(0), np.float32(NEG)).astype(np.float32).reshape(P, -1))
    half = DH // 2
    inv = np.power(10000.0, (-np.arange(half, dtype=np.float32) / np.float32(half)).astype(np.float64))
    inv = inv.astype(np.float32)

    def rope(pos):
        ang = (pos.astype(np.float32)[:, None] * inv[None, :]).astype(np.float64)
        return np.cos(ang).astype(np.float32), np.sin(ang).astype(np.float32)

    for i in range(NT):
        c, s = rope(p + P * i)
        add(f"cos{i}", c)
        add(f"sin{i}", s)
    c, s = rope(np.tile(ends, KVH))
    add("cosc", c)
    add("sinc", s)
    add("iota", np.tile(np.arange(SLOT_TOK, dtype=np.float32), (P, 2)))
    add("over", np.tile(np.arange(MAX_OVER, dtype=np.float32), (P, 1)))
    add("sum4", np.tile(np.eye(32, dtype=np.float32), (4, 1)))
    add("mhalf", np.full((P, 8), -0.5, np.float32))
    add("pcol", p[:, None].astype(np.float32))
    return np.concatenate(cols, 1), parts


CONST, CPART = const_table()
VROWS = 100


def hybrid_layer(nc, A, const, out):
    with ExitStack() as ctx:
        def sb(name, *shape, dt=F32):
            return ctx.enter_context(nc.sbuf_tensor(name, list(shape), dt))

        sems = {}

        def S(name):
            if name not in sems:
                sems[name] = ctx.enter_context(nc.semaphore(name))
            return sems[name]

        ring = sb("ring", P, NSLOT, SLOT)
        cst = sb("cst", P, CONST.shape[1])
        x_sb = sb("x_sb", P, NT, D)
        uT = sb("uT", P, KT, SEQ)
        mT = sb("mT", P, 2048)
        sc = sb("sc", P, 2048)
        cp = sb("cp", P, 8 * (SEQ + 3))
        qk = sb("qk", P, 8, SEQ)
        vo = sb("vo", P, 2056)
        nkv = sb("nkv", P, NT, 512)
        nqr = sb("nqr", P, 1024)
        mq = sb("mq", P, 2048)
        bg0 = sb("bg0", P, 2048)
        bg1 = sb("bg1", P, 2048)
        sp_ = sb("sp_", P, 3712)
        kcv = sb("kcv", P, 158)
        vcol = sb("vcol", P, VROWS)
        bcg = sb("bcg", P, 288)
        st = sb("st", P, 256)
        bif = sb("bif", 4, 2)
        gsb = sb("gsb", P, NT, 24)
        rank_it = sb("rank_it", P, NT, ITEMS + 2)
        w_it = sb("w_it", P, NT, ITEMS)
        idx = sb("idx", 1, 32, dt=I32)

        banks = [ctx.enter_context(nc.psum_tensor(f"bank{i}", [P, 512], F32)) for i in range(NB)]
        bank_full = [S(f"bank_full{i}") for i in range(NB)]
        bank_free = [S(f"bank_free{i}") for i in range(NB)]
        w_full = [S(f"w_full{i}") for i in range(NSLOT)]

        def C(name):
            a, n = CPART[name]
            return cst[:, a:a + n]

        def bank(job):
            return banks[BANK[job]]

        def arrived(eng, job):
            eng.wait_ge(bank_full[BANK[job]], TURN[job] + 1)

        def read(ins, job):
            return ins.then_inc(bank_free[BANK[job]], 1)

        def was_read(eng, job):
            eng.wait_ge(bank_free[BANK[job]], TURN[job] + 1)

        def mid(ap, n):
            return ap.unsqueeze(1).to_broadcast([ap.shape[0], n, ap.shape[1]])

        def last(ap, n):
            return ap.unsqueeze(2).to_broadcast([ap.shape[0], ap.shape[1], n])

        ident = C("ident")
        ones = C("ones")
        memn = sc[:, :].rearrange("p (i d) -> p i d", i=NT)
        un = cp[:, 0:2048].rearrange("p (i d) -> p i d", i=NT)
        memT = mT[:, :].rearrange("p (k t) -> p k t", k=KT)
        mergedT = mT[:, :].rearrange("p (k t) -> p k t", k=KT)
        mkv = sc[:, :].rearrange("p (i d) -> p i d", i=NT)
        pre = cp[:, :].rearrange("p (j t) -> p j t", j=8)
        x2 = sc[:, :].rearrange("p (i d) -> p i d", i=NT)
        vaug = vo[:, 0:NT * 4 * 129].rearrange("p (i h e) -> p i h e", i=NT, h=4)
        osig = vo[:, 1032:2056].rearrange("p (i n) -> p i n", i=NT)
        k2 = vo[:, 0:1024].rearrange("p (b h t) -> p b h t", b=2, h=2)
        blk = vo[:, 1024:2048].rearrange("p (b m n) -> p b m n", b=2, m=16)
        vec = bg0[0:VROWS, 0:P]
        wif = bg0[:, 128:192].rearrange("p (k n) -> p k n", k=KT)
        wng = bg0[:, 192:384].rearrange("p (k n) -> p k n", k=KT)
        rows = bg1[0:4, 0:1280]
        nq_sb = nqr[:, :].rearrange("p (i n) -> p i n", i=NT)
        heads = sc[:, :].rearrange("p (i k t) -> p i k t", i=2, k=4)
        hT_mem = [heads[:, k // 2, k % 2, :] for k in range(4)]
        hT_nsa = [heads[:, k // 2, 2 + k % 2, :] for k in range(4)]
        hT_ml = [nqr[:, 256 * k:256 * k + 256] for k in range(4)]
        mqn = nq_sb
        mqT = mq[:, 0:1024].rearrange("p (h t) -> p h t", h=4)
        mkT = mq[:, 1024:2048].rearrange("p (h t) -> p h t", h=4)
        qT = mq[:, 0:1024].rearrange("p (h t) -> p h t", h=4)
        kT = mq[:, 1024:2048].rearrange("p (b t) -> p b t", b=4)
        kcT, vc = kcv[:, 0:30], kcv[:, 30:158]
        tmp = mT[:, 0:512]
        w2 = mT[:, 512:768].rearrange("p (b f d) -> p b f d", b=2, f=2)
        kcn = mT[:, 768:896]
        hid = mT[:, 896:1016].rearrange("p (b f n) -> p b f n", b=2, f=2)
        hsg = mT[:, 1016:1136].rearrange("p (b f n) -> p b f n", b=2, f=2)
        ksq = mT[:, 1136:1536]
        hidp = mT[:, 1536:2048].rearrange("p (b f) -> p b f", b=2)
        qr = cp[:, 0:1024].rearrange("p (i n) -> p i n", i=NT)
        kr = cp[:, 1024:2048].rearrange("p (i b g u d) -> p i b g u d", i=NT, b=2, g=2, u=2)
        Pm = [sp_[:, 800 * b:800 * b + 512].rearrange("p (i m) -> p i m", i=NT) for b in range(2)]
        PTm = [sp_[:, 1600 + 1024 * b:1600 + 1024 * b + 512].rearrange("p (m t) -> p m t", m=2) for b in range(2)]
        sqA = sp_[:, 1600:2624].rearrange("p (i n) -> p i n", i=NT)
        sqB = sp_[:, 2624:3648].rearrange("p (i n) -> p i n", i=NT)
        Dt = sp_[:, 0:384]
        wd = [sp_[:, 384:768], sp_[:, 768:1152]]
        num = sp_[:, 1152:2184].rearrange("p (h i e) -> p h i e", h=4, i=NT)
        hml = sp_[:, 2184:3208].rearrange("p (i h e) -> p i h e", i=NT, h=4)
        Sn = [sp_[:, 800 * b:800 * b + 798] for b in range(2)]
        PTn = [sp_[:, 1600 + 1024 * b:2624 + 1024 * b] for b in range(2)]

        g_q, g_k = bcg[:, 0:64], bcg[:, 64:256]
        g_ml, g_mq, g_mk = bg1[:, 1280:1792], bg1[:, 1792:1920], bg1[:, 1920:2048]
        b_r = bcg[:, 256:288]
        g_ffn = bg1[:, 0:1024]
        b_dn = nqr[0:32, :]

        r_f, r_B, r_g, r_M, r_nm = (rows[:, 256 * n:256 * n + 256] for n in range(5))

        Gm = sp_[:, 0:256].rearrange("p (i n) -> p i n", i=NT)
        Gw = sp_[:, 256:512].rearrange("p (i n) -> p i n", i=NT)
        STs = sp_[:, 512:768]
        xgT = sp_[:, 768:1792].rearrange("p (c n) -> p c n", c=KT)
        gt = [sp_[:, 1792 + 256 * b:2048 + 256 * b] for b in range(2)]
        ut = [sp_[:, 2304 + 256 * b:2560 + 256 * b] for b in range(2)]
        act_sb = sp_[:, 2304:2816]
        sg = [sp_[:, 2816 + 256 * b:3072 + 256 * b] for b in range(2)]
        y_sb = mq[:, 0:1024]
        actT = mq[:, 1024:1536]
        brow = bg0[0:1, :]
        lg = bg1[:, 1024:1088].rearrange("p (i e) -> p i e", i=NT)
        top = bg1[:, 1088:1104].rearrange("p (i e) -> p i e", i=NT)
        sel = bg1[:, 1104:1168].rearrange("p (i e) -> p i e", i=NT)
        eqv = bg1[:, 1168:1232].rearrange("p (i e) -> p i e", i=NT)
        cum = bg1[:, 1232:1296].rearrange("p (i e) -> p i e", i=NT)
        ngt = bg1[:, 1296:1298]
        rTs = mq[0:32, 1536:2048]
        nov = bg1[0:32, 1300:1301]
        ost = bg1[0:32, 1302:1303]
        oen = bg1[0:32, 1304:1305]
        ovs = bg1[0:32, 1306:1307]
        Eov = bg1[0:32, 1312:1312 + MAX_OVER]
        Aov = bg1[0:32, 1328:1328 + MAX_OVER]
        cntc = bg1[0:32, 1344:1347]
        few = bg1[0:1, 1352:1352 + MAX_OVER // 2]
        npair = bg1[0:1, 1364:1365]

        ACC = [[banks[2 * i + h] for h in range(2)] for i in range(NT)]
        BG, BX, BH = banks[4], banks[5], [banks[6], banks[7]]

        out_t = out[0].rearrange("(i p) d -> p i d", p=P)
        w_in = A["w_in"][0]
        w_mkv = A["w_mem_kv"][0]
        w_gu, b_gu, w_dn = A["w_gu"][0], A["b_gu"][0], A["w_down"][0]

        block = ctx.enter_context(nc.Block())

        def item_chunks(eng, e):
            for q in range(4):
                yield (ring[:, q, :].rearrange("p (c n) -> p c n", c=2),
                       w_gu[e].rearrange("(c p) n -> p c n", p=P)[:, 2 * q:2 * q + 2, :])
            for d in range(2):
                yield (ring[:, 4 + d, :].rearrange("p (c n) -> p c n", c=4),
                       w_dn[e].rearrange("(c p) n -> p c n", p=P)[:, 4 * d:4 * d + 4, :])

        @block.sync
        def _(sp):
            sp.dma_start(memn, A["mem"][0].rearrange("(i p) d -> p i d", p=P)).then_inc(S("mem_in"), 16)
            sp.dma_start(cst[:, :], const).then_inc(S("cst_in"), 16)
            sp.dma_start(x_sb[:, :, :], A["x"][0].rearrange("(i p) d -> p i d", p=P)).then_inc(S("x_in"), 16)

            def cols(a, c0, n=512):
                return a[:, c0:c0 + n].rearrange("(c p) n -> p c n", p=P)

            src = {
                "mk": cols(w_mkv, 0), "mv": cols(w_mkv, 512), "mq": cols(w_in, C_MQ),
                "qk0": cols(w_in, 0), "qk1": cols(w_in, 512), "v": cols(w_in, C_V), "o": cols(w_in, C_O),
                "nq": cols(w_in, C_NQ), "nkv": cols(w_in, C_NKV), "kcvc": cols(w_in, C_KCVC, 256),
                "w1k": A["cmp_w1_k"][0].rearrange("(m l) d f -> (l d) m f", l=2),
                "w1v": A["cmp_w1_v"][0].rearrange("(m l) d f -> (l d) m f", l=2),
                "wbm": cols(A["w_br_mem"][0], 0, D), "wbl": cols(A["w_br_ml"][0], 0, D),
                "wbn": cols(A["w_br_nsa"][0], 0, D),
                "wo0": cols(A["w_out"][0], 0), "wo1": cols(A["w_out"][0], 512),
                "wr": A["w_router"][0].rearrange("(c p) n -> p c n", p=P),
            }
            for b, name in enumerate(("bgl", "bgn", "bgm")):
                for h in range(2):
                    src[f"{name}{h}"] = cols(w_in, C_BR + D * b + 512 * h)
            sp.wait_ge(S("vec_in"), 16 * 9)
            for n, (name, _) in enumerate(CHUNKS):
                s = src[name]
                if n >= NSLOT:
                    arrived(sp, CHUNKS[n - NSLOT][1])
                dst = ring[:, n % NSLOT, 0:s.shape[1] * s.shape[2]].rearrange("p (c n) -> p c n", c=s.shape[1])
                sp.dma_start(dst, s).then_inc(w_full[n % NSLOT], 16)
            for q, (dst, s) in enumerate(item_chunks(sp, 0)):
                arrived(sp, CHUNKS[len(CHUNKS) - NSLOT + q][1])
                sp.dma_start(dst, s).then_inc(w_full[q], 16)

            arrived(sp, "pn11")
            sp.wait_ge(S("merged"), 8)
            sp.dma_start(brow, b_gu[0:1, :]).then_inc(S("brow_in"), 16)

            def load_item(i, e):
                sp.wait_ge(S("brow_used"), i)
                sp.dma_start(brow, b_gu[bass.ds(e, 1), :]).then_inc(S("brow_in"), 16)
                for q, (dst, s) in enumerate(item_chunks(sp, e)):
                    if q < 4:
                        sp.wait_ge(S("gu_done"), i * 4 + (q - 3))
                    else:
                        sp.wait_ge(S("down_done"), i * 2 + (q - 5))
                    sp.dma_start(dst, s).then_inc(w_full[q], 16)

            with sp.Fori(1, NE) as e:
                load_item(e, e)
            sp.wait_ge(S("idx_ready"), 1)
            n_pairs = sp.value_load(idx[0:1, MAX_OVER:MAX_OVER + 1], min_val=0, max_val=MAX_OVER // 2)
            with sp.If(n_pairs > 0):
                with sp.Fori(0, n_pairs * 2) as k:
                    e = sp.value_load(idx[0:1, bass.ds(k, 1)], min_val=0, max_val=NE - 1)
                    load_item(k + NE, e)
            for t in range(NT):
                sp.wait_ge(S("out_left"), t + 1)
                sp.dma_start(out_t[:, t, 0:512], x_sb[:, t, 0:512]).then_inc(S("out_done"), 16)
            sp.wait_ge(S("out_done"), 16 * 2 * NT)

        @block.gpsimd
        def _(pool):
            pool.dma_start(wif, w_in[:, C_IF:C_IF + 8].rearrange("(c p) n -> p c n", p=P)).then_inc(S("small_in"), 16)
            pool.dma_start(wng, w_in[:, C_NG:C_NG + 24].rearrange("(c p) n -> p c n", p=P)).then_inc(S("small_in"), 16)
            pool.dma_start(bif[:, 0:1], A["ml_b_i"].rearrange("a h -> h a")).then_inc(S("small_in"), 16)
            pool.dma_start(bif[:, 1:2], A["ml_b_f"].rearrange("a h -> h a")).then_inc(S("small_in"), 16)

            def everywhere(dst, a):
                pool.dma_start(dst, a.partition_broadcast(P)).then_inc(S("bc_in"), 16)

            everywhere(g_q, A["nsa_g_q"][0])
            everywhere(g_k, A["nsa_g_k"][0].rearrange("b d -> (b d)"))
            everywhere(g_ml, A["ml_g_out"][0].rearrange("b d -> (b d)"))
            everywhere(g_mq, A["mem_g_q"][0])
            everywhere(g_mk, A["mem_g_k"][0])
            everywhere(b_r, A["b_router"][0])
            powers = [0]

            def power(ap):
                powers[0] += 1
                pool.wait_ge(S("mean_ready"), powers[0])
                nc.gpsimd.tensor_tensor(ap, ap, C("mhalf")[0:ap.shape[0], 0:ap.shape[1]], ALU.pow).then_inc(S("rstd_done"), 1)

            pool.wait_ge(S("cst_in"), 16)
            for c in range(8, 12):
                power(st[:, c:c + 1])
            for c in range(16, 32, 4):
                power(st[:, c:c + 4])
            arrived(pool, "mv1")
            pool.dma_start(w2[:, 0], A["cmp_w2_k"][0].rearrange("(f p) d -> p f d", p=P)).then_inc(S("w2_in"), 16)
            pool.dma_start(w2[:, 1], A["cmp_w2_v"][0].rearrange("(f p) d -> p f d", p=P)).then_inc(S("w2_in"), 16)
            for c in (128, 136):
                power(st[:, c:c + 8])
            power(st[:, 168:176])
            for c in range(144, 152, 2):
                power(st[:, c:c + 2])
            power(st[0:30, 152:153])
            pool.wait_ge(S("merged"), 4)
            pool.dma_start(b_dn, A["b_down"][0]).then_inc(S("bdn_in"), 16)
            pool.dma_start(g_ffn, A["g_ffn"][0].partition_broadcast(P)).then_inc(S("gffn_in"), 16)
            for c in (12, 13):
                power(st[:, c:c + 1])

        @block.tensor
        def _(pe):
            at = [0]

            def begin(job):
                assert JOBS[at[0]] == job, (job, JOBS[at[0]])
                at[0] += 1
                if TURN[job] >= 1:
                    pe.wait_ge(bank_free[BANK[job]], TURN[job])
                return banks[BANK[job]]

            def done(mm, job):
                mm.then_inc(bank_full[BANK[job]], 1)

            def chunk(name):
                n = CHUNK_NO[name]
                pe.wait_ge(w_full[n % NSLOT], 16 * (n // NSLOT + 1))
                return ring[:, n % NSLOT, :]

            def transposes(job, parts):
                b = begin(job)
                for o, a in parts:
                    mm = nc.tensor.transpose(b[0:a.shape[1], o:o + a.shape[0]], a, ident[0:a.shape[0], 0:a.shape[0]])
                done(mm, job)

            def tiles(a):
                return [a[:, k, :] for k in range(KT)]

            def natural(jobs, w, n, src=tiles(uT), kt=KT, c0=0):
                for i, job in jobs:
                    b = begin(job)
                    for k in range(kt):
                        mm = nc.tensor.matmul(b[:, 0:n], src[k][:, P * i:P * i + P], w[:, k, c0:c0 + n],
                                              start=k == 0, stop=k == kt - 1)
                    done(mm, job)

            def slot3(name, kt, n):
                return chunk(name)[:, 0:kt * n].rearrange("p (k n) -> p k n", k=kt)

            pe.wait_ge(S("cst_in"), 16)
            pe.wait_ge(S("vec_in"), 16 * 9)
            transposes("vecT", [(0, vec)])
            for i in range(NT):
                pe.wait_ge(S("mem_norm"), i + 1)
                for h in range(2):
                    transposes(f"memT{i}{h}", [(P * k, memn[:, i, P * (4 * h + k):P * (4 * h + k) + P]) for k in range(4)])
            for i in range(NT):
                pe.wait_ge(S("x_norm"), i + 1)
                for h in range(2):
                    transposes(f"uT{i}{h}", [(P * k, un[:, i, P * (4 * h + k):P * (4 * h + k) + P]) for k in range(4)])
            for x in ("00", "01", "10", "11"):
                was_read(pe, f"memT{x}")
            for part in ("mk", "mv"):
                natural([(i, f"{part}{i}") for i in range(NT)], slot3(part, KT, 512), 512, src=tiles(memT))
            for x in ("00", "01", "10", "11"):
                was_read(pe, f"uT{x}")
            natural([(i, f"mq{i}") for i in range(NT)], slot3("mq", KT, 512), 512)
            for n in range(4):
                w = slot3(f"qk{n // 2}", KT, 512)
                b = begin(f"qk{n}")
                for j in range(2):
                    c0 = 256 * (n % 2) + P * j
                    for k in range(KT):
                        mm = nc.tensor.matmul(b[:, 256 * j:256 * j + 256], w[:, k, c0:c0 + P], uT[:, k, :],
                                              start=k == 0, stop=k == KT - 1)
                done(mm, f"qk{n}")
            pe.wait_ge(S("mk_norm"), 1)
            for i in range(NT):
                transposes(f"mkT{i}", [(P * h, mkv[:, i, P * h:P * h + P]) for h in range(4)])
            natural([(i, f"v{i}") for i in range(NT)], slot3("v", KT, 512), 512)
            pe.wait_ge(S("mq_norm"), 1)
            for i in range(NT):
                transposes(f"mqT{i}", [(P * h, mqn[:, i, P * h:P * h + P]) for h in range(4)])
            pe.wait_ge(S("small_in"), 16 * 4)
            b = begin("gif")
            for j in range(2):
                for k in range(KT):
                    mm = nc.tensor.matmul(b[0:4, 256 * j:256 * j + 256], wif[:, k, 4 * j:4 * j + 4], uT[:, k, :],
                                          start=k == 0, stop=k == KT - 1)
            done(mm, "gif")
            for i in range(NT):
                was_read(pe, f"mkT{i}")
                was_read(pe, f"mqT{i}")

            def mem_scores(h):
                b = begin(f"ms{h}")
                for i in range(NT):
                    mm = nc.tensor.matmul(b[:, 256 * i:256 * i + 256], mqT[:, h, P * i:P * i + P], mkT[:, h, :],
                                          start=True, stop=True)
                done(mm, f"ms{h}")

            def mem_turn(h):
                pe.wait_ge(S("memP"), h + 1)
                transposes(f"mP{h}", [(256 * m + P * i, Pm[h % 2][:, i, P * m:P * m + P]) for m in range(2) for i in range(NT)])

            def mem_out(pair):
                b = begin(f"mo{pair}")
                for j in range(2):
                    h = 2 * pair + j
                    was_read(pe, f"mP{h}")
                    for m in range(2):
                        mm = nc.tensor.matmul(b[:, 256 * j:256 * j + 256], mkv[:, m, 512 + P * h:512 + P * h + P],
                                              PTm[h % 2][:, m, :], start=m == 0, stop=m == 1)
                done(mm, f"mo{pair}")

            mem_scores(0)
            mem_scores(1)
            natural([(i, f"o{i}") for i in range(NT)], slot3("o", KT, 512), 512)
            pe.wait_ge(S("rows_ready"), 1)
            transposes("gT", [(4 * i, r_g[:, P * i:P * i + P]) for i in range(NT)]
                       + [(8 + 4 * i, r_nm[:, P * i:P * i + P]) for i in range(NT)])
            mem_turn(0)
            mem_scores(2)
            mem_turn(1)
            mem_scores(3)
            mem_out(0)
            natural([(i, f"nq{i}") for i in range(NT)], slot3("nq", KT, 512), 512)
            b = begin("ngate")
            for i in range(NT):
                for k in range(KT):
                    mm = nc.tensor.matmul(b[:, 24 * i:24 * i + 24], uT[:, k, P * i:P * i + P], wng[:, k, :],
                                          start=k == 0, stop=k == KT - 1)
            done(mm, "ngate")
            mem_turn(2)
            mem_turn(3)
            mem_out(1)

            def ml_scores(h):
                b = begin(f"ST{h}")
                nc.tensor.matmul(b[:, 0:256], qk[:, 4 + h, 0:P], qk[:, h, :], start=True, stop=True)
                mm = nc.tensor.matmul(b[:, 256:384], qk[:, 4 + h, P:SEQ], qk[:, h, P:SEQ], start=True, stop=True)
                done(mm, f"ST{h}")
                b = begin(f"MB{h}")
                mm = nc.tensor.matmul(b[:, 0:256], ident[0:4, h:h + 1].to_broadcast([4, P]), r_M, start=True, stop=True)
                done(mm, f"MB{h}")

            def ml_out(h):
                pe.wait_ge(S("wd_ready"), h + 1)
                b = begin(f"num{h}")
                w = wd[h % 2]
                nc.tensor.matmul(b[:, 0:129], w[:, 0:P], vaug[:, 0, h, :], start=True, stop=True)
                nc.tensor.matmul(b[:, 256:385], w[:, P:256], vaug[:, 0, h, :], start=True, stop=False)
                mm = nc.tensor.matmul(b[:, 256:385], w[:, 256:384], vaug[:, 1, h, :], start=False, stop=True)
                done(mm, f"num{h}")

            def turned(job, w, c0, src, kt):
                b = begin(job)
                for j in range(2):
                    for k in range(kt):
                        mm = nc.tensor.matmul(b[:, 256 * j:256 * j + 256], w[:, k, c0 + P * j:c0 + P * j + P], src[k],
                                              start=k == 0, stop=k == kt - 1)
                done(mm, job)

            def bgate(name, hh, j):
                turned(f"{name}{hh}{j}", slot3(f"{name}{hh}", KT, 512), 256 * j, tiles(uT), KT)

            pe.wait_ge(S("qk_ready"), 2)
            pe.wait_ge(S("ones_col"), 1)
            was_read(pe, "v0")
            was_read(pe, "v1")
            ml_scores(0)
            bgate("bgm", 0, 0)
            ml_scores(1)
            ml_out(0)
            bgate("bgm", 0, 1)
            ml_scores(2)
            ml_out(1)
            bgate("bgm", 1, 0)
            ml_scores(3)
            ml_out(2)
            bgate("bgm", 1, 1)
            ml_out(3)

            natural([(i, f"nkv{i}") for i in range(NT)], slot3("nkv", KT, 512), 512)
            w = slot3("kcvc", KT, 256)
            b = begin("kcvc")
            for j in range(2):
                for k in range(KT):
                    mm = nc.tensor.matmul(b[:, 256 * j:256 * j + 256], w[:, k, P * j:P * j + P], uT[:, k, :],
                                          start=k == 0, stop=k == KT - 1)
            done(mm, "kcvc")
            pe.wait_ge(S("q_roped"), 1)
            for i in range(NT):
                transposes(f"nqT{i}", [(P * j, qr[:, i, P * j:P * j + P]) for j in range(4)])
            pe.wait_ge(S("hml_ready"), 1)
            for i in range(NT):
                transposes(f"hmlT{i}", [(P * h, hml[:, i, h, :]) for h in range(4)])
            for n, (name, job) in enumerate((("w1k", "hk"), ("w1v", "hv"))):
                w = slot3(name, 16, CMP_HID)
                pe.wait_ge(S("blk_ready"), 2 * n + 2)
                b = begin(job)
                for m in range(4):
                    for g in range(4):
                        mm = nc.tensor.matmul(b[32 * g:32 * g + 32, 0:CMP_HID], blk[:, n, 4 * m + g, :],
                                              w[:, 4 * m + g, :], start=m == 0, stop=m == 3)
                done(mm, job)
            pe.wait_ge(S("k_roped"), 1)
            for i in range(NT):
                transposes(f"nkT{i}", [(P * (2 * br + g), kr[:, i, br, g].rearrange("p u d -> p (u d)"))
                                       for br in range(2) for g in range(2)])
            for n, job in enumerate(("hk", "hv")):
                was_read(pe, job)
                b = begin(job + "T")
                for f in range(2):
                    mm = nc.tensor.matmul(b[:, 32 * f:32 * f + 32], hidp[:, n, P * f:P * f + P], C("sum4"), start=True, stop=True)
                done(mm, job + "T")
            bgate("bgl", 0, 0)
            bgate("bgl", 0, 1)
            pe.wait_ge(S("hid_ready"), 1)
            pe.wait_ge(S("w2_in"), 32)
            b = begin("kc")
            for f in range(2):
                mm = nc.tensor.matmul(b[0:30, 0:DH], hid[:, 0, f, :], w2[:, 0, f, :], start=f == 0, stop=f == 1)
            done(mm, "kc")
            pe.wait_ge(S("hid_ready"), 2)
            b = begin("vc")
            for g in range(2):
                for f in range(2):
                    mm = nc.tensor.matmul(b[0:NCMP, DH * g:DH * g + DH], hid[:, 1, f, NCMP * g:NCMP * g + NCMP],
                                          w2[:, 1, f, :], start=f == 0, stop=f == 1)
            done(mm, "vc")
            bgate("bgl", 1, 0)
            bgate("bgl", 1, 1)
            pe.wait_ge(S("kc_roped"), 1)
            transposes("kcT", [(0, kcn[0:30, :])])
            for x in ("nqT0", "nqT1", "nkT0", "nkT1", "vc", "kcT"):
                was_read(pe, x)

            def nsa_scores(h):
                r, j, g = DH * (h % 2), h // 2, h // GROUP
                q = [qT[r:r + DH, j, P * i:P * i + P] for i in range(NT)]
                b = begin(f"sA{h}")
                for br in range(2):
                    mm = nc.tensor.matmul(b[:, 256 * br:256 * br + 256], q[1], kT[r:r + DH, 2 * br + g, :], start=True, stop=True)
                done(mm, f"sA{h}")
                b = begin(f"sB{h}")
                for br in range(2):
                    nc.tensor.matmul(b[:, P * br:P * br + P], q[0], kT[r:r + DH, 2 * br + g, 0:P], start=True, stop=True)
                for i in range(NT):
                    o = 256 + NCMP * i
                    mm = nc.tensor.matmul(b[:, o:o + NCMP], q[i], kcT[r:r + DH, NCMP * g:NCMP * g + NCMP], start=True, stop=True)
                done(mm, f"sB{h}")

            def nsa_turn(h):
                pe.wait_ge(S("nsaP"), h + 1)
                s = Sn[h % 2]
                for br, job in enumerate((f"tA{h}", f"tB{h}")):
                    transposes(job, [(0, s[:, 512 + P * br:512 + P * br + P]),
                                     (P, s[:, 256 * br:256 * br + P]),
                                     (256, s[:, 256 * br + P:256 * br + 256]),
                                     (384, s[:, 768 + NCMP * br:768 + NCMP * br + NCMP])])

            def nsa_out(h):
                r, g = DH * (h % 2), h // GROUP
                was_read(pe, f"tA{h}")
                was_read(pe, f"tB{h}")
                if h % 2 == 0:
                    return
                b = begin(f"nv{h // 2}")
                for hh in (h - 1, h):
                    r, t = DH * (hh % 2), PTn[hh % 2]
                    o = b[r:r + DH, :]
                    for br in range(2):
                        v = nkv[:, :, 256 * br + P + DH * g:256 * br + P + DH * g + DH]
                        nc.tensor.matmul(o[:, 0:256], v[:, 0, :], t[:, 384 * br:384 * br + 256], start=br == 0, stop=False)
                        nc.tensor.matmul(o[:, P:256], v[:, 1, :], t[:, 384 * br + 256:384 * br + 384], start=False, stop=False)
                    mm = nc.tensor.matmul(o[:, 0:256], vc[0:NCMP, DH * g:DH * g + DH], t[0:NCMP, 768:1024], start=False, stop=True)
                done(mm, f"nv{h // 2}")

            def project(name, wname, hT):
                w = slot3(wname, 4, D)
                for hh in range(2):
                    for j in range(2):
                        turned(f"{name}{hh}{j}", w, 512 * hh + 256 * j, hT, 4)

            nsa_scores(0)
            nsa_scores(1)
            was_read(pe, "mo0")
            was_read(pe, "mo1")
            project("pm", "wbm", hT_mem)
            for h in range(QH):
                nsa_turn(h)
                if h + 2 < QH:
                    nsa_scores(h + 2)
                if h == 0:
                    was_read(pe, "hmlT0")
                    was_read(pe, "hmlT1")
                    project("pl", "wbl", hT_ml)
                if h in (1, 2):
                    bgate("bgn", 0, h - 1)
                if h in (4, 5):
                    bgate("bgn", 1, h - 4)
                nsa_out(h)
            for j in range(4):
                was_read(pe, f"nv{j}")
            project("pn", "wbn", hT_nsa)

            pe.wait_ge(S("merged"), 8)
            mg = tiles(mergedT)

            def x1_turn(i, h):
                was_read(pe, f"wo{h}{i}")
                transposes(f"xT{i}{h}", [(P * k, x_sb[:, i, P * (4 * h + k):P * (4 * h + k) + P]) for k in range(4)])

            for hh in range(2):
                natural([(i, f"wo{hh}{i}") for i in range(NT)], slot3(f"wo{hh}", KT, 512), 512, src=mg)
            for h in range(2):
                for i in range(NT):
                    x1_turn(i, h)
            for name in JOBS[-len(TAIL) - NB:-len(TAIL)]:
                was_read(pe, name)
            for i in range(NT):
                for hh in range(2):
                    nc.tensor.matmul(ACC[i][hh][:, :], ident, x_sb[:, i, 512 * hh:512 * hh + 512],
                                     start=True, stop=False, skip_group_check=True)
            w = slot3("wr", KT, NE)
            for x in ("00", "10", "01", "11"):
                was_read(pe, f"xT{x}")
            b = begin("lT")
            for k in range(KT):
                g = k % 4
                mm = nc.tensor.matmul(b[32 * g:32 * g + 32, 0:SEQ], w[:, k, :], uT[:, k, :], start=k < 4, stop=k >= 4)
            done(mm, "lT")
            was_read(pe, "lT")
            b = begin("lg")
            for i in range(NT):
                mm = nc.tensor.matmul(b[:, NE * i:NE * i + NE], cp[:, P * i:P * i + P], C("sum4"), start=True, stop=True)
            done(mm, "lg")
            pe.wait_ge(S("sel_ready"), 1)
            b = begin("rank")
            nc.tensor.matmul(b[:, 0:NE], C("strict"), sel[:, 0, :], start=True, stop=True)
            nc.tensor.matmul(b[:, NE:2 * NE], ones, sel[:, 0, :], start=True, stop=False)
            nc.tensor.matmul(b[:, NE:2 * NE], C("strict"), sel[:, 1, :], start=False, stop=True)
            for i in range(NT):
                mm = nc.tensor.matmul(b[0:NE, 64:65], sel[:, i, :], ones[:, 0:1], start=i == 0, stop=i == NT - 1)
            done(mm, "rank")
            pe.wait_ge(S("rank_ready"), 1)
            transposes("rT", [(P * i, rank_it[:, i, 0:NE]) for i in range(NT)]
                       + [(256 + P * i, w_it[:, i, 0:NE]) for i in range(NT)])
            b = begin("ov")
            nc.tensor.matmul(b[0:NE, 0:1], C("strict")[0:NE, 0:NE], nov, start=True, stop=True)
            mm = nc.tensor.matmul(b[0:1, 1:2], nov, ones[0:NE, 0:1], start=True, stop=True)
            done(mm, "ov")
            pe.wait_ge(S("over_ready"), 1)
            b = begin("it")
            for i in range(NT):
                o = MAX_OVER * i
                nc.tensor.matmul(b[:, o:o + MAX_OVER], rTs[:, P * i:P * i + P], Eov, start=True, stop=False)
                nc.tensor.matmul(b[:, o:o + MAX_OVER], ones[0:NE, :], Aov, start=False, stop=True)
            for i in range(NT):
                o = MAX_OVER * (2 + i)
                nc.tensor.matmul(b[:, o:o + MAX_OVER], rTs[:, 256 + P * i:256 + P * i + P], Eov, start=True, stop=True)
            mm = nc.tensor.matmul(b[0:1, 64:64 + MAX_OVER], C("pcol")[0:NE, :], Eov, start=True, stop=True)
            done(mm, "it")
            assert at[0] == len(JOBS)
            pe.wait_ge(S("bdn_in"), 16)
            for i in range(NT):
                for hh in range(2):
                    nc.tensor.matmul(ACC[i][hh][:, :], rTs[:, 256 + P * i:256 + P * i + P],
                                     b_dn[:, 512 * hh:512 * hh + 512], start=False, stop=False, skip_group_check=True)
            for name in TAIL[-4:]:
                was_read(pe, name)

            def gather():
                for half, b in ((1, BX), (0, BG)):
                    for c in range(4):
                        for i in range(NT):
                            o = P * (4 * half + c)
                            mm = nc.tensor.matmul(b[:, P * c:P * c + P], x2[:, i, o:o + P], Gm[:, i, :],
                                                  start=i == 0, stop=i == NT - 1)
                    mm.then_inc(S("g_full"), 1)

            def scatter(last=False):
                for t in range(NT):
                    for hh in range(2):
                        mm = nc.tensor.matmul(ACC[t][hh][:, :], STs[:, P * t:P * t + P],
                                              y_sb[:, 512 * hh:512 * hh + 512], start=False, stop=last, skip_group_check=True)
                    if last:
                        mm.then_inc(S("sum_ready"), 1)
                if not last:
                    mm.then_inc(S("scattered"), 1)

            def up(i, par):
                pe.wait_ge(S("brow_in"), i * 16 + 16)
                for b in range(2):
                    for hh in range(2):
                        o = 1024 * b + 512 * hh
                        mm = nc.tensor.matmul(BH[b][64 * hh:64 * hh + 64, :], ones[0:1, 0:64], brow[:, o:o + 512],
                                              start=True, stop=False, skip_group_check=True)
                mm.then_inc(S("brow_used"), 1)
                for q in range(4):
                    pe.wait_ge(w_full[q], i * 16 + 16 * (TRUNK_TURNS + 1))
                    w = ring[:, q, :].rearrange("p (c n) -> p c n", c=2)
                    for c in range(2):
                        k = 2 * q + c
                        for b in range(2):
                            for hh in range(2):
                                o = 1024 * b + 512 * hh
                                mm = nc.tensor.matmul(BH[b][64 * hh:64 * hh + 64, :], xgT[:, k, 64 * par:64 * par + 64],
                                                      w[:, c, o:o + 512], start=False, stop=k == KT - 1,
                                                      skip_group_check=True)
                    mm.then_inc(S("gu_done"), 1)

            def down(i):
                pe.wait_ge(S("act_ready"), i * 2 + 2)
                for q in range(4):
                    mm = nc.tensor.transpose(BX[:, P * q:P * q + P], act_sb[:, P * q:P * q + P], ident)
                mm.then_inc(S("a_full"), 1)
                pe.wait_ge(S("a_evac"), i + 1)
                for d in range(2):
                    pe.wait_ge(w_full[4 + d], i * 16 + 16 * (TRUNK_TURNS + 1))
                    w = ring[:, 4 + d, :].rearrange("p (c n) -> p c n", c=4)
                    for c in range(4):
                        k = 4 * d + c
                        o = P * (2 * (k // 4) + k % 2) + 64 * ((k // 2) % 2)
                        for hh in range(2):
                            mm = nc.tensor.matmul(BG[64 * hh:64 * hh + 64, :], actT[:, o:o + 64],
                                                  w[:, c, 512 * hh:512 * hh + 512],
                                                  start=k == 0, stop=k == KT - 1, skip_group_check=True)
                    mm.then_inc(S("down_done"), 1)

            def pair(j):
                pe.wait_ge(S("g_evac"), j * 2 + 2)
                pe.wait_ge(S("st_evac"), j + 1)
                up(j * 2, 0)
                pe.wait_ge(S("y_evac"), j * 2 + 1)
                scatter()
                down(j * 2)
                up(j * 2 + 1, 1)
                pe.wait_ge(S("G_ready"), j + 2)
                pe.wait_ge(S("y_evac"), j * 2 + 2)
                gather()
                pe.wait_ge(S("Gw_ready"), j + 1)
                pe.wait_ge(S("act_ready"), j * 4 + 4)
                for t in range(NT):
                    mm = nc.tensor.transpose(BH[0][:, P * t:P * t + P], Gw[:, t, :], ident)
                mm.then_inc(S("st_full"), 1)
                pe.wait_ge(S("g_evac"), j * 2 + 4)
                down(j * 2 + 1)

            pe.wait_ge(S("G_ready"), 1)
            pe.wait_ge(S("x2_ready"), 2)
            gather()
            with pe.Fori(0, NE // 2) as j:
                pair(j)
            pe.wait_ge(S("idx_ready"), 1)
            n_pairs = pe.value_load(idx[0:1, MAX_OVER:MAX_OVER + 1], min_val=0, max_val=MAX_OVER // 2)
            with pe.If(n_pairs > 0):
                with pe.Fori(0, n_pairs) as k:
                    pair(k + NE // 2)
            pe.wait_ge(S("last_y"), 1)
            scatter(last=True)

        @block.scalar
        def _(act):
            def copy(job, dst, src):
                arrived(act, job)
                read(nc.scalar.activation(dst, src, ACT.Copy), job)

            def row(a, r, n):
                act.dma_start(vec[r:r + n, :], a).then_inc(S("vec_in"), 16)

            row(A["g_mix"].rearrange("a (n p) -> (a n) p", p=P), 0, 8)
            row(A["g_mem"].rearrange("a (n p) -> (a n) p", p=P), 8, 8)
            row(A["ml_conv_w"][0].rearrange("j (n p) -> (j n) p", p=P), 16, 32)
            row(A["ml_conv_b"].rearrange("a (n p) -> (a n) p", p=P), 48, 8)
            row(A["cmp_b1_k"].rearrange("a (n p) -> (a n) p", p=P), 56, 2)
            row(A["cmp_b1_v"].rearrange("a (n p) -> (a n) p", p=P), 58, 2)
            row(A["cmp_pos_k"][0].rearrange("(m l) d -> m (l d)", l=2), 60, 16)
            row(A["cmp_pos_v"][0].rearrange("(m l) d -> m (l d)", l=2), 76, 16)
            row(A["g_ffn"].rearrange("a (n p) -> (a n) p", p=P), 92, 8)

            act.wait_ge(S("mem_in"), 16)
            for i in range(NT):
                nc.scalar.activation(uT[:, 0:4, :].rearrange("p k t -> p (k t)"), memn[:, i, :], ACT.Square,
                                     accum_out=st[:, i:i + 1]).then_inc(S("sumsq"), 1)
                act.wait_ge(S("sumsq"), i + 1)
            act.wait_ge(S("x_in"), 16)
            for i in range(NT):
                nc.scalar.activation(uT[:, 4:8, :].rearrange("p k t -> p (k t)"), x_sb[:, i, :], ACT.Square,
                                     accum_out=st[:, 2 + i:3 + i]).then_inc(S("sumsq"), 1)
                act.wait_ge(S("sumsq"), 3 + i)

            def copy_and_square(job, dst, sq):
                arrived(act, job)
                nc.scalar.activation(dst, bank(job)[:, :], ACT.Copy)
                read(nc.scalar.activation(sq, bank(job)[:, :], ACT.Square), job)

            for x in ("10", "11"):
                arrived(act, f"memT{x}")
            for i in range(NT):
                copy_and_square(f"mk{i}", mkv[:, i, 0:512], sqA[:, i, :])
            for i in range(NT):
                copy(f"mv{i}", mkv[:, i, 512:1024], bank(f"mv{i}")[:, :])
            for i in range(NT):
                copy_and_square(f"mq{i}", mqn[:, i, :], sqB[:, i, :])
            arrived(act, "uT11")
            act.wait_ge(S("pad_zero"), 1)
            for n in range(4):
                copy(f"qk{n}", pre[:, 2 * n:2 * n + 2, 3:3 + SEQ],
                     bank(f"qk{n}")[:, :].rearrange("p (j t) -> p j t", j=2))
            for i in range(NT):
                copy(f"mkT{i}", mkT[:, :, P * i:P * i + P], bank(f"mkT{i}")[:, :].rearrange("p (h t) -> p h t", h=4))
            for i in range(NT):
                copy(f"v{i}", vaug[:, i, :, 0:P], bank(f"v{i}")[:, :].rearrange("p (h t) -> p h t", h=4))
            for i in range(NT):
                copy(f"mqT{i}", mqT[:, :, P * i:P * i + P], bank(f"mqT{i}")[:, :].rearrange("p (h t) -> p h t", h=4))
            for n in range(2):
                act.wait_ge(S("conv_done"), 1)
                nc.scalar.activation(cp[:, 1024 * n:1024 * n + 1024], qk[:, 4 * n:4 * n + 4, :].rearrange("p j t -> p (j t)"),
                                     ACT.Sigmoid).then_inc(S("conv_sig"), 1)
            act.wait_ge(S("absf"), 1)
            nc.scalar.activation(r_B, r_B, ACT.Exp, scale=-1.0).then_inc(S("act_rows"), 1)
            act.wait_ge(S("act_rows"), 1)
            nc.scalar.activation(r_B, r_B, ACT.Ln, bias=1.0).then_inc(S("act_rows"), 1)

            def mem_exp(h):
                act.wait_ge(S("mem_nmax"), h + 1)
                if h >= 2:
                    arrived(act, f"mP{h - 2}")
                for i in range(NT):
                    ins = nc.scalar.activation(Pm[h % 2][:, i, :], bank(f"ms{h}")[:, 256 * i:256 * i + 256], ACT.Exp,
                                               bias=st[:, 32 + 2 * h + i:33 + 2 * h + i],
                                               accum_out=st[:, 40 + 2 * h + i:41 + 2 * h + i])
                read(ins, f"ms{h}")

            def mem_turned(h):
                copy(f"mP{h}", PTm[h % 2], bank(f"mP{h}")[:, :].rearrange("p (m t) -> p m t", m=2))

            act.wait_ge(S("mk_norm"), 1)
            act.wait_ge(S("mq_norm"), 1)
            mem_exp(0)
            mem_exp(1)
            for i in range(NT):
                arrived(act, f"o{i}")
                read(nc.scalar.activation(osig[:, i, :], bank(f"o{i}")[:, :], ACT.Sigmoid), f"o{i}")
            mem_turned(0)
            mem_exp(2)
            mem_turned(1)
            mem_exp(3)
            arrived(act, "mkT1")
            copy("mo0", heads[:, 0, 0:2, :], bank("mo0")[:, :].rearrange("p (h t) -> p h t", h=2))
            for i in range(NT):
                copy(f"nq{i}", nq_sb[:, i, :], bank(f"nq{i}")[:, :])
            arrived(act, "ngate")
            read(nc.scalar.activation(gsb[:, :, :].rearrange("p i n -> p (i n)"), bank("ngate")[:, 0:48], ACT.Sigmoid), "ngate")
            mem_turned(2)
            mem_turned(3)
            copy("mo1", heads[:, 1, 0:2, :], bank("mo1")[:, :].rearrange("p (h t) -> p h t", h=2))

            def gate(name, dst, hh, j):
                job = f"{name}{hh}{j}"
                arrived(act, job)
                o = 1024 * hh + 512 * j
                read(nc.scalar.activation(dst[:, o:o + 512], bank(job)[:, :], ACT.Sigmoid), job)

            def ml_exp(h):
                was_read(act, f"MB{h}")
                nc.scalar.activation(Dt, Dt, ACT.Exp, scale=-1.0).then_inc(S("ml_exp"), 1)

            def ml_num(h):
                copy(f"num{h}", num[:, h], bank(f"num{h}")[:, :].rearrange("p (i e) -> p i e", i=2)[:, :, 0:129])

            was_read(act, "gT")
            nc.scalar.activation(st[:, 64:72], st[:, 56:64], ACT.Exp).then_inc(S("expm"), 1)
            ml_exp(0)
            gate("bgm", bg0, 0, 0)
            ml_exp(1)
            ml_num(0)
            gate("bgm", bg0, 0, 1)
            ml_exp(2)
            ml_num(1)
            gate("bgm", bg0, 1, 0)
            ml_exp(3)
            ml_num(2)
            gate("bgm", bg0, 1, 1)
            ml_num(3)
            act.wait_ge(S("h_div"), 1)
            nc.scalar.activation(sp_[:, 0:1024], hml.rearrange("p i h e -> p (i h e)"), ACT.Square).then_inc(S("h_sq"), 1)
            for i in range(NT):
                copy(f"nkv{i}", nkv[:, i, :], bank(f"nkv{i}")[:, :])
            act.wait_ge(S("hml_ready"), 1)
            arrived(act, "kcvc")
            for n in range(2):
                for g in range(2):
                    s = bank("kcvc")[DH * g:DH * g + DH, 256 * n:256 * n + 256]
                    nc.scalar.activation(k2[0:DH, n, g, :], s, ACT.Copy)
                    ins = nc.scalar.activation(k2[DH:P, n, g, 0:255], s[:, 1:256], ACT.Copy)
            read(ins, "kcvc")
            arrived(act, "mo1")
            for i in range(NT):
                copy(f"nqT{i}", qT[:, :, P * i:P * i + P], bank(f"nqT{i}")[:, :].rearrange("p (h t) -> p h t", h=4))
            for i in range(NT):
                copy(f"hmlT{i}", nqr[:, :].rearrange("p (h t) -> p h t", h=4)[:, :, P * i:P * i + P], bank(f"hmlT{i}")[:, :].rearrange("p (h t) -> p h t", h=4))
            for n, job in enumerate(("hk", "hv")):
                copy(job, hidp[:, n, :], bank(job)[:, 0:CMP_HID])
            for i in range(NT):
                copy(f"nkT{i}", kT[:, :, P * i:P * i + P], bank(f"nkT{i}")[:, :].rearrange("p (h t) -> p h t", h=4))
            for n, job in enumerate(("hkT", "hvT")):
                arrived(act, job)
                for f in range(2):
                    s = bank(job)[:, 32 * f:32 * f + 30]
                    col = vcol[:, 56 + 2 * n + f:57 + 2 * n + f]
                    nc.scalar.activation(hid[:, n, f, :], s, ACT.Identity, bias=col)
                    ins = nc.scalar.activation(hsg[:, n, f, :], s, ACT.Sigmoid, bias=col)
                read(ins, job)
            gate("bgl", bg1, 0, 0)
            gate("bgl", bg1, 0, 1)
            copy("vc", vc[0:NCMP, :], bank("vc")[0:NCMP, 0:128])
            gate("bgl", bg1, 1, 0)
            gate("bgl", bg1, 1, 1)
            copy("kcT", kcT, bank("kcT")[:, 0:30])

            def nsa_exp(h):
                act.wait_ge(S("nsa_nmax"), h + 1)
                s, o = Sn[h % 2], 80 + 16 * (h % 2)
                segs = [(768 + NCMP * i, NCMP, 3 * i) for i in range(2)]
                segs += [(512 + P * br, P, 1 + br) for br in range(2)] + [(256 * br, 256, 4 + br) for br in range(2)]
                for a, n, c in segs:
                    ins = nc.scalar.activation(s[:, a:a + n], s[:, a:a + n], ACT.Exp, bias=st[:, o + c:o + c + 1],
                                               accum_out=st[:, o + 8 + c:o + 9 + c])
                ins.then_inc(S("nsa_exp"), 1)

            def nsa_turned(h):
                if h >= 2:
                    arrived(act, f"nv{h // 2 - 1}")
                for br, job in enumerate((f"tA{h}", f"tB{h}")):
                    arrived(act, job)
                    nc.scalar.activation(PTn[h % 2][:, 384 * br:384 * br + 384], bank(job)[:, 0:384], ACT.Copy)
                    read(nc.scalar.activation(PTn[h % 2][0:NCMP, 768 + P * br:768 + P * br + P],
                                              bank(job)[0:NCMP, 384:512], ACT.Copy), job)

            nsa_exp(0)
            nsa_exp(1)
            for h in range(QH):
                nsa_turned(h)
                if h + 2 < QH:
                    nsa_exp(h + 2)
                if h in (1, 2):
                    was_read(act, "pm11")
                    gate("bgn", bg0, 0, h - 1)
                if h in (4, 5):
                    gate("bgn", bg0, 1, h - 4)
                if h % 2 == 1:
                    copy(f"nv{h // 2}", hT_nsa[h // 2], bank(f"nv{h // 2}")[:, 0:256])
            for i in range(NT):
                was_read(act, f"wo1{i}")
                nc.scalar.activation(cp[:, 1024:2048], x_sb[:, i, :], ACT.Square,
                                     accum_out=st[:, 4 + i:5 + i]).then_inc(S("sumsq"), 1)
                act.wait_ge(S("sumsq"), 5 + i)
            copy("lT", cp[:, 0:SEQ], bank("lT")[:, 0:SEQ])
            act.wait_ge(S("lg_ready"), 1)
            for i in range(NT):
                ins = nc.scalar.activation(lg[:, i, :], lg[:, i, :], ACT.Exp, bias=st[:, 120 + i:121 + i])
            ins.then_inc(S("lg_exp"), 1)

            def tokens(n):
                for k, (half, b) in enumerate(((1, BX), (0, BG))):
                    act.wait_ge(S("g_full"), n + (k + 1))
                    nc.scalar.activation(xgT[:, 4 * half:4 * half + 4, :].rearrange("p c n -> p (c n)"), b[:, :],
                                         ACT.Copy).then_inc(S("g_evac"), 1)

            def gates(i):
                for b in range(2):
                    act.wait_ge(S("g_clip"), i * 2 + (b + 1))
                    nc.scalar.activation(sg[b], gt[b], ACT.Sigmoid, scale=ALPHA).then_inc(S("g_sig"), 1)

            def results(i, par):
                act.wait_ge(S("a_full"), i + 1)
                nc.scalar.activation(actT, BX[:, :], ACT.Copy).then_inc(S("a_evac"), 1)
                act.wait_ge(S("down_done"), i * 2 + 2)
                nc.scalar.activation(y_sb[64 * par:64 * par + 64, 0:512], BG[0:64, :], ACT.Copy)
                nc.scalar.activation(y_sb[64 * par:64 * par + 64, 512:1024], BG[64:P, :], ACT.Copy).then_inc(S("y_evac"), 1)

            def pair(j):
                gates(j * 2)
                act.wait_ge(S("scattered"), j + 1)
                results(j * 2, 0)
                gates(j * 2 + 1)
                tokens(j * 2 + 2)
                act.wait_ge(S("st_full"), j + 1)
                nc.scalar.activation(STs, BH[0][:, 0:256], ACT.Copy).then_inc(S("st_evac"), 1)
                results(j * 2 + 1, 1)

            arrived(act, "nv3")
            nc.scalar.activation(STs, C("ones")[:, 0:1].to_broadcast([P, 256]), ACT.Copy, scale=0.0).then_inc(S("st_evac"), 1)
            nc.scalar.activation(y_sb, C("ones")[:, 0:1].to_broadcast([P, 1024]), ACT.Copy, scale=0.0).then_inc(S("y_evac"), 1)
            tokens(0)
            with act.Fori(0, NE // 2) as j:
                pair(j)
            act.wait_ge(S("idx_ready"), 1)
            n_pairs = act.value_load(idx[0:1, MAX_OVER:MAX_OVER + 1], min_val=0, max_val=MAX_OVER // 2)
            with act.If(n_pairs > 0):
                with act.Fori(0, n_pairs) as k:
                    pair(k + NE // 2)
            nc.scalar.activation(sg[0][:, 0:1], sg[0][:, 1:2], ACT.Copy).then_inc(S("last_y"), 1)
            act.wait_ge(S("last_y"), 1)
            for t in range(NT):
                act.wait_ge(S("sum_ready"), t + 1)
                nc.scalar.activation(x_sb[:, t, 512:1024], ACC[t][1][:, :], ACT.Copy).then_inc(S("out_right"), 1)
                act.wait_ge(S("out_right"), t + 1)
                act.dma_start(out_t[:, t, 512:1024], x_sb[:, t, 512:1024]).then_inc(S("out_done"), 16)

        @block.vector
        def _(dve):
            V = nc.vector
            counts = {}

            def step(ins, name="dve"):
                counts[name] = counts.get(name, 0) + 1
                ins.then_inc(S(name), 1)
                dve.wait_ge(S(name), counts[name])

            def step_read(ins, job):
                read(ins, job)
                was_read(dve, job)

            def rstd(dst, src, n):
                step(V.tensor_scalar(dst, src, 1.0 / n, EPS, ALU.mult, ALU.add), "mean_ready")
                dve.wait_ge(S("rstd_done"), counts["mean_ready"])

            step(V.memset(rank_it[:, :, ITEMS:], UNSEL))
            step(V.memset(vaug[:, :, :, P:P + 1], 1.0), "ones_col")
            for i in range(NT):
                dve.wait_ge(S("sumsq"), i + 1)
                rstd(st[:, 8 + i:9 + i], st[:, i:i + 1], D)
                step(V.tensor_scalar(memn[:, i, :], memn[:, i, :], st[:, 8 + i:9 + i], None, ALU.mult), "mem_norm")
            for i in range(NT):
                dve.wait_ge(S("sumsq"), 3 + i)
                rstd(st[:, 10 + i:11 + i], st[:, 2 + i:3 + i], D)
                step(V.tensor_scalar(un[:, i, :], x_sb[:, i, :], st[:, 10 + i:11 + i], None, ALU.mult), "x_norm")
            arrived(dve, "vecT")
            step_read(V.tensor_copy(vcol[:, :], bank("vecT")[:, 0:VROWS]), "vecT")
            for name, dst, g0 in (("memT", memT, 8), ("uT", uT, 0)):
                for i in range(NT):
                    for h in range(2):
                        job = f"{name}{i}{h}"
                        arrived(dve, job)
                        read(V.tensor_tensor(dst[:, 4 * h:4 * h + 4, P * i:P * i + P],
                                             bank(job)[:, :].rearrange("p (k t) -> p k t", k=4),
                                             last(vcol[:, g0 + 4 * h:g0 + 4 * h + 4], P), ALU.mult), job)
            dve.wait_ge(S("cst_in"), 16)
            dve.wait_ge(S("bc_in"), 16 * 6)
            step(V.tensor_scalar(g_q, g_q, DH ** -0.5, None, ALU.mult))
            step(V.tensor_scalar(g_mq, g_mq, DH_MEM ** -0.5, None, ALU.mult))
            arrived(dve, "uT11")
            step(V.memset(pre[:, :, 0:3], 0.0), "pad_zero")

            def head_norm(x, ss, g, hd, sq, nh):
                step(V.tensor_reduce(ss, sq, AX.X, ALU.add))
                rstd(ss, ss, hd)
                step(V.tensor_tensor(x, x, last(ss, hd), ALU.mult))
                return V.tensor_tensor(x, x, mid(g, nh), ALU.mult)

            for name, x, sq, g, o in (("mk", mkv[:, :, 0:512], sqA, g_mk, 16), ("mq", mqn, sqB, g_mq, 24)):
                for i in range(NT):
                    was_read(dve, f"{name}{i}")
                for i in range(NT):
                    ins = head_norm(x[:, i, :].rearrange("p (h e) -> p h e", h=4), st[:, o + 4 * i:o + 4 * i + 4], g, DH_MEM,
                                    sq[:, i, :].rearrange("p (h e) -> p h e", h=4), 4)
                    step(ins, f"{name}_norm" if i == NT - 1 else "dve")
            for n in range(2):
                for j in range(4 * n, 4 * n + 4):
                    was_read(dve, f"qk{j // 2}")
                    step(V.tensor_scalar(qk[:, j, :], pre[:, j, 0:SEQ], vcol[:, 16 + j:17 + j], vcol[:, 48 + j:49 + j],
                                         ALU.mult, ALU.add))
                    for a in range(1, CONV):
                        col = vcol[:, 16 + 8 * a + j:17 + 8 * a + j]
                        ins = V.scalar_tensor_tensor(out=qk[:, j, :], in0=pre[:, j, a:a + SEQ], scalar=col, in1=qk[:, j, :],
                                                     op0=ALU.mult, op1=ALU.add)
                        step(ins, "conv_done" if (j, a) == (7, CONV - 1) else "dve")
            arrived(dve, "gif")
            step(V.tensor_scalar(r_f, bank("gif")[0:4, 256:512], bif[:, 1:2], None, ALU.add))
            step(V.scalar_tensor_tensor(out=r_B, in0=r_f, scalar=-1.0, in1=r_f, op0=ALU.mult, op1=ALU.max), "absf")
            for n in range(2):
                dve.wait_ge(S("conv_sig"), n + 1)
                q = qk[:, 4 * n:4 * n + 4, :].rearrange("p j t -> p (j t)")
                step(V.tensor_tensor(q, q, cp[:, 1024 * n:1024 * n + 1024], ALU.mult), "qk_ready")
            dve.wait_ge(S("act_rows"), 2)
            step(V.scalar_tensor_tensor(out=r_f, in0=r_f, scalar=0.0, in1=r_B, op0=ALU.min, op1=ALU.subtract))
            step(V.memset(r_M, 1.0))
            step(V.tensor_tensor_scan(r_B, r_M, r_f, 0.0, ALU.mult, ALU.add))
            step_read(V.scalar_tensor_tensor(out=r_g, in0=bank("gif")[0:4, 0:256], scalar=bif[:, 0:1], in1=r_B,
                                             op0=ALU.add, op1=ALU.subtract), "gif")
            step(V.memset(r_f, 0.0))
            step(V.tensor_tensor_scan(r_M, r_f, r_g, 0.0, ALU.add, ALU.max))
            step(V.scalar_tensor_tensor(out=r_nm, in0=r_B, scalar=-1.0, in1=r_M, op0=ALU.mult, op1=ALU.subtract), "rows_ready")

            def mem_max(h):
                arrived(dve, f"ms{h}")
                c = st[:, 32 + 2 * h:34 + 2 * h]
                step(V.tensor_reduce(c, bank(f"ms{h}")[:, :].rearrange("p (i m) -> p i m", i=2), AX.X, ALU.max))
                step(V.tensor_scalar(c, c, -1.0, None, ALU.mult), "mem_nmax")

            def mem_norm(h):
                was_read(dve, f"ms{h}")
                c = st[:, 40 + 2 * h:42 + 2 * h]
                step(V.reciprocal(c, c))
                step(V.tensor_tensor(Pm[h % 2], Pm[h % 2], last(c, 256), ALU.mult), "memP")

            mem_max(0)
            mem_max(1)
            mem_norm(0)
            arrived(dve, "gT")
            step(V.tensor_copy(st[:, 48:64], bank("gT")[:, 0:16]))
            step_read(V.tensor_copy(st[:, 72:80], bank("gT")[:, 0:8]), "gT")
            mem_max(2)
            mem_norm(1)
            mem_max(3)
            mem_norm(2)
            mem_norm(3)

            def rope(dst, src, cos, sin, nh):
                pr = src.shape[0]
                c, s = mid(cos[0:pr], nh), mid(sin[0:pr], nh)
                a = tmp[0:pr, 0:32 * nh].rearrange("p (h d) -> p h d", h=nh)
                b = tmp[0:pr, 256:256 + 32 * nh].rearrange("p (h d) -> p h d", h=nh)
                lo, hi = src[:, :, 0:32], src[:, :, 32:64]
                V.tensor_tensor(a, lo, c, ALU.mult)
                step(V.tensor_tensor(b, hi, s, ALU.mult))
                for d in dst:
                    ins = V.tensor_tensor(d[:, :, 0:32], a, b, ALU.subtract)
                step(ins)
                V.tensor_tensor(a, hi, c, ALU.mult)
                step(V.tensor_tensor(b, lo, s, ALU.mult))
                for d in dst:
                    ins = V.tensor_tensor(d[:, :, 32:64], a, b, ALU.add)
                return ins

            for i in range(NT):
                was_read(dve, f"nq{i}")
                q = nq_sb[:, i, :].rearrange("p (h e) -> p h e", h=QH)
                sq = qr[:, i, :].rearrange("p (h e) -> p h e", h=QH)
                step(V.tensor_tensor(sq, q, q, ALU.mult))
                step(head_norm(q, st[:, 128 + 8 * i:136 + 8 * i], g_q, DH, sq, QH))
                step(rope([sq], q, C(f"cos{i}"), C(f"sin{i}"), QH), "q_roped" if i == NT - 1 else "dve")

            arrived(dve, "mo1")
            was_read(dve, "mP3")
            for h in range(NH_ML):
                arrived(dve, f"MB{h}")
                V.tensor_scalar(Dt[:, 0:256], bank(f"MB{h}")[:, 0:256], st[:, 72 + h:73 + h], 0.0, ALU.subtract, ALU.max)
                step_read(V.tensor_scalar(Dt[:, 256:384], bank(f"MB{h}")[:, P:256], st[:, 76 + h:77 + h], 0.0,
                                          ALU.subtract, ALU.max), f"MB{h}")
                arrived(dve, f"ST{h}")
                dve.wait_ge(S("ml_exp"), h + 1)
                if h >= 2:
                    arrived(dve, f"num{h - 2}")
                w = wd[h % 2]
                step_read(V.scalar_tensor_tensor(out=w, in0=bank(f"ST{h}")[:, 0:384], scalar=DH_ML ** -0.5, in1=Dt,
                                                 op0=ALU.mult, op1=ALU.mult), f"ST{h}")
                V.tensor_tensor(w[:, 0:P], w[:, 0:P], C("upper"), ALU.mult)
                step(V.tensor_tensor(w[:, 256:384], w[:, 256:384], C("upper"), ALU.mult), "wd_ready")
            for h in range(NH_ML):
                was_read(dve, f"num{h}")
            dve.wait_ge(S("expm"), 1)
            den = st[:, 160:168].rearrange("p (i h) -> p i h", i=NT)
            nd = num[:, :, :, P].rearrange("p h i -> p i h")
            step(V.scalar_tensor_tensor(out=den, in0=nd, scalar=-1.0, in1=nd, op0=ALU.mult, op1=ALU.max))
            step(V.tensor_tensor(st[:, 160:168], st[:, 160:168], st[:, 64:72], ALU.max))
            step(V.reciprocal(st[:, 160:168], st[:, 160:168]))
            for i in range(NT):
                ins = V.tensor_tensor(hml[:, i], num[:, :, i, 0:P], last(st[:, 160 + 4 * i:164 + 4 * i], P), ALU.mult)
            step(ins, "h_div")
            dve.wait_ge(S("h_sq"), 1)
            hv = hml.rearrange("p i h e -> p (i h) e")
            step(V.tensor_reduce(st[:, 168:176], sp_[:, 0:1024].rearrange("p (a e) -> p a e", e=P), AX.X, ALU.add))
            rstd(st[:, 168:176], st[:, 168:176], DH_ML)
            step(V.tensor_tensor(hv, hv, last(st[:, 168:176], P), ALU.mult))
            h2 = hml.rearrange("p i h e -> p i (h e)")
            step(V.tensor_tensor(h2, h2, mid(g_ml, NT), ALU.mult))
            was_read(dve, "o1")
            step(V.tensor_tensor(h2, h2, osig, ALU.mult), "hml_ready")

            step(V.memset(blk[:, :, :, 2 * NCMP:], 0.0))
            was_read(dve, "kcvc")
            for n in range(2):
                for g in range(2):
                    src = k2[:, n, g, :]
                    src = bass.AP(src.tensor, src.offset, [list(src.ap[0]), [2, 16], [16, NCMP]])
                    pos = last(vcol[:, 60 + 16 * n:76 + 16 * n], NCMP)
                    step(V.tensor_tensor(blk[:, n, :, NCMP * g:NCMP * g + NCMP], src, pos, ALU.add), "blk_ready")

            for i in range(NT):
                was_read(dve, f"nkv{i}")
                for br in range(2):
                    k = nkv[:, i, 256 * br:256 * br + P].rearrange("p (g e) -> p g e", g=KVH)
                    sq = ksq[:, 0:P].rearrange("p (g e) -> p g e", g=KVH)
                    step(V.tensor_tensor(sq, k, k, ALU.mult))
                    o = 144 + 2 * (2 * i + br)
                    step(head_norm(k, st[:, o:o + 2], g_k[:, DH * (1 + br):DH * (2 + br)], DH, sq, KVH))
                    ins = rope([kr[:, i, br, :, u, :] for u in range(2)], k, C(f"cos{i}"), C(f"sin{i}"), KVH)
                    step(ins, "k_roped" if (i, br) == (1, 1) else "dve")
            for n, job in enumerate(("hkT", "hvT")):
                was_read(dve, job)
                step(V.tensor_tensor(hid[:, n], hid[:, n], hsg[:, n], ALU.mult), "hid_ready")
            arrived(dve, "kc")
            kn = ksq[0:30, 128:192].unsqueeze(1)
            step_read(V.tensor_copy(ksq[0:30, 128:192], bank("kc")[0:30, 0:DH]), "kc")
            ksq1 = ksq[0:30, 192:256].unsqueeze(1)
            step(V.tensor_tensor(ksq1, kn, kn, ALU.mult))
            step(head_norm(kn, st[0:30, 152:153], g_k[0:30, 0:DH], DH, ksq1, 1))
            step(rope([kcn[0:30, DH * u:DH * u + DH].unsqueeze(1) for u in range(2)], kn, C("cosc"), C("sinc"), 1), "kc_roped")

            def merge(name, gates, first):
                for n in range(4):
                    job = f"{name}{n // 2}{n % 2}"
                    arrived(dve, job)
                    m, g = mT[:, 512 * n:512 * n + 512], gates[:, 512 * n:512 * n + 512]
                    if first:
                        step_read(V.tensor_tensor(m, bank(job)[:, :], g, ALU.mult), job)
                    else:
                        step_read(V.tensor_tensor(g, bank(job)[:, :], g, ALU.mult), job)
                        step(V.tensor_tensor(m, m, g, ALU.add), "merged")

            def nsa_mask(h):
                s, o = Sn[h % 2], 80 + 16 * (h % 2)
                if h >= 2:
                    arrived(dve, f"tB{h - 2}")
                arrived(dve, f"sA{h}")
                s1 = s[:, 0:512].rearrange("p (b m) -> p b m", b=2)
                s0 = s[:, 512:768].rearrange("p (b m) -> p b m", b=2)
                sc_ = s[:, 768:798]
                step_read(V.tensor_tensor(s1, bank(f"sA{h}")[:, :].rearrange("p (b m) -> p b m", b=2),
                                          mid(C("mask256"), 2), ALU.add), f"sA{h}")
                arrived(dve, f"sB{h}")
                V.tensor_tensor(s0, bank(f"sB{h}")[:, 0:256].rearrange("p (b m) -> p b m", b=2),
                                mid(C("mask256")[:, P:256], 2), ALU.add)
                step_read(V.tensor_tensor(sc_, bank(f"sB{h}")[:, 256:286], C("cmpadd"), ALU.add), f"sB{h}")
                V.tensor_reduce(st[:, o + 4:o + 6], s1, AX.X, ALU.max)
                V.tensor_reduce(st[:, o + 1:o + 3], s0, AX.X, ALU.max)
                step(V.tensor_reduce(st[:, o:o + 6].rearrange("p (i b) -> p i b", i=2)[:, :, 0],
                                     sc_.rearrange("p (i n) -> p i n", i=2), AX.X, ALU.max))
                step(V.tensor_scalar(st[:, o:o + 6], st[:, o:o + 6], -1.0, None, ALU.mult), "nsa_nmax")

            def nsa_weights(h):
                s, o = Sn[h % 2], 88 + 16 * (h % 2)
                dve.wait_ge(S("nsa_exp"), h + 1)
                sc_ = s[:, 768:798]
                step(V.tensor_tensor(sc_, sc_, C("cmp01"), ALU.mult))
                c3 = st[:, o:o + 6].rearrange("p (i b) -> p i b", i=2)
                step(V.tensor_reduce(c3[:, :, 0], sc_.rearrange("p (i n) -> p i n", i=2), AX.X, ALU.add))
                step(V.tensor_scalar(st[:, o:o + 6], st[:, o:o + 6], 1e-30, None, ALU.max))
                step(V.reciprocal(st[:, o:o + 6], st[:, o:o + 6]))
                step(V.tensor_tensor(c3, c3, gsb[:, :, 3 * h:3 * h + 3], ALU.mult))
                s1 = s[:, 0:512].rearrange("p (b m) -> p b m", b=2)
                s0 = s[:, 512:768].rearrange("p (b m) -> p b m", b=2)
                sc2 = sc_.rearrange("p (i n) -> p i n", i=2)
                V.tensor_tensor(s1, s1, last(st[:, o + 4:o + 6], 256), ALU.mult)
                V.tensor_tensor(s0, s0, last(st[:, o + 1:o + 3], P), ALU.mult)
                step(V.tensor_tensor(sc2, sc2, c3[:, :, 0].unsqueeze(2).to_broadcast([P, 2, NCMP]), ALU.mult), "nsaP")

            arrived(dve, "hmlT1")
            was_read(dve, "ngate")
            nsa_mask(0)
            nsa_mask(1)
            nsa_weights(0)
            was_read(dve, "bgm11")
            merge("pm", bg0, True)
            for h in range(QH):
                if h + 2 < QH:
                    nsa_mask(h + 2)
                if h == 0:
                    was_read(dve, "bgl11")
                    nsa_weights(1)
                    merge("pl", bg1, False)
                elif h + 1 < QH:
                    nsa_weights(h + 1)
            was_read(dve, "bgn11")
            merge("pn", bg0, False)
            for hh in range(2):
                for i in range(NT):
                    job = f"wo{hh}{i}"
                    arrived(dve, job)
                    xs = x_sb[:, i, 512 * hh:512 * hh + 512]
                    step_read(V.tensor_tensor(xs, xs, bank(job)[:, :], ALU.add), job)
            for h in range(2):
                for i in range(NT):
                    job = f"xT{i}{h}"
                    arrived(dve, job)
                    read(V.tensor_tensor(uT[:, 4 * h:4 * h + 4, P * i:P * i + P],
                                         bank(job)[:, :].rearrange("p (k t) -> p k t", k=4),
                                         last(vcol[:, 92 + 4 * h:96 + 4 * h], P), ALU.mult), job)
            dve.wait_ge(S("gffn_in"), 16)
            for i in range(NT):
                dve.wait_ge(S("sumsq"), 5 + i)
                rstd(st[:, 12 + i:13 + i], st[:, 4 + i:5 + i], D)
            for i in range(NT):
                step(V.scalar_tensor_tensor(out=x2[:, i, :], in0=x_sb[:, i, :], scalar=st[:, 12 + i:13 + i], in1=g_ffn,
                                            op0=ALU.mult, op1=ALU.mult), "x2_ready")

            arrived(dve, "lg")
            for i in range(NT):
                ins = V.scalar_tensor_tensor(out=lg[:, i, :], in0=bank("lg")[:, NE * i:NE * i + NE], scalar=st[:, 12 + i:13 + i],
                                             in1=b_r, op0=ALU.mult, op1=ALU.add)
            step_read(ins, "lg")
            for i in range(NT):
                ins = V.max(top[:, i, :], lg[:, i, :])
            step(ins)
            for i in range(NT):
                V.tensor_scalar(sel[:, i, :], lg[:, i, :], top[:, i, TOPK - 1:TOPK], None, ALU.is_gt)
                ins = V.tensor_scalar(eqv[:, i, :], lg[:, i, :], top[:, i, TOPK - 1:TOPK], None, ALU.is_equal)
            step(ins)
            step(V.tensor_scalar(st[:, 120:122], top[:, :, 0], -1.0, None, ALU.mult), "lg_ready")
            step(V.tensor_reduce(ngt, sel, AX.X, ALU.add))
            step(V.tensor_scalar(ngt, ngt, -1.0, float(TOPK), ALU.mult, ALU.add))
            for i in range(NT):
                ins = V.tensor_tensor_scan(cum[:, i, :], ones[:, 0:NE], eqv[:, i, :], 0.0, ALU.mult, ALU.add)
            step(ins)
            for i in range(NT):
                ins = V.scalar_tensor_tensor(out=cum[:, i, :], in0=cum[:, i, :], scalar=ngt[:, i:i + 1], in1=eqv[:, i, :],
                                             op0=ALU.is_le, op1=ALU.mult)
            step(ins)
            step(V.tensor_tensor(sel, sel, cum, ALU.add), "sel_ready")
            dve.wait_ge(S("lg_exp"), 1)
            wts = w_it[:, :, 0:NE]
            step(V.tensor_tensor(wts, lg, sel, ALU.mult))
            step(V.tensor_reduce(st[:, 122:124], wts, AX.X, ALU.add))
            step(V.reciprocal(st[:, 122:124], st[:, 122:124]))
            step(V.tensor_tensor(wts, wts, last(st[:, 122:124], NE), ALU.mult))
            arrived(dve, "rank")
            rk = rank_it[:, :, 0:NE]
            step(V.scalar_tensor_tensor(out=rk, in0=bank("rank")[:, 0:64].rearrange("p (i e) -> p i e", i=2), scalar=-UNSEL,
                                        in1=sel, op0=ALU.add, op1=ALU.mult))
            step(V.tensor_scalar(rk, rk, UNSEL, None, ALU.add))
            for n in range(3):
                ins = V.tensor_scalar(cntc[:, n:n + 1], bank("rank")[0:NE, 64:65], float(SLOT_TOK * (n + 1)), None, ALU.is_gt)
            step_read(ins, "rank")
            step(V.tensor_reduce(nov, cntc, AX.X, ALU.add), "rank_ready")
            arrived(dve, "rT")
            step_read(V.tensor_copy(rTs, bank("rT")[0:NE, :]), "rT")
            arrived(dve, "ov")
            step(V.tensor_copy(ost, bank("ov")[0:NE, 0:1]))
            step_read(V.tensor_scalar(few, C("over")[0:1, 0:MAX_OVER].rearrange("p (k two) -> p k two", two=2)[:, :, 0],
                                      bank("ov")[0:1, 1:2], None, ALU.is_lt), "ov")
            step(V.tensor_reduce(npair, few, AX.X, ALU.add))
            step(V.tensor_copy(idx[0:1, MAX_OVER:MAX_OVER + 1], npair))
            step(V.tensor_tensor(oen, ost, nov, ALU.add))
            ov = C("over")[0:NE, :]
            step(V.tensor_scalar(Eov, ov, ost, None, ALU.is_ge))
            step(V.scalar_tensor_tensor(out=Eov, in0=ov, scalar=oen, in1=Eov, op0=ALU.is_lt, op1=ALU.mult))
            step(V.tensor_scalar(Aov, ov, ost, 1.0, ALU.subtract, ALU.add))
            step(V.scalar_tensor_tensor(out=Aov, in0=Aov, scalar=-float(SLOT_TOK), in1=Eov, op0=ALU.mult, op1=ALU.mult), "over_ready")
            arrived(dve, "it")
            step(V.tensor_copy(idx[0:1, 0:MAX_OVER], bank("it")[0:1, 64:64 + MAX_OVER]), "idx_ready")
            V.tensor_copy(w_it[:, :, NE:ITEMS], bank("it")[:, 2 * MAX_OVER:4 * MAX_OVER].rearrange("p (i k) -> p i k", i=2))
            step_read(V.tensor_copy(rank_it[:, :, NE:ITEMS], bank("it")[:, 0:2 * MAX_OVER].rearrange("p (i k) -> p i k", i=2)), "it")

            def onehot(j):
                for t in range(NT):
                    for p in range(2):
                        ins = V.tensor_scalar(Gm[:, t, 64 * p:64 * p + 64], C("iota")[:, 0:64],
                                              rank_it[:, t, bass.ds(j * 2 + p, 1)], None, ALU.is_equal)
                ins.then_inc(S("G_ready"), 1)

            def activate(i):
                dve.wait_ge(S("gu_done"), i * 4 + 4)
                for b in range(2):
                    h = BH[b][:, :].rearrange("p (f two) -> p f two", two=2)
                    V.tensor_scalar(gt[b], h[:, :, 0], LIMIT, None, ALU.min).then_inc(S("g_clip"), 1)
                    V.tensor_scalar(ut[b], h[:, :, 1], -LIMIT, LIMIT, ALU.max, ALU.min).then_inc(S("u_clip"), 1)
                for b in range(2):
                    dve.wait_ge(S("g_sig"), i * 2 + (b + 1))
                    V.tensor_tensor(gt[b], gt[b], sg[b], ALU.mult).then_inc(S("gs_done"), 1)
                dve.wait_ge(S("u_clip"), i * 2 + 2)
                dve.wait_ge(S("gs_done"), i * 2 + 2)
                for b in range(2):
                    V.scalar_tensor_tensor(out=ut[b], in0=ut[b], scalar=1.0, in1=gt[b],
                                           op0=ALU.add, op1=ALU.mult).then_inc(S("act_ready"), 1)

            def pair(j):
                dve.wait_ge(S("gu_done"), j * 8 + 1)
                for t in range(NT):
                    for p in range(2):
                        o = j * 2 + p
                        ins = V.tensor_scalar(Gw[:, t, 64 * p:64 * p + 64], C("iota")[:, 0:64], rank_it[:, t, bass.ds(o, 1)],
                                              w_it[:, t, bass.ds(o, 1)], ALU.is_equal, ALU.mult)
                ins.then_inc(S("Gw_ready"), 1)
                onehot(j + 1)
                activate(j * 2)
                activate(j * 2 + 1)

            onehot(0)
            with dve.Fori(0, NE // 2) as j:
                pair(j)
            dve.wait_ge(S("idx_ready"), 1)
            n_pairs = dve.value_load(idx[0:1, MAX_OVER:MAX_OVER + 1], min_val=0, max_val=MAX_OVER // 2)
            with dve.If(n_pairs > 0):
                with dve.Fori(0, n_pairs) as k:
                    pair(k + NE // 2)
            for t in range(NT):
                dve.wait_ge(S("sum_ready"), t + 1)
                V.tensor_copy(x_sb[:, t, 0:512], ACC[t][0][:, :]).then_inc(S("out_left"), 1)


_INS = ["x", "mem", "g_mix", "w_in", "ml_conv_w", "ml_conv_b", "ml_b_i", "ml_b_f", "ml_g_out", "nsa_g_q", "nsa_g_k",
        "cmp_pos_k", "cmp_w1_k", "cmp_b1_k", "cmp_w2_k", "cmp_pos_v", "cmp_w1_v", "cmp_b1_v", "cmp_w2_v", "g_mem",
        "w_mem_kv", "mem_g_q", "mem_g_k", "w_br_ml", "w_br_nsa", "w_br_mem", "w_out", "g_ffn", "w_router", "b_router",
        "w_gu", "b_gu", "w_down", "b_down"]


def kernel(**inputs):
    import concourse.bacc as bacc
    from concourse.bass_utils import run_bass_kernel_spmd as run

    nc = bacc.Bacc("TRN2", target_bir_lowering=False, num_devices=1)
    arrays, A = {}, {}
    for name in _INS:
        a = np.ascontiguousarray(inputs[name])
        arrays[f"in_{name}"] = a
        A[name] = nc.dram_tensor(f"in_{name}", a.shape, mybir.dt.from_np(a.dtype), kind="ExternalInput").ap()
    arrays["shape_consts"] = CONST
    const = nc.dram_tensor("shape_consts", CONST.shape, F32, kind="ExternalInput").ap()
    out = nc.dram_tensor("out", (1, SEQ, D), F32, kind="ExternalOutput").ap()
    hybrid_layer(nc, A, const, out)
    r = run(nc, [arrays], core_ids=[0])
    return r.results[0]["out"]
```

```python
from contextlib import ExitStack

import numpy as np

import concourse.bass as bass
from concourse import mybir

F32 = mybir.dt.float32
I32 = mybir.dt.int32
ALU = mybir.AluOpType
ACT = mybir.ActivationFunctionType
AX = mybir.AxisListType

P = 128
D = 1024
SEQ = 256
NT = SEQ // P
KT = D // P
NH_ML, DH_ML = 4, 128
QH, KVH, DH = 8, 2, 64
GROUP = QH // KVH
NH_MEM, DH_MEM = 4, 128
CMP_BLOCK, CMP_STRIDE, CMP_HID = 32, 16, 256
NCMP = (SEQ - CMP_BLOCK) // CMP_STRIDE + 1
CONV = 4
NE, TOPK = 32, 4
SLOT_TOK = 64
ITEMS = NE + SEQ * TOPK // SLOT_TOK
EPS = 1e-6
NEG = -1e30
LIMIT, ALPHA = 7.0, 1.702
UNSEL = -4096.0

C_MLQ, C_V, C_O, C_IF = 0, 1024, 1536, 2048
C_NQ, C_KCVC, C_NKV, C_NG, C_MQ, C_BR = 2056, 2568, 2824, 3336, 3360, 3872

NSLOT = 6
SLOT = 4096
TWICE = 4


CHUNKS = [("mk", "mk1"), ("mv", "mv1"), ("mq", "mq1"), ("qk0", "qk1"), ("qk1", "qk3"), ("v", "v1"),
          ("o", "o1"), ("nq", "nq1"), ("bgm0", "bgm01"), ("bgm1", "bgm11"), ("nkv", "nkv1"),
          ("kcvc", "kcvc"), ("w1k", "hk"), ("w1v", "hv"), ("bgl0", "bgl01"), ("bgl1", "bgl11"),
          ("wbm", "pm11"), ("wbl", "pl11"), ("bgn0", "bgn01"), ("bgn1", "bgn11"), ("wbn", "pn11"),
          ("wo0", "wo01"), ("wo1", "wo11"), ("wr", "lT")]
SLOT_OF = {name: n % NSLOT for n, (name, _) in enumerate(CHUNKS)}
CHUNK_NO = {name: n for n, (name, _) in enumerate(CHUNKS)}
TRUNK_TURNS = len(CHUNKS) // NSLOT
assert TRUNK_TURNS * NSLOT == len(CHUNKS)


def job_order():
    four = [f"{a}{b}" for a in range(2) for b in range(2)]
    jobs = ["vecT"] + [f"memT{x}" for x in four] + [f"uT{x}" for x in four]
    jobs += ["mk0", "mk1", "mv0", "mv1", "mq0", "mq1", "qk0", "qk1", "qk2", "qk3"]
    jobs += ["mkT0", "mkT1", "v0", "v1", "mqT0", "mqT1", "gif", "ms0", "ms1", "o0", "o1", "gT"]
    jobs += ["mP0", "ms2", "mP1", "ms3", "mo0", "nq0", "nq1", "ngate", "mP2", "mP3", "mo1"]
    jobs += ["ST0", "MB0", "bgm00", "ST1", "MB1", "num0", "bgm01", "ST2", "MB2", "num1",
             "bgm10", "ST3", "MB3", "num2", "bgm11", "num3"]
    jobs += ["nkv0", "nkv1", "kcvc", "nqT0", "nqT1", "hmlT0", "hmlT1", "hk", "hv"]
    jobs += ["bgl00", "hkT", "hvT", "bgl01", "nkT0", "nkT1", "kc", "vc", "bgl10", "bgl11", "kcT"]
    jobs += ["sA0", "sB0", "sA1", "sB1"]
    jobs += [f"pm{x}" for x in four]
    filler = {0: [f"pl{x}" for x in four], 1: ["bgn00"], 2: ["bgn01"], 4: ["bgn10"], 5: ["bgn11"]}
    for h in range(QH):
        jobs += [f"tA{h}", f"tB{h}"]
        if h + 2 < QH:
            jobs += [f"sA{h + 2}", f"sB{h + 2}"]
        jobs += filler.get(h, [])
        if h % 2 == 1:
            jobs += [f"nv{h // 2}"]
    jobs += [f"pn{x}" for x in four]
    jobs += ["wo00", "wo01", "wo10", "wo11"]
    return jobs


JOBS = job_order()
NB = 8
TAIL = ["xT00", "xT10", "xT01", "xT11", "lT", "lg", "rank", "rT", "first", "it"]
BANK, TURN = {}, {}
for n, name in enumerate(JOBS + TAIL):
    BANK[name] = n % NB if n < len(JOBS) else 4 + (n - len(JOBS)) % 4
    TURN[name] = sum(BANK[other] == BANK[name] for other in list(BANK)[:-1])
JOBS += TAIL
assert len(BANK) == len(JOBS)


def const_table():
    parts, at = {}, 0
    cols = []

    def add(name, a):
        nonlocal at
        full = np.zeros((P, a.shape[1]), np.float32)
        full[:a.shape[0]] = a
        parts[name] = (at, a.shape[1])
        at += a.shape[1]
        cols.append(full)

    p = np.arange(P)
    add("ident", np.eye(P, dtype=np.float32))
    causal = np.where(p[None, :] > p[:, None], np.float32(NEG), np.float32(0)).astype(np.float32)
    add("mask256", np.concatenate([np.zeros((P, P), np.float32), causal], 1))
    add("upper", (p[:, None] <= p[None, :]).astype(np.float32))
    add("strict", (p[:, None] < p[None, :]).astype(np.float32))
    add("ones", np.ones((P, P), np.float32))
    ends = np.arange(NCMP) * CMP_STRIDE + CMP_BLOCK - 1
    ok = np.stack([ends[None, :] <= (p + P * i)[:, None] for i in range(NT)], 1)
    add("cmp01", ok.astype(np.float32).reshape(P, -1))
    add("cmpadd", np.where(ok, np.float32(0), np.float32(NEG)).astype(np.float32).reshape(P, -1))
    half = DH // 2
    inv = np.power(10000.0, (-np.arange(half, dtype=np.float32) / np.float32(half)).astype(np.float64))
    inv = inv.astype(np.float32)

    def rope(pos):
        ang = (pos.astype(np.float32)[:, None] * inv[None, :]).astype(np.float64)
        return np.cos(ang).astype(np.float32), np.sin(ang).astype(np.float32)

    for i in range(NT):
        c, s = rope(p + P * i)
        add(f"cos{i}", c)
        add(f"sin{i}", s)
    c, s = rope(np.tile(ends, KVH))
    add("cosc", c)
    add("sinc", s)
    add("iota", np.tile(np.arange(SLOT_TOK, dtype=np.float32), (P, 2)))
    add("sum4", np.tile(np.eye(32, dtype=np.float32), (4, 1)))
    add("mhalf", np.full((P, 8), -0.5, np.float32))
    add("pcol", p[:, None].astype(np.float32))
    add("odd", (p % 2)[:, None].astype(np.float32))
    return np.concatenate(cols, 1), parts


CONST, CPART = const_table()
VROWS = 100


def hybrid_layer(nc, A, const, out):
    with ExitStack() as ctx:
        def sb(name, *shape, dt=F32):
            return ctx.enter_context(nc.sbuf_tensor(name, list(shape), dt))

        sems = {}

        def S(name):
            if name not in sems:
                sems[name] = ctx.enter_context(nc.semaphore(name))
            return sems[name]

        scratch = [("qk", 2048), ("vo", 2056), ("mT", 2048), ("cp", 8 * (SEQ + 3)), ("uT", 2048), ("x_sb", 2048),
                   ("nkv", NT * 512), ("nqr", 1024), ("bg1", 2048)]
        mem = sb("ring", P, NSLOT * SLOT + sum(n for _, n in scratch))
        ring = mem[:, 0:(NSLOT + TWICE) * SLOT].rearrange("p (s n) -> p s n", n=SLOT)
        where, a = {}, NSLOT * SLOT
        for name, n in scratch:
            where[name] = mem[:, a:a + n]
            a += n
        qk = where["qk"].rearrange("p (j t) -> p j t", j=8)
        vo = where["vo"]
        mT = where["mT"]
        cp = where["cp"]
        uT = where["uT"].rearrange("p (k t) -> p k t", k=KT)
        x_sb = where["x_sb"].rearrange("p (i d) -> p i d", i=NT)
        nkv = where["nkv"].rearrange("p (i n) -> p i n", i=NT)
        nqr = where["nqr"]
        bg1 = where["bg1"]
        cst = sb("cst", P, CONST.shape[1])
        sc = sb("sc", P, 2048)
        mq = sb("mq", P, 2048)
        bg0 = sb("bg0", P, 2048)
        sp_ = sb("sp_", P, 3712)
        kcv = sb("kcv", P, 158)
        vcol = sb("vcol", P, VROWS)
        bcg = sb("bcg", P, 288)
        st = sb("st", P, 176)
        bif = sb("bif", 4, 2)
        gsb = sb("gsb", P, NT, 24)
        rank_it = sb("rank_it", P, NT, ITEMS + 2)
        w_it = sb("w_it", P, NT, ITEMS)
        idx = sb("idx", 1, NE + 2 * ITEMS + 1, dt=I32)

        banks = [ctx.enter_context(nc.psum_tensor(f"bank{i}", [P, 512], F32)) for i in range(NB)]
        bank_full = [S(f"bank_full{i}") for i in range(NB)]
        bank_free = [S(f"bank_free{i}") for i in range(NB)]
        w_full = [S(f"w_full{i}") for i in range(NSLOT + TWICE)]

        def C(name):
            a, n = CPART[name]
            return cst[:, a:a + n]

        def bank(job):
            return banks[BANK[job]]

        def arrived(eng, job):
            eng.wait_ge(bank_full[BANK[job]], TURN[job] + 1)

        def read(ins, job):
            return ins.then_inc(bank_free[BANK[job]], 1)

        def was_read(eng, job):
            eng.wait_ge(bank_free[BANK[job]], TURN[job] + 1)

        def mid(ap, n):
            return ap.unsqueeze(1).to_broadcast([ap.shape[0], n, ap.shape[1]])

        def last(ap, n):
            return ap.unsqueeze(2).to_broadcast([ap.shape[0], ap.shape[1], n])

        ident = C("ident")
        ones = C("ones")
        memn = sc[:, :].rearrange("p (i d) -> p i d", i=NT)
        un = cp[:, 0:2048].rearrange("p (i d) -> p i d", i=NT)
        memT = mT[:, :].rearrange("p (k t) -> p k t", k=KT)
        mergedT = mT[:, :].rearrange("p (k t) -> p k t", k=KT)
        mkv = sc[:, :].rearrange("p (i d) -> p i d", i=NT)
        pre = cp[:, :].rearrange("p (j t) -> p j t", j=8)
        x2 = sc[:, :].rearrange("p (i d) -> p i d", i=NT)
        vaug = vo[:, 0:NT * 4 * 129].rearrange("p (i h e) -> p i h e", i=NT, h=4)
        osig = vo[:, 1032:2056].rearrange("p (i n) -> p i n", i=NT)
        k2 = vo[:, 0:1024].rearrange("p (b h t) -> p b h t", b=2, h=2)
        blk = vo[:, 1024:2048].rearrange("p (b m n) -> p b m n", b=2, m=16)
        vec = bg0[0:VROWS, 0:P]
        wif = bg0[:, 128:192].rearrange("p (k n) -> p k n", k=KT)
        wng = bg0[:, 192:384].rearrange("p (k n) -> p k n", k=KT)
        rows = bg1[0:4, 0:1280]
        nq_sb = nqr[:, :].rearrange("p (i n) -> p i n", i=NT)
        heads = sc[:, :].rearrange("p (i k t) -> p i k t", i=2, k=4)
        hT_mem = [heads[:, k // 2, k % 2, :] for k in range(4)]
        hT_nsa = [heads[:, k // 2, 2 + k % 2, :] for k in range(4)]
        hT_ml = [nqr[:, 256 * k:256 * k + 256] for k in range(4)]
        mqn = nq_sb
        mqT = mq[:, 0:1024].rearrange("p (h t) -> p h t", h=4)
        mkT = mq[:, 1024:2048].rearrange("p (h t) -> p h t", h=4)
        qT = mq[:, 0:1024].rearrange("p (h t) -> p h t", h=4)
        kT = mq[:, 1024:2048].rearrange("p (b t) -> p b t", b=4)
        kcT, vc = kcv[:, 0:30], kcv[:, 30:158]
        tmp = mT[:, 0:512]
        w2 = mT[:, 512:768].rearrange("p (b f d) -> p b f d", b=2, f=2)
        kcn = mT[:, 768:896]
        hid = mT[:, 896:1016].rearrange("p (b f n) -> p b f n", b=2, f=2)
        hsg = mT[:, 1016:1136].rearrange("p (b f n) -> p b f n", b=2, f=2)
        ksq = mT[:, 1136:1536]
        hidp = mT[:, 1536:2048].rearrange("p (b f) -> p b f", b=2)
        qr = cp[:, 0:1024].rearrange("p (i n) -> p i n", i=NT)
        kr = cp[:, 1024:2048].rearrange("p (i b g u d) -> p i b g u d", i=NT, b=2, g=2, u=2)
        Pm = [sp_[:, 800 * b:800 * b + 512].rearrange("p (i m) -> p i m", i=NT) for b in range(2)]
        PTm = [sp_[:, 1600 + 1024 * b:1600 + 1024 * b + 512].rearrange("p (m t) -> p m t", m=2) for b in range(2)]
        sqA = sp_[:, 1600:2624].rearrange("p (i n) -> p i n", i=NT)
        sqB = sp_[:, 2624:3648].rearrange("p (i n) -> p i n", i=NT)
        Dt = sp_[:, 0:384]
        wd = [sp_[:, 384:768], sp_[:, 768:1152]]
        num = sp_[:, 1152:2184].rearrange("p (h i e) -> p h i e", h=4, i=NT)
        hml = sp_[:, 2184:3208].rearrange("p (i h e) -> p i h e", i=NT, h=4)
        Sn = [sp_[:, 800 * b:800 * b + 798] for b in range(2)]
        PTn = [sp_[:, 1600 + 1024 * b:2624 + 1024 * b] for b in range(2)]

        g_q, g_k = bcg[:, 0:64], bcg[:, 64:256]
        g_ml, g_mq, g_mk = bg1[:, 1280:1792], bg1[:, 1792:1920], bg1[:, 1920:2048]
        b_r = bcg[:, 256:288]
        g_ffn = bg1[:, 0:1024]
        b_dn = bg0[0:NE, 0:D]

        r_f, r_B, r_g, r_M, r_nm = (rows[:, 256 * n:256 * n + 256] for n in range(5))

        Gm = sp_[:, 0:256].rearrange("p (i n) -> p i n", i=NT)
        Gw = sp_[:, 256:512].rearrange("p (i n) -> p i n", i=NT)
        STs = sp_[:, 512:768]
        xgT = sp_[:, 768:1792].rearrange("p (c n) -> p c n", c=KT)
        gt = [sp_[:, 1792 + 256 * b:2048 + 256 * b] for b in range(2)]
        ut = [sp_[:, 2304 + 256 * b:2560 + 256 * b] for b in range(2)]
        act_sb = sp_[:, 2304:2816]
        sg = [sp_[:, 2816 + 256 * b:3072 + 256 * b] for b in range(2)]
        y_sb = mq[:, 0:1024]
        actT = mq[:, 1024:1536]
        brow = (bg0[32:33, :], bg0[64:65, :])
        brow_in = (S("brow_even"), S("brow_odd"))
        lg = bg1[:, 1024:1088].rearrange("p (i e) -> p i e", i=NT)
        top = bg1[:, 1088:1104].rearrange("p (i e) -> p i e", i=NT)
        sel = bg1[:, 1104:1168].rearrange("p (i e) -> p i e", i=NT)
        eqv = bg1[:, 1168:1232].rearrange("p (i e) -> p i e", i=NT)
        cum = bg1[:, 1232:1296].rearrange("p (i e) -> p i e", i=NT)
        ngt = bg1[:, 1296:1298]
        rTs = mq[0:32, 1536:2048]
        nit = bg1[0:32, 1300:1301]
        first = bg1[0:32, 1302:1303]
        end = bg1[0:32, 1304:1305]
        Eit = bg1[0:32, 1312:1312 + ITEMS]
        Ait = bg1[0:32, 1360:1360 + ITEMS]
        cntc = bg1[0:32, 1408:1411]
        few = bg1[0:1, 1412:1412 + ITEMS // 2 - 1]
        nlast = bg1[0:1, 1440:1441]
        before = bg1[0:1, 1448:1448 + NE]

        ACC = [[banks[2 * i + h] for h in range(2)] for i in range(NT)]
        BG, BX, BH = banks[4], banks[5], [banks[6], banks[7]]

        out_t = out[0].rearrange("(i p) d -> p i d", p=P)
        w_in = A["w_in"][0]
        w_mkv = A["w_mem_kv"][0]
        w_gu, b_gu, w_dn = A["w_gu"][0], A["b_gu"][0], A["w_down"][0]

        block = ctx.enter_context(nc.Block())

        def load_chunk(sp, e, q, odd):
            if q < 4:
                n, src = 2, w_gu[e].rearrange("(c p) n -> p c n", p=P)[:, 2 * q:2 * q + 2, :]
            else:
                n, src = 4, w_dn[e].rearrange("(c p) n -> p c n", p=P)[:, 4 * (q - 4):4 * (q - 4) + 4, :]
            slot = q + NSLOT if odd and q < TWICE else q
            sp.dma_start(ring[:, slot, :].rearrange("p (c n) -> p c n", c=n), src).then_inc(w_full[slot], 16)

        def lines(a):
            return a.rearrange("a (n p) -> (a n) p", p=P)

        vec_rows = [(lines(A["g_mix"]), 0, 8), (lines(A["g_mem"]), 8, 8),
                    (A["ml_conv_w"][0].rearrange("j (n p) -> (j n) p", p=P), 16, 32),
                    (lines(A["ml_conv_b"]), 48, 8), (lines(A["cmp_b1_k"]), 56, 2), (lines(A["cmp_b1_v"]), 58, 2),
                    (A["cmp_pos_k"][0].rearrange("(m l) d -> m (l d)", l=2), 60, 16),
                    (A["cmp_pos_v"][0].rearrange("(m l) d -> m (l d)", l=2), 76, 16), (lines(A["g_ffn"]), 92, 8)]

        def load_rows(eng, a, r, n):
            eng.dma_start(vec[r:r + n, :], a).then_inc(S("vec_in"), 16)

        @block.sync
        def _(sp):
            sp.dma_start(memn, A["mem"][0].rearrange("(i p) d -> p i d", p=P)).then_inc(S("mem_in"), 16)
            sp.dma_start(cst[:, :], const).then_inc(S("cst_in"), 16)
            sp.dma_start(x_sb[:, :, :], A["x"][0].rearrange("(i p) d -> p i d", p=P)).then_inc(S("x_in"), 16)
            for args in vec_rows[5:]:
                load_rows(sp, *args)

            def cols(a, c0, n=512):
                return a[:, c0:c0 + n].rearrange("(c p) n -> p c n", p=P)

            src = {
                "mk": cols(w_mkv, 0), "mv": cols(w_mkv, 512), "mq": cols(w_in, C_MQ),
                "qk0": cols(w_in, 0), "qk1": cols(w_in, 512), "v": cols(w_in, C_V), "o": cols(w_in, C_O),
                "nq": cols(w_in, C_NQ), "nkv": cols(w_in, C_NKV), "kcvc": cols(w_in, C_KCVC, 256),
                "w1k": A["cmp_w1_k"][0].rearrange("(m l) d f -> (l d) m f", l=2),
                "w1v": A["cmp_w1_v"][0].rearrange("(m l) d f -> (l d) m f", l=2),
                "wbm": cols(A["w_br_mem"][0], 0, D), "wbl": cols(A["w_br_ml"][0], 0, D),
                "wbn": cols(A["w_br_nsa"][0], 0, D),
                "wo0": cols(A["w_out"][0], 0), "wo1": cols(A["w_out"][0], 512),
                "wr": A["w_router"][0].rearrange("(c p) n -> p c n", p=P),
            }
            for b, name in enumerate(("bgl", "bgn", "bgm")):
                for h in range(2):
                    src[f"{name}{h}"] = cols(w_in, C_BR + D * b + 512 * h)
            sp.wait_ge(S("vec_in"), 16 * len(vec_rows))
            for n, (name, _) in enumerate(CHUNKS):
                s = src[name]
                if n >= NSLOT:
                    arrived(sp, CHUNKS[n - NSLOT][1])
                dst = ring[:, n % NSLOT, 0:s.shape[1] * s.shape[2]].rearrange("p (c n) -> p c n", c=s.shape[1])
                sp.dma_start(dst, s).then_inc(w_full[n % NSLOT], 16)
            for q in range(NSLOT):
                arrived(sp, CHUNKS[len(CHUNKS) - NSLOT + q][1])
                load_chunk(sp, 0, q, False)

            arrived(sp, "pn11")
            sp.wait_ge(S("merged"), 8)
            for e in range(2):
                sp.dma_start(brow[e], b_gu[e:e + 1, :]).then_inc(brow_in[e], 16)
            for q in range(TWICE):
                arrived(sp, ("hv", "lg", "rank", "nv3")[q])
                if q == 2:
                    sp.wait_ge(S("x2_ready"), 2)
                if q == 3:
                    sp.wait_ge(S("idx_ready"), 1)
                load_chunk(sp, 1, q, True)

            def load_round(e, odd, order):
                f = sp.value_load(idx[0:1, bass.ds(e, 1)], min_val=0, max_val=ITEMS - 1)
                if TWICE - 1 in order:
                    sp.wait_ge(S("brow_used"), f + 1)
                    sp.dma_start(brow[not odd], b_gu[bass.ds(e + 1, 1), :]).then_inc(brow_in[not odd], 16)
                for q in order:
                    if q < 4:
                        sp.wait_ge(S("gu_done"), f * 4 + (q + 1))
                    else:
                        sp.wait_ge(S("down_done"), f * 2 + (q - 3))
                    if q < TWICE:
                        load_chunk(sp, e + 1, q, not odd)
                    else:
                        load_chunk(sp, e, q, odd)

            load_round(1, True, [0, 1, 2, 3, 4, 5])
            steady = [0, 1, 4, 5, 2, 3]
            with sp.Fori(1, NE // 2 - 1) as r:
                load_round(r * 2, False, steady)
                load_round(r * 2 + 1, True, steady)
            load_round(NE - 2, False, steady)
            load_round(NE - 1, True, [4, 5])
            for t in range(NT):
                sp.wait_ge(S("out_left"), t + 1)
                sp.dma_start(out_t[:, t, 0:512], x2[:, t, 0:512]).then_inc(S("out_done"), 16)
            sp.wait_ge(S("out_done"), 16 * 2 * NT)

        @block.gpsimd
        def _(pool):
            pool.dma_start(wif, w_in[:, C_IF:C_IF + 8].rearrange("(c p) n -> p c n", p=P)).then_inc(S("small_in"), 16)
            pool.dma_start(wng, w_in[:, C_NG:C_NG + 24].rearrange("(c p) n -> p c n", p=P)).then_inc(S("small_in"), 16)
            pool.dma_start(bif[:, 0:1], A["ml_b_i"].rearrange("a h -> h a")).then_inc(S("small_in"), 16)
            pool.dma_start(bif[:, 1:2], A["ml_b_f"].rearrange("a h -> h a")).then_inc(S("small_in"), 16)

            def everywhere(dst, a):
                pool.dma_start(dst, a.partition_broadcast(P)).then_inc(S("bc_in"), 16)

            everywhere(g_q, A["nsa_g_q"][0])
            everywhere(g_k, A["nsa_g_k"][0].rearrange("b d -> (b d)"))
            everywhere(g_ml, A["ml_g_out"][0].rearrange("b d -> (b d)"))
            everywhere(g_mq, A["mem_g_q"][0])
            everywhere(g_mk, A["mem_g_k"][0])
            everywhere(b_r, A["b_router"][0])
            powers = [0]

            def power(ap):
                powers[0] += 1
                pool.wait_ge(S("mean_ready"), powers[0])
                nc.gpsimd.tensor_tensor(ap, ap, C("mhalf")[0:ap.shape[0], 0:ap.shape[1]], ALU.pow).then_inc(S("rstd_done"), 1)

            pool.wait_ge(S("cst_in"), 16)
            for c in range(8, 12):
                power(st[:, c:c + 1])
            for c in range(16, 32, 4):
                power(st[:, c:c + 4])
            arrived(pool, "mv1")
            pool.dma_start(w2[:, 0], A["cmp_w2_k"][0].rearrange("(f p) d -> p f d", p=P)).then_inc(S("w2_in"), 16)
            pool.dma_start(w2[:, 1], A["cmp_w2_v"][0].rearrange("(f p) d -> p f d", p=P)).then_inc(S("w2_in"), 16)
            for c in (128, 136):
                power(st[:, c:c + 8])
            power(st[:, 168:176])
            for c in range(144, 152, 2):
                power(st[:, c:c + 2])
            power(st[0:30, 152:153])
            pool.wait_ge(S("merged"), 4)
            pool.dma_start(g_ffn, A["g_ffn"][0].partition_broadcast(P)).then_inc(S("gffn_in"), 16)
            for c in (12, 13):
                power(st[:, c:c + 1])
            pool.wait_ge(S("merged"), 8)
            pool.dma_start(b_dn, A["b_down"][0]).then_inc(S("bdn_in"), 16)

        @block.tensor
        def _(pe):
            at = [0]

            def begin(job):
                assert JOBS[at[0]] == job, (job, JOBS[at[0]])
                at[0] += 1
                if TURN[job] >= 1:
                    pe.wait_ge(bank_free[BANK[job]], TURN[job])
                return banks[BANK[job]]

            def done(mm, job):
                mm.then_inc(bank_full[BANK[job]], 1)

            def chunk(name):
                n = CHUNK_NO[name]
                pe.wait_ge(w_full[n % NSLOT], 16 * (n // NSLOT + 1))
                return ring[:, n % NSLOT, :]

            def transposes(job, parts):
                b = begin(job)
                for o, a in parts:
                    mm = nc.tensor.transpose(b[0:a.shape[1], o:o + a.shape[0]], a, ident[0:a.shape[0], 0:a.shape[0]])
                done(mm, job)

            def tiles(a):
                return [a[:, k, :] for k in range(KT)]

            def natural(jobs, w, n, src=tiles(uT), kt=KT, c0=0):
                for i, job in jobs:
                    b = begin(job)
                    for k in range(kt):
                        mm = nc.tensor.matmul(b[:, 0:n], src[k][:, P * i:P * i + P], w[:, k, c0:c0 + n],
                                              start=k == 0, stop=k == kt - 1)
                    done(mm, job)

            def slot3(name, kt, n):
                return chunk(name)[:, 0:kt * n].rearrange("p (k n) -> p k n", k=kt)

            pe.wait_ge(S("cst_in"), 16)
            pe.wait_ge(S("vec_in"), 16 * len(vec_rows))
            transposes("vecT", [(0, vec)])
            for i in range(NT):
                pe.wait_ge(S("mem_norm"), i + 1)
                for h in range(2):
                    transposes(f"memT{i}{h}", [(P * k, memn[:, i, P * (4 * h + k):P * (4 * h + k) + P]) for k in range(4)])
            for i in range(NT):
                pe.wait_ge(S("x_norm"), i + 1)
                for h in range(2):
                    transposes(f"uT{i}{h}", [(P * k, un[:, i, P * (4 * h + k):P * (4 * h + k) + P]) for k in range(4)])
            for x in ("00", "01", "10", "11"):
                was_read(pe, f"memT{x}")
            for part in ("mk", "mv"):
                natural([(i, f"{part}{i}") for i in range(NT)], slot3(part, KT, 512), 512, src=tiles(memT))
            for x in ("00", "01", "10", "11"):
                was_read(pe, f"uT{x}")
            natural([(i, f"mq{i}") for i in range(NT)], slot3("mq", KT, 512), 512)
            for n in range(4):
                w = slot3(f"qk{n // 2}", KT, 512)
                b = begin(f"qk{n}")
                for j in range(2):
                    c0 = 256 * (n % 2) + P * j
                    for k in range(KT):
                        mm = nc.tensor.matmul(b[:, 256 * j:256 * j + 256], w[:, k, c0:c0 + P], uT[:, k, :],
                                              start=k == 0, stop=k == KT - 1)
                done(mm, f"qk{n}")
            pe.wait_ge(S("mk_norm"), 1)
            for i in range(NT):
                transposes(f"mkT{i}", [(P * h, mkv[:, i, P * h:P * h + P]) for h in range(4)])
            natural([(i, f"v{i}") for i in range(NT)], slot3("v", KT, 512), 512)
            pe.wait_ge(S("mq_norm"), 1)
            for i in range(NT):
                transposes(f"mqT{i}", [(P * h, mqn[:, i, P * h:P * h + P]) for h in range(4)])
            pe.wait_ge(S("small_in"), 16 * 4)
            b = begin("gif")
            for j in range(2):
                for k in range(KT):
                    mm = nc.tensor.matmul(b[0:4, 256 * j:256 * j + 256], wif[:, k, 4 * j:4 * j + 4], uT[:, k, :],
                                          start=k == 0, stop=k == KT - 1)
            done(mm, "gif")
            for i in range(NT):
                was_read(pe, f"mkT{i}")
                was_read(pe, f"mqT{i}")

            def mem_scores(h):
                b = begin(f"ms{h}")
                for i in range(NT):
                    mm = nc.tensor.matmul(b[:, 256 * i:256 * i + 256], mqT[:, h, P * i:P * i + P], mkT[:, h, :],
                                          start=True, stop=True)
                done(mm, f"ms{h}")

            def mem_turn(h):
                pe.wait_ge(S("memP"), h + 1)
                transposes(f"mP{h}", [(256 * m + P * i, Pm[h % 2][:, i, P * m:P * m + P]) for m in range(2) for i in range(NT)])

            def mem_out(pair):
                b = begin(f"mo{pair}")
                for j in range(2):
                    h = 2 * pair + j
                    was_read(pe, f"mP{h}")
                    for m in range(2):
                        mm = nc.tensor.matmul(b[:, 256 * j:256 * j + 256], mkv[:, m, 512 + P * h:512 + P * h + P],
                                              PTm[h % 2][:, m, :], start=m == 0, stop=m == 1)
                done(mm, f"mo{pair}")

            mem_scores(0)
            mem_scores(1)
            natural([(i, f"o{i}") for i in range(NT)], slot3("o", KT, 512), 512)
            pe.wait_ge(S("rows_ready"), 1)
            transposes("gT", [(4 * i, r_g[:, P * i:P * i + P]) for i in range(NT)]
                       + [(8 + 4 * i, r_nm[:, P * i:P * i + P]) for i in range(NT)])
            mem_turn(0)
            mem_scores(2)
            mem_turn(1)
            mem_scores(3)
            mem_out(0)
            natural([(i, f"nq{i}") for i in range(NT)], slot3("nq", KT, 512), 512)
            b = begin("ngate")
            for i in range(NT):
                for k in range(KT):
                    mm = nc.tensor.matmul(b[:, 24 * i:24 * i + 24], uT[:, k, P * i:P * i + P], wng[:, k, :],
                                          start=k == 0, stop=k == KT - 1)
            done(mm, "ngate")
            mem_turn(2)
            mem_turn(3)
            mem_out(1)

            def ml_scores(h):
                b = begin(f"ST{h}")
                nc.tensor.matmul(b[:, 0:256], qk[:, 4 + h, 0:P], qk[:, h, :], start=True, stop=True)
                mm = nc.tensor.matmul(b[:, 256:384], qk[:, 4 + h, P:SEQ], qk[:, h, P:SEQ], start=True, stop=True)
                done(mm, f"ST{h}")
                b = begin(f"MB{h}")
                mm = nc.tensor.matmul(b[:, 0:256], ident[0:4, h:h + 1].to_broadcast([4, P]), r_M, start=True, stop=True)
                done(mm, f"MB{h}")

            def ml_out(h):
                pe.wait_ge(S("wd_ready"), h + 1)
                b = begin(f"num{h}")
                w = wd[h % 2]
                nc.tensor.matmul(b[:, 0:129], w[:, 0:P], vaug[:, 0, h, :], start=True, stop=True)
                nc.tensor.matmul(b[:, 256:385], w[:, P:256], vaug[:, 0, h, :], start=True, stop=False)
                mm = nc.tensor.matmul(b[:, 256:385], w[:, 256:384], vaug[:, 1, h, :], start=False, stop=True)
                done(mm, f"num{h}")

            def turned(job, w, c0, src, kt):
                b = begin(job)
                for j in range(2):
                    for k in range(kt):
                        mm = nc.tensor.matmul(b[:, 256 * j:256 * j + 256], w[:, k, c0 + P * j:c0 + P * j + P], src[k],
                                              start=k == 0, stop=k == kt - 1)
                done(mm, job)

            def bgate(name, hh, j):
                turned(f"{name}{hh}{j}", slot3(f"{name}{hh}", KT, 512), 256 * j, tiles(uT), KT)

            pe.wait_ge(S("qk_ready"), 2)
            pe.wait_ge(S("ones_col"), 1)
            was_read(pe, "v0")
            was_read(pe, "v1")
            ml_scores(0)
            bgate("bgm", 0, 0)
            ml_scores(1)
            ml_out(0)
            bgate("bgm", 0, 1)
            ml_scores(2)
            ml_out(1)
            bgate("bgm", 1, 0)
            ml_scores(3)
            ml_out(2)
            bgate("bgm", 1, 1)
            ml_out(3)

            natural([(i, f"nkv{i}") for i in range(NT)], slot3("nkv", KT, 512), 512)
            w = slot3("kcvc", KT, 256)
            b = begin("kcvc")
            for j in range(2):
                for k in range(KT):
                    mm = nc.tensor.matmul(b[:, 256 * j:256 * j + 256], w[:, k, P * j:P * j + P], uT[:, k, :],
                                          start=k == 0, stop=k == KT - 1)
            done(mm, "kcvc")
            pe.wait_ge(S("q_roped"), 1)
            for i in range(NT):
                transposes(f"nqT{i}", [(P * j, qr[:, i, P * j:P * j + P]) for j in range(4)])
            pe.wait_ge(S("hml_ready"), 1)
            for i in range(NT):
                transposes(f"hmlT{i}", [(P * h, hml[:, i, h, :]) for h in range(4)])
            for n, (name, job) in enumerate((("w1k", "hk"), ("w1v", "hv"))):
                w = slot3(name, 16, CMP_HID)
                pe.wait_ge(S("blk_ready"), 2 * n + 2)
                b = begin(job)
                for m in range(4):
                    for g in range(4):
                        mm = nc.tensor.matmul(b[32 * g:32 * g + 32, 0:CMP_HID], blk[:, n, 4 * m + g, :],
                                              w[:, 4 * m + g, :], start=m == 0, stop=m == 3)
                done(mm, job)
            bgate("bgl", 0, 0)
            for n, job in enumerate(("hk", "hv")):
                was_read(pe, job)
                b = begin(job + "T")
                for f in range(2):
                    mm = nc.tensor.matmul(b[:, 32 * f:32 * f + 32], hidp[:, n, P * f:P * f + P], C("sum4"), start=True, stop=True)
                done(mm, job + "T")
            bgate("bgl", 0, 1)
            pe.wait_ge(S("k_roped"), 1)
            for i in range(NT):
                transposes(f"nkT{i}", [(P * (2 * br + g), kr[:, i, br, g].rearrange("p u d -> p (u d)"))
                                       for br in range(2) for g in range(2)])
            pe.wait_ge(S("hid_ready"), 1)
            pe.wait_ge(S("w2_in"), 32)
            b = begin("kc")
            for f in range(2):
                mm = nc.tensor.matmul(b[0:30, 0:DH], hid[:, 0, f, :], w2[:, 0, f, :], start=f == 0, stop=f == 1)
            done(mm, "kc")
            pe.wait_ge(S("hid_ready"), 2)
            b = begin("vc")
            for g in range(2):
                for f in range(2):
                    mm = nc.tensor.matmul(b[0:NCMP, DH * g:DH * g + DH], hid[:, 1, f, NCMP * g:NCMP * g + NCMP],
                                          w2[:, 1, f, :], start=f == 0, stop=f == 1)
            done(mm, "vc")
            bgate("bgl", 1, 0)
            bgate("bgl", 1, 1)
            pe.wait_ge(S("kc_roped"), 1)
            transposes("kcT", [(0, kcn[0:30, :])])
            for x in ("nqT0", "nqT1", "nkT0", "nkT1", "vc", "kcT"):
                was_read(pe, x)

            def nsa_scores(h):
                r, j, g = DH * (h % 2), h // 2, h // GROUP
                q = [qT[r:r + DH, j, P * i:P * i + P] for i in range(NT)]
                b = begin(f"sA{h}")
                for br in range(2):
                    mm = nc.tensor.matmul(b[:, 256 * br:256 * br + 256], q[1], kT[r:r + DH, 2 * br + g, :], start=True, stop=True)
                done(mm, f"sA{h}")
                b = begin(f"sB{h}")
                for br in range(2):
                    nc.tensor.matmul(b[:, P * br:P * br + P], q[0], kT[r:r + DH, 2 * br + g, 0:P], start=True, stop=True)
                for i in range(NT):
                    o = 256 + NCMP * i
                    mm = nc.tensor.matmul(b[:, o:o + NCMP], q[i], kcT[r:r + DH, NCMP * g:NCMP * g + NCMP], start=True, stop=True)
                done(mm, f"sB{h}")

            def nsa_turn(h):
                pe.wait_ge(S("nsaP"), h + 1)
                s = Sn[h % 2]
                for br, job in enumerate((f"tA{h}", f"tB{h}")):
                    transposes(job, [(0, s[:, 512 + P * br:512 + P * br + P]),
                                     (P, s[:, 256 * br:256 * br + P]),
                                     (256, s[:, 256 * br + P:256 * br + 256]),
                                     (384, s[:, 768 + NCMP * br:768 + NCMP * br + NCMP])])

            def nsa_out(h):
                r, g = DH * (h % 2), h // GROUP
                was_read(pe, f"tA{h}")
                was_read(pe, f"tB{h}")
                if h % 2 == 0:
                    return
                b = begin(f"nv{h // 2}")
                for hh in (h - 1, h):
                    r, t = DH * (hh % 2), PTn[hh % 2]
                    o = b[r:r + DH, :]
                    for br in range(2):
                        v = nkv[:, :, 256 * br + P + DH * g:256 * br + P + DH * g + DH]
                        nc.tensor.matmul(o[:, 0:256], v[:, 0, :], t[:, 384 * br:384 * br + 256], start=br == 0, stop=False)
                        nc.tensor.matmul(o[:, P:256], v[:, 1, :], t[:, 384 * br + 256:384 * br + 384], start=False, stop=False)
                    mm = nc.tensor.matmul(o[:, 0:256], vc[0:NCMP, DH * g:DH * g + DH], t[0:NCMP, 768:1024], start=False, stop=True)
                done(mm, f"nv{h // 2}")

            def project(name, wname, hT):
                w = slot3(wname, 4, D)
                for hh in range(2):
                    for j in range(2):
                        turned(f"{name}{hh}{j}", w, 512 * hh + 256 * j, hT, 4)

            nsa_scores(0)
            nsa_scores(1)
            was_read(pe, "mo0")
            was_read(pe, "mo1")
            project("pm", "wbm", hT_mem)
            for h in range(QH):
                nsa_turn(h)
                if h + 2 < QH:
                    nsa_scores(h + 2)
                if h == 0:
                    was_read(pe, "hmlT0")
                    was_read(pe, "hmlT1")
                    project("pl", "wbl", hT_ml)
                if h in (1, 2):
                    bgate("bgn", 0, h - 1)
                if h in (4, 5):
                    bgate("bgn", 1, h - 4)
                nsa_out(h)
            for j in range(4):
                was_read(pe, f"nv{j}")
            project("pn", "wbn", hT_nsa)

            pe.wait_ge(S("merged"), 8)
            mg = tiles(mergedT)

            def x1_turn(i, h):
                was_read(pe, f"wo{h}{i}")
                transposes(f"xT{i}{h}", [(P * k, x_sb[:, i, P * (4 * h + k):P * (4 * h + k) + P]) for k in range(4)])

            for hh in range(2):
                natural([(i, f"wo{hh}{i}") for i in range(NT)], slot3(f"wo{hh}", KT, 512), 512, src=mg)
            for h in range(2):
                for i in range(NT):
                    x1_turn(i, h)
            w = slot3("wr", KT, NE)
            for x in ("00", "10", "01", "11"):
                was_read(pe, f"xT{x}")
            b = begin("lT")
            for k in range(KT):
                g = k % 4
                mm = nc.tensor.matmul(b[32 * g:32 * g + 32, 0:SEQ], w[:, k, :], uT[:, k, :], start=k < 4, stop=k >= 4)
            done(mm, "lT")
            was_read(pe, "lT")
            b = begin("lg")
            for i in range(NT):
                mm = nc.tensor.matmul(b[:, NE * i:NE * i + NE], cp[:, P * i:P * i + P], C("sum4"), start=True, stop=True)
            done(mm, "lg")
            for name in JOBS[-len(TAIL) - NB:-len(TAIL)]:
                was_read(pe, name)
            for i in range(NT):
                for hh in range(2):
                    nc.tensor.matmul(ACC[i][hh][:, :], ident, x_sb[:, i, 512 * hh:512 * hh + 512],
                                     start=True, stop=False, skip_group_check=True)
            pe.wait_ge(S("sel_ready"), 1)
            b = begin("rank")
            nc.tensor.matmul(b[:, 0:NE], C("strict"), sel[:, 0, :], start=True, stop=True)
            nc.tensor.matmul(b[:, NE:2 * NE], ones, sel[:, 0, :], start=True, stop=False)
            nc.tensor.matmul(b[:, NE:2 * NE], C("strict"), sel[:, 1, :], start=False, stop=True)
            for i in range(NT):
                mm = nc.tensor.matmul(b[0:NE, 64:65], sel[:, i, :], ones[:, 0:1], start=i == 0, stop=i == NT - 1)
            done(mm, "rank")
            pe.wait_ge(S("rank_ready"), 1)
            transposes("rT", [(P * i, rank_it[:, i, 0:NE]) for i in range(NT)]
                       + [(256 + P * i, w_it[:, i, 0:NE]) for i in range(NT)])
            b = begin("first")
            nc.tensor.matmul(b[0:NE, 0:1], C("strict")[0:NE, 0:NE], nit, start=True, stop=True)
            nc.tensor.matmul(b[0:1, 32:64], nit, C("strict")[0:NE, 0:NE], start=True, stop=True)
            mm = nc.tensor.matmul(b[0:1, 64:65], nit, ones[0:NE, 0:1], start=True, stop=True)
            done(mm, "first")
            was_read(pe, "rT")
            pe.wait_ge(S("items_ready"), 1)
            b = begin("it")
            for i in range(NT):
                o = ITEMS * i
                nc.tensor.matmul(b[:, o:o + ITEMS], rTs[:, P * i:P * i + P], Eit, start=True, stop=False)
                nc.tensor.matmul(b[:, o:o + ITEMS], ones[0:NE, :], Ait, start=False, stop=True)
            for i in range(NT):
                o = ITEMS * (2 + i)
                nc.tensor.matmul(b[:, o:o + ITEMS], rTs[:, 256 + P * i:256 + P * i + P], Eit, start=True, stop=True)
            nc.tensor.matmul(b[0:1, 4 * ITEMS:5 * ITEMS], C("pcol")[0:NE, :], Eit, start=True, stop=True)
            mm = nc.tensor.matmul(b[0:1, 5 * ITEMS:6 * ITEMS], C("odd")[0:NE, :], Eit, start=True, stop=True)
            done(mm, "it")
            assert at[0] == len(JOBS)
            for name in TAIL[-4:]:
                was_read(pe, name)

            def gather():
                for half, b in ((1, BX), (0, BG)):
                    for c in range(4):
                        for i in range(NT):
                            o = P * (4 * half + c)
                            mm = nc.tensor.matmul(b[:, P * c:P * c + P], x2[:, i, o:o + P], Gm[:, i, :],
                                                  start=i == 0, stop=i == NT - 1)
                    mm.then_inc(S("g_full"), 1)

            def scatter(last=False):
                for t in range(NT):
                    for hh in range(2):
                        mm = nc.tensor.matmul(ACC[t][hh][:, :], STs[:, P * t:P * t + P],
                                              y_sb[:, 512 * hh:512 * hh + 512], start=False, stop=last, skip_group_check=True)
                    if last:
                        mm.then_inc(S("sum_ready"), 1)
                if not last:
                    mm.then_inc(S("scattered"), 1)

            def up(i, e, odd, par):
                def bias(row):
                    pe.wait_ge(brow_in[row], e * 8 + (8 if row else 16))
                    p = 32 + 32 * row
                    for b in range(2):
                        for hh in range(2):
                            o = 1024 * b + 512 * hh
                            mm = nc.tensor.matmul(BH[b][64 * hh:64 * hh + 64, :], ones[p:p + 1, 0:64], brow[row][:, o:o + 512],
                                                  start=True, stop=False, skip_group_check=True)
                    mm.then_inc(S("brow_used"), 1)

                def part(q, slot):
                    pe.wait_ge(w_full[slot], e * 8 + (8 if slot >= NSLOT else 16 * (TRUNK_TURNS + 1)))
                    w = ring[:, slot, :].rearrange("p (c n) -> p c n", c=2)
                    for c in range(2):
                        k = 2 * q + c
                        for b in range(2):
                            for hh in range(2):
                                o = 1024 * b + 512 * hh
                                mm = nc.tensor.matmul(BH[b][64 * hh:64 * hh + 64, :], xgT[:, k, 64 * par:64 * par + 64],
                                                      w[:, c, o:o + 512], start=False, stop=k == KT - 1,
                                                      skip_group_check=True)
                    mm.then_inc(S("gu_done"), 1)

                with pe.If(odd > 0):
                    bias(1)
                    for q in range(TWICE):
                        part(q, NSLOT + q)
                with pe.Else():
                    bias(0)
                    for q in range(TWICE):
                        part(q, q)

            def down(i, e):
                pe.wait_ge(S("act_ready"), i * 2 + 2)
                for q in range(4):
                    mm = nc.tensor.transpose(BX[:, P * q:P * q + P], act_sb[:, P * q:P * q + P], ident)
                mm.then_inc(S("a_full"), 1)
                pe.wait_ge(S("a_evac"), i + 1)
                for d in range(2):
                    pe.wait_ge(w_full[4 + d], e * 16 + 16 * (TRUNK_TURNS + 1))
                    w = ring[:, 4 + d, :].rearrange("p (c n) -> p c n", c=4)
                    for c in range(4):
                        k = 4 * d + c
                        o = P * (2 * (k // 4) + k % 2) + 64 * ((k // 2) % 2)
                        for hh in range(2):
                            mm = nc.tensor.matmul(BG[64 * hh:64 * hh + 64, :], actT[:, o:o + 64],
                                                  w[:, c, 512 * hh:512 * hh + 512],
                                                  start=k == 0, stop=k == KT - 1, skip_group_check=True)
                    mm.then_inc(S("down_done"), 1)

            def pair(j, final=False):
                e0, e1 = [pe.value_load(idx[0:1, bass.ds(j * 2 + (NE + par), 1)], min_val=0, max_val=NE - 1)
                          for par in range(2)]
                odd0, odd1 = [pe.value_load(idx[0:1, bass.ds(j * 2 + (NE + ITEMS + par), 1)], min_val=0, max_val=1)
                              for par in range(2)]
                pe.wait_ge(S("g_evac"), j * 2 + 2)
                pe.wait_ge(S("st_evac"), j + 1)
                up(j * 2, e0, odd0, 0)
                pe.wait_ge(S("y_evac"), j * 2 + 1)
                scatter()
                down(j * 2, e0)
                up(j * 2 + 1, e1, odd1, 1)
                pe.wait_ge(S("y_evac"), j * 2 + 2)
                if not final:
                    pe.wait_ge(S("G_ready"), j + 2)
                    gather()
                else:
                    pe.wait_ge(S("bdn_in"), 16)
                    for i in range(NT):
                        for hh in range(2):
                            nc.tensor.matmul(ACC[i][hh][:, :], rTs[:, 256 + P * i:256 + P * i + P],
                                             b_dn[:, 512 * hh:512 * hh + 512], start=False, stop=False, skip_group_check=True)
                pe.wait_ge(S("Gw_ready"), j + 1)
                pe.wait_ge(S("act_ready"), j * 4 + 4)
                for t in range(NT):
                    mm = nc.tensor.transpose(BH[0][:, P * t:P * t + P], Gw[:, t, :], ident)
                mm.then_inc(S("st_full"), 1)
                if not final:
                    pe.wait_ge(S("g_evac"), j * 2 + 4)
                down(j * 2 + 1, e1)

            pe.wait_ge(S("G_ready"), 1)
            pe.wait_ge(S("x2_ready"), 2)
            gather()
            pe.wait_ge(S("idx_ready"), 1)
            last_pair = pe.value_load(idx[0:1, NE + 2 * ITEMS:], min_val=NE // 2 - 1, max_val=ITEMS // 2 - 1)
            with pe.Fori(0, last_pair) as j:
                pair(j)
            pair(last_pair, final=True)
            pe.wait_ge(S("last_y"), 1)
            scatter(last=True)

        @block.scalar
        def _(act):
            def copy(job, dst, src):
                arrived(act, job)
                read(nc.scalar.activation(dst, src, ACT.Copy), job)

            for args in vec_rows[:5]:
                load_rows(act, *args)

            act.wait_ge(S("mem_in"), 16)
            for i in range(NT):
                nc.scalar.activation(uT[:, 0:4, :].rearrange("p k t -> p (k t)"), memn[:, i, :], ACT.Square,
                                     accum_out=st[:, i:i + 1]).then_inc(S("sumsq"), 1)
                act.wait_ge(S("sumsq"), i + 1)
            act.wait_ge(S("x_in"), 16)
            for i in range(NT):
                nc.scalar.activation(uT[:, 4:8, :].rearrange("p k t -> p (k t)"), x_sb[:, i, :], ACT.Square,
                                     accum_out=st[:, 2 + i:3 + i]).then_inc(S("sumsq"), 1)
                act.wait_ge(S("sumsq"), 3 + i)

            def copy_and_square(job, dst, sq):
                arrived(act, job)
                nc.scalar.activation(dst, bank(job)[:, :], ACT.Copy)
                read(nc.scalar.activation(sq, bank(job)[:, :], ACT.Square), job)

            for x in ("10", "11"):
                arrived(act, f"memT{x}")
            for i in range(NT):
                copy_and_square(f"mk{i}", mkv[:, i, 0:512], sqA[:, i, :])
            for i in range(NT):
                copy(f"mv{i}", mkv[:, i, 512:1024], bank(f"mv{i}")[:, :])
            for i in range(NT):
                copy_and_square(f"mq{i}", mqn[:, i, :], sqB[:, i, :])
            arrived(act, "uT11")
            act.wait_ge(S("pad_zero"), 1)
            for n in range(4):
                copy(f"qk{n}", pre[:, 2 * n:2 * n + 2, 3:3 + SEQ],
                     bank(f"qk{n}")[:, :].rearrange("p (j t) -> p j t", j=2))
            for i in range(NT):
                copy(f"mkT{i}", mkT[:, :, P * i:P * i + P], bank(f"mkT{i}")[:, :].rearrange("p (h t) -> p h t", h=4))
            for i in range(NT):
                copy(f"v{i}", vaug[:, i, :, 0:P], bank(f"v{i}")[:, :].rearrange("p (h t) -> p h t", h=4))
            for i in range(NT):
                copy(f"mqT{i}", mqT[:, :, P * i:P * i + P], bank(f"mqT{i}")[:, :].rearrange("p (h t) -> p h t", h=4))
            for n in range(2):
                act.wait_ge(S("conv_done"), 1)
                nc.scalar.activation(cp[:, 1024 * n:1024 * n + 1024], qk[:, 4 * n:4 * n + 4, :].rearrange("p j t -> p (j t)"),
                                     ACT.Sigmoid).then_inc(S("conv_sig"), 1)
            act.wait_ge(S("absf"), 1)
            nc.scalar.activation(r_B, r_B, ACT.Exp, scale=-1.0).then_inc(S("act_rows"), 1)
            act.wait_ge(S("act_rows"), 1)
            nc.scalar.activation(r_B, r_B, ACT.Ln, bias=1.0).then_inc(S("act_rows"), 1)

            def mem_exp(h):
                act.wait_ge(S("mem_nmax"), h + 1)
                if h >= 2:
                    arrived(act, f"mP{h - 2}")
                for i in range(NT):
                    ins = nc.scalar.activation(Pm[h % 2][:, i, :], bank(f"ms{h}")[:, 256 * i:256 * i + 256], ACT.Exp,
                                               bias=st[:, 32 + 2 * h + i:33 + 2 * h + i],
                                               accum_out=st[:, 40 + 2 * h + i:41 + 2 * h + i])
                read(ins, f"ms{h}")

            def mem_turned(h):
                copy(f"mP{h}", PTm[h % 2], bank(f"mP{h}")[:, :].rearrange("p (m t) -> p m t", m=2))

            act.wait_ge(S("mk_norm"), 1)
            act.wait_ge(S("mq_norm"), 1)
            mem_exp(0)
            mem_exp(1)
            for i in range(NT):
                arrived(act, f"o{i}")
                read(nc.scalar.activation(osig[:, i, :], bank(f"o{i}")[:, :], ACT.Sigmoid), f"o{i}")
            mem_turned(0)
            mem_exp(2)
            mem_turned(1)
            mem_exp(3)
            arrived(act, "mkT1")
            copy("mo0", heads[:, 0, 0:2, :], bank("mo0")[:, :].rearrange("p (h t) -> p h t", h=2))
            for i in range(NT):
                copy(f"nq{i}", nq_sb[:, i, :], bank(f"nq{i}")[:, :])
            arrived(act, "ngate")
            read(nc.scalar.activation(gsb[:, :, :].rearrange("p i n -> p (i n)"), bank("ngate")[:, 0:48], ACT.Sigmoid), "ngate")
            mem_turned(2)
            mem_turned(3)
            copy("mo1", heads[:, 1, 0:2, :], bank("mo1")[:, :].rearrange("p (h t) -> p h t", h=2))

            def gate(name, dst, hh, j):
                job = f"{name}{hh}{j}"
                arrived(act, job)
                o = 1024 * hh + 512 * j
                read(nc.scalar.activation(dst[:, o:o + 512], bank(job)[:, :], ACT.Sigmoid), job)

            def ml_exp(h):
                was_read(act, f"MB{h}")
                nc.scalar.activation(Dt, Dt, ACT.Exp, scale=-1.0).then_inc(S("ml_exp"), 1)

            def ml_num(h):
                copy(f"num{h}", num[:, h], bank(f"num{h}")[:, :].rearrange("p (i e) -> p i e", i=2)[:, :, 0:129])

            was_read(act, "gT")
            nc.scalar.activation(st[:, 64:72], st[:, 56:64], ACT.Exp).then_inc(S("expm"), 1)
            ml_exp(0)
            gate("bgm", bg0, 0, 0)
            ml_exp(1)
            ml_num(0)
            gate("bgm", bg0, 0, 1)
            ml_exp(2)
            ml_num(1)
            gate("bgm", bg0, 1, 0)
            ml_exp(3)
            ml_num(2)
            gate("bgm", bg0, 1, 1)
            ml_num(3)
            act.wait_ge(S("h_div"), 1)
            nc.scalar.activation(sp_[:, 0:1024], hml.rearrange("p i h e -> p (i h e)"), ACT.Square).then_inc(S("h_sq"), 1)
            for i in range(NT):
                copy(f"nkv{i}", nkv[:, i, :], bank(f"nkv{i}")[:, :])
            act.wait_ge(S("hml_ready"), 1)
            arrived(act, "kcvc")
            for n in range(2):
                for g in range(2):
                    s = bank("kcvc")[DH * g:DH * g + DH, 256 * n:256 * n + 256]
                    nc.scalar.activation(k2[0:DH, n, g, :], s, ACT.Copy)
                    ins = nc.scalar.activation(k2[DH:P, n, g, 0:255], s[:, 1:256], ACT.Copy)
            read(ins, "kcvc")
            arrived(act, "mo1")
            for i in range(NT):
                copy(f"nqT{i}", qT[:, :, P * i:P * i + P], bank(f"nqT{i}")[:, :].rearrange("p (h t) -> p h t", h=4))
            for i in range(NT):
                copy(f"hmlT{i}", nqr[:, :].rearrange("p (h t) -> p h t", h=4)[:, :, P * i:P * i + P], bank(f"hmlT{i}")[:, :].rearrange("p (h t) -> p h t", h=4))
            for n, job in enumerate(("hk", "hv")):
                copy(job, hidp[:, n, :], bank(job)[:, 0:CMP_HID])
            gate("bgl", bg1, 0, 0)
            for n, job in enumerate(("hkT", "hvT")):
                arrived(act, job)
                for f in range(2):
                    s = bank(job)[:, 32 * f:32 * f + 30]
                    col = vcol[:, 56 + 2 * n + f:57 + 2 * n + f]
                    nc.scalar.activation(hid[:, n, f, :], s, ACT.Identity, bias=col)
                    ins = nc.scalar.activation(hsg[:, n, f, :], s, ACT.Sigmoid, bias=col)
                read(ins, job)
            gate("bgl", bg1, 0, 1)
            for i in range(NT):
                copy(f"nkT{i}", kT[:, :, P * i:P * i + P], bank(f"nkT{i}")[:, :].rearrange("p (h t) -> p h t", h=4))
            copy("vc", vc[0:NCMP, :], bank("vc")[0:NCMP, 0:128])
            gate("bgl", bg1, 1, 0)
            gate("bgl", bg1, 1, 1)
            copy("kcT", kcT, bank("kcT")[:, 0:30])

            def nsa_exp(h):
                act.wait_ge(S("nsa_nmax"), h + 1)
                s, o = Sn[h % 2], 80 + 16 * (h % 2)
                segs = [(768 + NCMP * i, NCMP, 3 * i) for i in range(2)]
                segs += [(512 + P * br, P, 1 + br) for br in range(2)] + [(256 * br, 256, 4 + br) for br in range(2)]
                for a, n, c in segs:
                    ins = nc.scalar.activation(s[:, a:a + n], s[:, a:a + n], ACT.Exp, bias=st[:, o + c:o + c + 1],
                                               accum_out=st[:, o + 8 + c:o + 9 + c])
                ins.then_inc(S("nsa_exp"), 1)

            def nsa_turned(h):
                if h >= 2:
                    arrived(act, f"nv{h // 2 - 1}")
                for br, job in enumerate((f"tA{h}", f"tB{h}")):
                    arrived(act, job)
                    nc.scalar.activation(PTn[h % 2][:, 384 * br:384 * br + 384], bank(job)[:, 0:384], ACT.Copy)
                    read(nc.scalar.activation(PTn[h % 2][0:NCMP, 768 + P * br:768 + P * br + P],
                                              bank(job)[0:NCMP, 384:512], ACT.Copy), job)

            nsa_exp(0)
            nsa_exp(1)
            for h in range(QH):
                nsa_turned(h)
                if h + 2 < QH:
                    nsa_exp(h + 2)
                if h in (1, 2):
                    was_read(act, "pm11")
                    gate("bgn", bg0, 0, h - 1)
                if h in (4, 5):
                    gate("bgn", bg0, 1, h - 4)
                if h % 2 == 1:
                    copy(f"nv{h // 2}", hT_nsa[h // 2], bank(f"nv{h // 2}")[:, 0:256])
            for i in range(NT):
                was_read(act, f"wo1{i}")
                nc.scalar.activation(cp[:, 1024:2048], x_sb[:, i, :], ACT.Square,
                                     accum_out=st[:, 4 + i:5 + i]).then_inc(S("sumsq"), 1)
                act.wait_ge(S("sumsq"), 5 + i)
            copy("lT", cp[:, 0:SEQ], bank("lT")[:, 0:SEQ])
            act.wait_ge(S("lg_ready"), 1)
            for i in range(NT):
                ins = nc.scalar.activation(lg[:, i, :], lg[:, i, :], ACT.Exp, bias=st[:, 120 + i:121 + i])
            ins.then_inc(S("lg_exp"), 1)

            def tokens(n):
                for k, (half, b) in enumerate(((1, BX), (0, BG))):
                    act.wait_ge(S("g_full"), n + (k + 1))
                    nc.scalar.activation(xgT[:, 4 * half:4 * half + 4, :].rearrange("p c n -> p (c n)"), b[:, :],
                                         ACT.Copy).then_inc(S("g_evac"), 1)

            def gates(i):
                for b in range(2):
                    act.wait_ge(S("g_clip"), i * 2 + (b + 1))
                    nc.scalar.activation(sg[b], gt[b], ACT.Sigmoid, scale=ALPHA).then_inc(S("g_sig"), 1)

            def results(i, par):
                act.wait_ge(S("a_full"), i + 1)
                nc.scalar.activation(actT, BX[:, :], ACT.Copy).then_inc(S("a_evac"), 1)
                act.wait_ge(S("down_done"), i * 2 + 2)
                nc.scalar.activation(y_sb[64 * par:64 * par + 64, 0:512], BG[0:64, :], ACT.Copy)
                nc.scalar.activation(y_sb[64 * par:64 * par + 64, 512:1024], BG[64:P, :], ACT.Copy).then_inc(S("y_evac"), 1)

            def pair(j, final=False):
                gates(j * 2)
                act.wait_ge(S("scattered"), j + 1)
                results(j * 2, 0)
                gates(j * 2 + 1)
                if not final:
                    tokens(j * 2 + 2)
                act.wait_ge(S("st_full"), j + 1)
                nc.scalar.activation(STs, BH[0][:, 0:256], ACT.Copy).then_inc(S("st_evac"), 1)
                results(j * 2 + 1, 1)

            arrived(act, "nv3")
            nc.scalar.activation(STs, C("ones")[:, 0:1].to_broadcast([P, 256]), ACT.Copy, scale=0.0).then_inc(S("st_evac"), 1)
            nc.scalar.activation(y_sb, C("ones")[:, 0:1].to_broadcast([P, 1024]), ACT.Copy, scale=0.0).then_inc(S("y_evac"), 1)
            tokens(0)
            act.wait_ge(S("idx_ready"), 1)
            last_pair = act.value_load(idx[0:1, NE + 2 * ITEMS:], min_val=NE // 2 - 1, max_val=ITEMS // 2 - 1)
            with act.Fori(0, last_pair) as j:
                pair(j)
            pair(last_pair, final=True)
            nc.scalar.activation(sg[0][:, 0:1], sg[0][:, 1:2], ACT.Copy).then_inc(S("last_y"), 1)
            act.wait_ge(S("last_y"), 1)
            for t in range(NT):
                act.wait_ge(S("sum_ready"), t + 1)
                nc.scalar.activation(x2[:, t, 512:1024], ACC[t][1][:, :], ACT.Copy).then_inc(S("out_right"), 1)
                act.wait_ge(S("out_right"), t + 1)
                act.dma_start(out_t[:, t, 512:1024], x2[:, t, 512:1024]).then_inc(S("out_done"), 16)

        @block.vector
        def _(dve):
            V = nc.vector
            counts = {}

            def step(ins, name="dve"):
                counts[name] = counts.get(name, 0) + 1
                ins.then_inc(S(name), 1)
                dve.wait_ge(S(name), counts[name])

            def step_read(ins, job):
                read(ins, job)
                was_read(dve, job)

            def rstd(dst, src, n):
                step(V.tensor_scalar(dst, src, 1.0 / n, EPS, ALU.mult, ALU.add), "mean_ready")
                dve.wait_ge(S("rstd_done"), counts["mean_ready"])

            step(V.memset(rank_it[:, :, ITEMS:], UNSEL))
            step(V.memset(vaug[:, :, :, P:P + 1], 1.0), "ones_col")
            for i in range(NT):
                dve.wait_ge(S("sumsq"), i + 1)
                rstd(st[:, 8 + i:9 + i], st[:, i:i + 1], D)
                step(V.tensor_scalar(memn[:, i, :], memn[:, i, :], st[:, 8 + i:9 + i], None, ALU.mult), "mem_norm")
            for i in range(NT):
                dve.wait_ge(S("sumsq"), 3 + i)
                rstd(st[:, 10 + i:11 + i], st[:, 2 + i:3 + i], D)
                step(V.tensor_scalar(un[:, i, :], x_sb[:, i, :], st[:, 10 + i:11 + i], None, ALU.mult), "x_norm")
            arrived(dve, "vecT")
            step_read(V.tensor_copy(vcol[:, :], bank("vecT")[:, 0:VROWS]), "vecT")
            for name, dst, g0 in (("memT", memT, 8), ("uT", uT, 0)):
                for i in range(NT):
                    for h in range(2):
                        job = f"{name}{i}{h}"
                        arrived(dve, job)
                        read(V.tensor_tensor(dst[:, 4 * h:4 * h + 4, P * i:P * i + P],
                                             bank(job)[:, :].rearrange("p (k t) -> p k t", k=4),
                                             last(vcol[:, g0 + 4 * h:g0 + 4 * h + 4], P), ALU.mult), job)
            dve.wait_ge(S("cst_in"), 16)
            dve.wait_ge(S("bc_in"), 16 * 6)
            step(V.tensor_scalar(g_q, g_q, DH ** -0.5, None, ALU.mult))
            step(V.tensor_scalar(g_mq, g_mq, DH_MEM ** -0.5, None, ALU.mult))
            arrived(dve, "uT11")
            step(V.memset(pre[:, :, 0:3], 0.0), "pad_zero")

            def head_norm(x, ss, g, hd, sq, nh):
                step(V.tensor_reduce(ss, sq, AX.X, ALU.add))
                rstd(ss, ss, hd)
                step(V.tensor_tensor(x, x, last(ss, hd), ALU.mult))
                return V.tensor_tensor(x, x, mid(g, nh), ALU.mult)

            for name, x, sq, g, o in (("mk", mkv[:, :, 0:512], sqA, g_mk, 16), ("mq", mqn, sqB, g_mq, 24)):
                for i in range(NT):
                    was_read(dve, f"{name}{i}")
                for i in range(NT):
                    ins = head_norm(x[:, i, :].rearrange("p (h e) -> p h e", h=4), st[:, o + 4 * i:o + 4 * i + 4], g, DH_MEM,
                                    sq[:, i, :].rearrange("p (h e) -> p h e", h=4), 4)
                    step(ins, f"{name}_norm" if i == NT - 1 else "dve")
            for n in range(2):
                for j in range(4 * n, 4 * n + 4):
                    was_read(dve, f"qk{j // 2}")
                    step(V.tensor_scalar(qk[:, j, :], pre[:, j, 0:SEQ], vcol[:, 16 + j:17 + j], vcol[:, 48 + j:49 + j],
                                         ALU.mult, ALU.add))
                    for a in range(1, CONV):
                        col = vcol[:, 16 + 8 * a + j:17 + 8 * a + j]
                        ins = V.scalar_tensor_tensor(out=qk[:, j, :], in0=pre[:, j, a:a + SEQ], scalar=col, in1=qk[:, j, :],
                                                     op0=ALU.mult, op1=ALU.add)
                        step(ins, "conv_done" if (j, a) == (7, CONV - 1) else "dve")
            arrived(dve, "gif")
            step(V.tensor_scalar(r_f, bank("gif")[0:4, 256:512], bif[:, 1:2], None, ALU.add))
            step(V.scalar_tensor_tensor(out=r_B, in0=r_f, scalar=-1.0, in1=r_f, op0=ALU.mult, op1=ALU.max), "absf")
            for n in range(2):
                dve.wait_ge(S("conv_sig"), n + 1)
                q = qk[:, 4 * n:4 * n + 4, :].rearrange("p j t -> p (j t)")
                step(V.tensor_tensor(q, q, cp[:, 1024 * n:1024 * n + 1024], ALU.mult), "qk_ready")
            dve.wait_ge(S("act_rows"), 2)
            step(V.scalar_tensor_tensor(out=r_f, in0=r_f, scalar=0.0, in1=r_B, op0=ALU.min, op1=ALU.subtract))
            step(V.memset(r_M, 1.0))
            step(V.tensor_tensor_scan(r_B, r_M, r_f, 0.0, ALU.mult, ALU.add))
            step_read(V.scalar_tensor_tensor(out=r_g, in0=bank("gif")[0:4, 0:256], scalar=bif[:, 0:1], in1=r_B,
                                             op0=ALU.add, op1=ALU.subtract), "gif")
            step(V.memset(r_f, 0.0))
            step(V.tensor_tensor_scan(r_M, r_f, r_g, 0.0, ALU.add, ALU.max))
            step(V.scalar_tensor_tensor(out=r_nm, in0=r_B, scalar=-1.0, in1=r_M, op0=ALU.mult, op1=ALU.subtract), "rows_ready")

            def mem_max(h):
                arrived(dve, f"ms{h}")
                c = st[:, 32 + 2 * h:34 + 2 * h]
                step(V.tensor_reduce(c, bank(f"ms{h}")[:, :].rearrange("p (i m) -> p i m", i=2), AX.X, ALU.max))
                step(V.tensor_scalar(c, c, -1.0, None, ALU.mult), "mem_nmax")

            def mem_norm(h):
                was_read(dve, f"ms{h}")
                c = st[:, 40 + 2 * h:42 + 2 * h]
                step(V.reciprocal(c, c))
                step(V.tensor_tensor(Pm[h % 2], Pm[h % 2], last(c, 256), ALU.mult), "memP")

            mem_max(0)
            mem_max(1)
            mem_norm(0)
            arrived(dve, "gT")
            step(V.tensor_copy(st[:, 48:64], bank("gT")[:, 0:16]))
            step_read(V.tensor_copy(st[:, 72:80], bank("gT")[:, 0:8]), "gT")
            mem_max(2)
            mem_norm(1)
            mem_max(3)
            mem_norm(2)
            mem_norm(3)

            def rope(dst, src, cos, sin, nh):
                pr = src.shape[0]
                c, s = mid(cos[0:pr], nh), mid(sin[0:pr], nh)
                a = tmp[0:pr, 0:32 * nh].rearrange("p (h d) -> p h d", h=nh)
                b = tmp[0:pr, 256:256 + 32 * nh].rearrange("p (h d) -> p h d", h=nh)
                lo, hi = src[:, :, 0:32], src[:, :, 32:64]
                V.tensor_tensor(a, lo, c, ALU.mult)
                step(V.tensor_tensor(b, hi, s, ALU.mult))
                for d in dst:
                    ins = V.tensor_tensor(d[:, :, 0:32], a, b, ALU.subtract)
                step(ins)
                V.tensor_tensor(a, hi, c, ALU.mult)
                step(V.tensor_tensor(b, lo, s, ALU.mult))
                for d in dst:
                    ins = V.tensor_tensor(d[:, :, 32:64], a, b, ALU.add)
                return ins

            for i in range(NT):
                was_read(dve, f"nq{i}")
                q = nq_sb[:, i, :].rearrange("p (h e) -> p h e", h=QH)
                sq = qr[:, i, :].rearrange("p (h e) -> p h e", h=QH)
                step(V.tensor_tensor(sq, q, q, ALU.mult))
                step(head_norm(q, st[:, 128 + 8 * i:136 + 8 * i], g_q, DH, sq, QH))
                step(rope([sq], q, C(f"cos{i}"), C(f"sin{i}"), QH), "q_roped" if i == NT - 1 else "dve")

            arrived(dve, "mo1")
            was_read(dve, "mP3")
            for h in range(NH_ML):
                arrived(dve, f"MB{h}")
                V.tensor_scalar(Dt[:, 0:256], bank(f"MB{h}")[:, 0:256], st[:, 72 + h:73 + h], 0.0, ALU.subtract, ALU.max)
                step_read(V.tensor_scalar(Dt[:, 256:384], bank(f"MB{h}")[:, P:256], st[:, 76 + h:77 + h], 0.0,
                                          ALU.subtract, ALU.max), f"MB{h}")
                arrived(dve, f"ST{h}")
                dve.wait_ge(S("ml_exp"), h + 1)
                if h >= 2:
                    arrived(dve, f"num{h - 2}")
                w = wd[h % 2]
                step_read(V.scalar_tensor_tensor(out=w, in0=bank(f"ST{h}")[:, 0:384], scalar=DH_ML ** -0.5, in1=Dt,
                                                 op0=ALU.mult, op1=ALU.mult), f"ST{h}")
                V.tensor_tensor(w[:, 0:P], w[:, 0:P], C("upper"), ALU.mult)
                step(V.tensor_tensor(w[:, 256:384], w[:, 256:384], C("upper"), ALU.mult), "wd_ready")
            for h in range(NH_ML):
                was_read(dve, f"num{h}")
            dve.wait_ge(S("expm"), 1)
            den = st[:, 160:168].rearrange("p (i h) -> p i h", i=NT)
            nd = num[:, :, :, P].rearrange("p h i -> p i h")
            step(V.scalar_tensor_tensor(out=den, in0=nd, scalar=-1.0, in1=nd, op0=ALU.mult, op1=ALU.max))
            step(V.tensor_tensor(st[:, 160:168], st[:, 160:168], st[:, 64:72], ALU.max))
            step(V.reciprocal(st[:, 160:168], st[:, 160:168]))
            for i in range(NT):
                ins = V.tensor_tensor(hml[:, i], num[:, :, i, 0:P], last(st[:, 160 + 4 * i:164 + 4 * i], P), ALU.mult)
            step(ins, "h_div")
            dve.wait_ge(S("h_sq"), 1)
            hv = hml.rearrange("p i h e -> p (i h) e")
            step(V.tensor_reduce(st[:, 168:176], sp_[:, 0:1024].rearrange("p (a e) -> p a e", e=P), AX.X, ALU.add))
            rstd(st[:, 168:176], st[:, 168:176], DH_ML)
            step(V.tensor_tensor(hv, hv, last(st[:, 168:176], P), ALU.mult))
            h2 = hml.rearrange("p i h e -> p i (h e)")
            step(V.tensor_tensor(h2, h2, mid(g_ml, NT), ALU.mult))
            was_read(dve, "o1")
            step(V.tensor_tensor(h2, h2, osig, ALU.mult), "hml_ready")

            step(V.memset(blk[:, :, :, 2 * NCMP:], 0.0))
            was_read(dve, "kcvc")
            for n in range(2):
                for g in range(2):
                    src = k2[:, n, g, :]
                    src = bass.AP(src.tensor, src.offset, [list(src.ap[0]), [2, 16], [16, NCMP]])
                    pos = last(vcol[:, 60 + 16 * n:76 + 16 * n], NCMP)
                    step(V.tensor_tensor(blk[:, n, :, NCMP * g:NCMP * g + NCMP], src, pos, ALU.add), "blk_ready")

            for i in range(NT):
                was_read(dve, f"nkv{i}")
                for br in range(2):
                    k = nkv[:, i, 256 * br:256 * br + P].rearrange("p (g e) -> p g e", g=KVH)
                    sq = ksq[:, 0:P].rearrange("p (g e) -> p g e", g=KVH)
                    step(V.tensor_tensor(sq, k, k, ALU.mult))
                    o = 144 + 2 * (2 * i + br)
                    step(head_norm(k, st[:, o:o + 2], g_k[:, DH * (1 + br):DH * (2 + br)], DH, sq, KVH))
                    ins = rope([kr[:, i, br, :, u, :] for u in range(2)], k, C(f"cos{i}"), C(f"sin{i}"), KVH)
                    step(ins, "k_roped" if (i, br) == (1, 1) else "dve")
            for n, job in enumerate(("hkT", "hvT")):
                was_read(dve, job)
                step(V.tensor_tensor(hid[:, n], hid[:, n], hsg[:, n], ALU.mult), "hid_ready")
            arrived(dve, "kc")
            kn = ksq[0:30, 128:192].unsqueeze(1)
            step_read(V.tensor_copy(ksq[0:30, 128:192], bank("kc")[0:30, 0:DH]), "kc")
            ksq1 = ksq[0:30, 192:256].unsqueeze(1)
            step(V.tensor_tensor(ksq1, kn, kn, ALU.mult))
            step(head_norm(kn, st[0:30, 152:153], g_k[0:30, 0:DH], DH, ksq1, 1))
            step(rope([kcn[0:30, DH * u:DH * u + DH].unsqueeze(1) for u in range(2)], kn, C("cosc"), C("sinc"), 1), "kc_roped")

            def merge(name, gates, first):
                for n in range(4):
                    job = f"{name}{n // 2}{n % 2}"
                    arrived(dve, job)
                    m, g = mT[:, 512 * n:512 * n + 512], gates[:, 512 * n:512 * n + 512]
                    if first:
                        step_read(V.tensor_tensor(m, bank(job)[:, :], g, ALU.mult), job)
                    else:
                        step_read(V.tensor_tensor(g, bank(job)[:, :], g, ALU.mult), job)
                        step(V.tensor_tensor(m, m, g, ALU.add), "merged")

            def nsa_mask(h):
                s, o = Sn[h % 2], 80 + 16 * (h % 2)
                if h >= 2:
                    arrived(dve, f"tB{h - 2}")
                arrived(dve, f"sA{h}")
                s1 = s[:, 0:512].rearrange("p (b m) -> p b m", b=2)
                s0 = s[:, 512:768].rearrange("p (b m) -> p b m", b=2)
                sc_ = s[:, 768:798]
                step_read(V.tensor_tensor(s1, bank(f"sA{h}")[:, :].rearrange("p (b m) -> p b m", b=2),
                                          mid(C("mask256"), 2), ALU.add), f"sA{h}")
                arrived(dve, f"sB{h}")
                V.tensor_tensor(s0, bank(f"sB{h}")[:, 0:256].rearrange("p (b m) -> p b m", b=2),
                                mid(C("mask256")[:, P:256], 2), ALU.add)
                step_read(V.tensor_tensor(sc_, bank(f"sB{h}")[:, 256:286], C("cmpadd"), ALU.add), f"sB{h}")
                V.tensor_reduce(st[:, o + 4:o + 6], s1, AX.X, ALU.max)
                V.tensor_reduce(st[:, o + 1:o + 3], s0, AX.X, ALU.max)
                step(V.tensor_reduce(st[:, o:o + 6].rearrange("p (i b) -> p i b", i=2)[:, :, 0],
                                     sc_.rearrange("p (i n) -> p i n", i=2), AX.X, ALU.max))
                step(V.tensor_scalar(st[:, o:o + 6], st[:, o:o + 6], -1.0, None, ALU.mult), "nsa_nmax")

            def nsa_weights(h):
                s, o = Sn[h % 2], 88 + 16 * (h % 2)
                dve.wait_ge(S("nsa_exp"), h + 1)
                sc_ = s[:, 768:798]
                step(V.tensor_tensor(sc_, sc_, C("cmp01"), ALU.mult))
                c3 = st[:, o:o + 6].rearrange("p (i b) -> p i b", i=2)
                step(V.tensor_reduce(c3[:, :, 0], sc_.rearrange("p (i n) -> p i n", i=2), AX.X, ALU.add))
                step(V.tensor_scalar(st[:, o:o + 6], st[:, o:o + 6], 1e-30, None, ALU.max))
                step(V.reciprocal(st[:, o:o + 6], st[:, o:o + 6]))
                step(V.tensor_tensor(c3, c3, gsb[:, :, 3 * h:3 * h + 3], ALU.mult))
                s1 = s[:, 0:512].rearrange("p (b m) -> p b m", b=2)
                s0 = s[:, 512:768].rearrange("p (b m) -> p b m", b=2)
                sc2 = sc_.rearrange("p (i n) -> p i n", i=2)
                V.tensor_tensor(s1, s1, last(st[:, o + 4:o + 6], 256), ALU.mult)
                V.tensor_tensor(s0, s0, last(st[:, o + 1:o + 3], P), ALU.mult)
                step(V.tensor_tensor(sc2, sc2, c3[:, :, 0].unsqueeze(2).to_broadcast([P, 2, NCMP]), ALU.mult), "nsaP")

            arrived(dve, "hmlT1")
            was_read(dve, "ngate")
            nsa_mask(0)
            nsa_mask(1)
            nsa_weights(0)
            was_read(dve, "bgm11")
            merge("pm", bg0, True)
            for h in range(QH):
                if h + 2 < QH:
                    nsa_mask(h + 2)
                if h == 0:
                    was_read(dve, "bgl11")
                    nsa_weights(1)
                    merge("pl", bg1, False)
                elif h + 1 < QH:
                    nsa_weights(h + 1)
            was_read(dve, "bgn11")
            merge("pn", bg0, False)
            for hh in range(2):
                for i in range(NT):
                    job = f"wo{hh}{i}"
                    arrived(dve, job)
                    xs = x_sb[:, i, 512 * hh:512 * hh + 512]
                    step_read(V.tensor_tensor(xs, xs, bank(job)[:, :], ALU.add), job)
            for h in range(2):
                for i in range(NT):
                    job = f"xT{i}{h}"
                    arrived(dve, job)
                    read(V.tensor_tensor(uT[:, 4 * h:4 * h + 4, P * i:P * i + P],
                                         bank(job)[:, :].rearrange("p (k t) -> p k t", k=4),
                                         last(vcol[:, 92 + 4 * h:96 + 4 * h], P), ALU.mult), job)
            for i in range(NT):
                dve.wait_ge(S("sumsq"), 5 + i)
                rstd(st[:, 12 + i:13 + i], st[:, 4 + i:5 + i], D)

            arrived(dve, "lg")
            for i in range(NT):
                ins = V.scalar_tensor_tensor(out=lg[:, i, :], in0=bank("lg")[:, NE * i:NE * i + NE], scalar=st[:, 12 + i:13 + i],
                                             in1=b_r, op0=ALU.mult, op1=ALU.add)
            step_read(ins, "lg")
            for i in range(NT):
                ins = V.max(top[:, i, :], lg[:, i, :])
            step(ins)
            for i in range(NT):
                V.tensor_scalar(sel[:, i, :], lg[:, i, :], top[:, i, TOPK - 1:TOPK], None, ALU.is_gt)
                ins = V.tensor_scalar(eqv[:, i, :], lg[:, i, :], top[:, i, TOPK - 1:TOPK], None, ALU.is_equal)
            step(ins)
            step(V.tensor_scalar(st[:, 120:122], top[:, :, 0], -1.0, None, ALU.mult), "lg_ready")
            step(V.tensor_reduce(ngt, sel, AX.X, ALU.add))
            step(V.tensor_scalar(ngt, ngt, -1.0, float(TOPK), ALU.mult, ALU.add))
            for i in range(NT):
                ins = V.tensor_tensor_scan(cum[:, i, :], ones[:, 0:NE], eqv[:, i, :], 0.0, ALU.mult, ALU.add)
            step(ins)
            for i in range(NT):
                ins = V.scalar_tensor_tensor(out=cum[:, i, :], in0=cum[:, i, :], scalar=ngt[:, i:i + 1], in1=eqv[:, i, :],
                                             op0=ALU.is_le, op1=ALU.mult)
            step(ins)
            step(V.tensor_tensor(sel, sel, cum, ALU.add), "sel_ready")
            dve.wait_ge(S("lg_exp"), 1)
            wts = w_it[:, :, 0:NE]
            step(V.tensor_tensor(wts, lg, sel, ALU.mult))
            step(V.tensor_reduce(st[:, 122:124], wts, AX.X, ALU.add))
            step(V.reciprocal(st[:, 122:124], st[:, 122:124]))
            step(V.tensor_tensor(wts, wts, last(st[:, 122:124], NE), ALU.mult))
            arrived(dve, "rank")
            rk = rank_it[:, :, 0:NE]
            step(V.scalar_tensor_tensor(out=rk, in0=bank("rank")[:, 0:64].rearrange("p (i e) -> p i e", i=2), scalar=-UNSEL,
                                        in1=sel, op0=ALU.add, op1=ALU.mult))
            step(V.tensor_scalar(rk, rk, UNSEL, None, ALU.add))
            for n in range(3):
                ins = V.tensor_scalar(cntc[:, n:n + 1], bank("rank")[0:NE, 64:65], float(SLOT_TOK * (n + 1)), None, ALU.is_gt)
            step_read(ins, "rank")
            step(V.tensor_reduce(nit, cntc, AX.X, ALU.add))
            step(V.tensor_scalar(nit, nit, 1.0, None, ALU.add), "rank_ready")
            dve.wait_ge(S("gffn_in"), 16)

            def norm_row(i):
                step(V.scalar_tensor_tensor(out=x2[:, i, :], in0=x_sb[:, i, :], scalar=st[:, 12 + i:13 + i], in1=g_ffn,
                                            op0=ALU.mult, op1=ALU.mult), "x2_ready")

            norm_row(0)
            arrived(dve, "rT")
            step_read(V.tensor_copy(rTs, bank("rT")[0:NE, :]), "rT")
            arrived(dve, "first")
            step(V.tensor_copy(first, bank("first")[0:NE, 0:1]))
            step(V.tensor_tensor(end, first, nit, ALU.add))
            k = C("iota")[0:NE, 0:ITEMS]
            step(V.tensor_scalar(Eit, k, first, None, ALU.is_ge))
            step(V.scalar_tensor_tensor(out=Eit, in0=k, scalar=end, in1=Eit, op0=ALU.is_lt, op1=ALU.mult))
            step(V.tensor_scalar(Ait, k, first, -float(SLOT_TOK), ALU.subtract, ALU.mult))
            step(V.tensor_tensor(Ait, Ait, Eit, ALU.mult), "items_ready")
            step(V.tensor_scalar(few, C("iota")[0:1, 2:ITEMS].rearrange("p (k two) -> p k two", two=2)[:, :, 0],
                                 bank("first")[0:1, 64:65], None, ALU.is_lt))
            step_read(V.tensor_scalar(before, bank("first")[0:1, 32:64], -1.0, None, ALU.add), "first")
            step(V.tensor_copy(idx[0:1, 0:NE], before))
            step(V.tensor_reduce(nlast, few, AX.X, ALU.add))
            step(V.tensor_copy(idx[0:1, NE + 2 * ITEMS:], nlast))
            norm_row(1)
            arrived(dve, "it")
            step(V.tensor_copy(rank_it[:, :, 0:ITEMS], bank("it")[:, 0:2 * ITEMS].rearrange("p (i k) -> p i k", i=2)))
            step(V.tensor_copy(idx[0:1, NE:NE + 2 * ITEMS], bank("it")[0:1, 4 * ITEMS:6 * ITEMS]), "idx_ready")
            step_read(V.tensor_copy(w_it[:, :, :], bank("it")[:, 2 * ITEMS:4 * ITEMS].rearrange("p (i k) -> p i k", i=2)), "it")

            def onehot(j):
                for t in range(NT):
                    for p in range(2):
                        ins = V.tensor_scalar(Gm[:, t, 64 * p:64 * p + 64], C("iota")[:, 0:64],
                                              rank_it[:, t, bass.ds(j * 2 + p, 1)], None, ALU.is_equal)
                ins.then_inc(S("G_ready"), 1)

            def activate(i):
                dve.wait_ge(S("gu_done"), i * 4 + 4)
                for b in range(2):
                    h = BH[b][:, :].rearrange("p (f two) -> p f two", two=2)
                    V.tensor_scalar(gt[b], h[:, :, 0], LIMIT, None, ALU.min).then_inc(S("g_clip"), 1)
                    V.tensor_scalar(ut[b], h[:, :, 1], -LIMIT, LIMIT, ALU.max, ALU.min).then_inc(S("u_clip"), 1)
                for b in range(2):
                    dve.wait_ge(S("g_sig"), i * 2 + (b + 1))
                    V.tensor_tensor(gt[b], gt[b], sg[b], ALU.mult).then_inc(S("gs_done"), 1)
                dve.wait_ge(S("u_clip"), i * 2 + 2)
                dve.wait_ge(S("gs_done"), i * 2 + 2)
                for b in range(2):
                    V.scalar_tensor_tensor(out=ut[b], in0=ut[b], scalar=1.0, in1=gt[b],
                                           op0=ALU.add, op1=ALU.mult).then_inc(S("act_ready"), 1)

            def pair(j):
                dve.wait_ge(S("gu_done"), j * 8 + 1)
                for t in range(NT):
                    for p in range(2):
                        o = j * 2 + p
                        ins = V.tensor_scalar(Gw[:, t, 64 * p:64 * p + 64], C("iota")[:, 0:64], rank_it[:, t, bass.ds(o, 1)],
                                              w_it[:, t, bass.ds(o, 1)], ALU.is_equal, ALU.mult)
                ins.then_inc(S("Gw_ready"), 1)
                onehot(j + 1)
                activate(j * 2)
                activate(j * 2 + 1)

            onehot(0)
            dve.wait_ge(S("idx_ready"), 1)
            last_pair = dve.value_load(idx[0:1, NE + 2 * ITEMS:], min_val=NE // 2 - 1, max_val=ITEMS // 2 - 1)
            with dve.Fori(0, last_pair + 1) as j:
                pair(j)
            for t in range(NT):
                dve.wait_ge(S("sum_ready"), t + 1)
                V.tensor_copy(x2[:, t, 0:512], ACC[t][0][:, :]).then_inc(S("out_left"), 1)


_INS = ["x", "mem", "g_mix", "w_in", "ml_conv_w", "ml_conv_b", "ml_b_i", "ml_b_f", "ml_g_out", "nsa_g_q", "nsa_g_k",
        "cmp_pos_k", "cmp_w1_k", "cmp_b1_k", "cmp_w2_k", "cmp_pos_v", "cmp_w1_v", "cmp_b1_v", "cmp_w2_v", "g_mem",
        "w_mem_kv", "mem_g_q", "mem_g_k", "w_br_ml", "w_br_nsa", "w_br_mem", "w_out", "g_ffn", "w_router", "b_router",
        "w_gu", "b_gu", "w_down", "b_down"]


def kernel(**inputs):
    import concourse.bacc as bacc
    from concourse.bass_utils import run_bass_kernel_spmd as run

    nc = bacc.Bacc("TRN2", target_bir_lowering=False, num_devices=1)
    arrays, A = {}, {}
    for name in _INS:
        a = np.ascontiguousarray(inputs[name])
        arrays[f"in_{name}"] = a
        A[name] = nc.dram_tensor(f"in_{name}", a.shape, mybir.dt.from_np(a.dtype), kind="ExternalInput").ap()
    arrays["shape_consts"] = CONST
    const = nc.dram_tensor("shape_consts", CONST.shape, F32, kind="ExternalInput").ap()
    out = nc.dram_tensor("out", (1, SEQ, D), F32, kind="ExternalOutput").ap()
    hybrid_layer(nc, A, const, out)
    r = run(nc, [arrays], core_ids=[0])
    return r.results[0]["out"]
```
